# Optimizing a Trainium2 kernel written in Bass

```python
import math
import jax, jax.numpy as jnp
from jax import lax
import numpy as np

D_MODEL = 1024
BATCH = 1
SEQ = 256
DEPTH = 2

HEAD_DIM = 64
EPS = 1e-6

SWA_Q_HEADS = 8
SWA_KV_HEADS = 2
SWA_GROUP = SWA_Q_HEADS // SWA_KV_HEADS
WINDOW = 128
BLOCK = 128
SWA_WIDTH = SWA_Q_HEADS * HEAD_DIM
KV_WIDTH = SWA_KV_HEADS * HEAD_DIM

SSM_WIDTH = D_MODEL // 2
SSM_GROUP_CH = 16
SSM_GROUPS = SSM_WIDTH // SSM_GROUP_CH
SSM_STATE = 64
DT_MIN = 0.001
DT_MAX = 0.1

EVEN_IN = SWA_WIDTH + 2 * KV_WIDTH + SSM_WIDTH
EVEN_MIX = SWA_WIDTH + SSM_WIDTH

SB_HEADS = D_MODEL // HEAD_DIM
SB_WIDTH = SB_HEADS * HEAD_DIM
SB_BLOCK = 128

D_FF = -(-8 * D_MODEL // (3 * 256)) * 256

N_EVEN = (DEPTH + 1) // 2
N_ODD = DEPTH // 2


def rmsnorm(x, g):
    xf = x.astype(jnp.float32)
    y = xf * lax.rsqrt(jnp.mean(xf * xf, axis=-1, keepdims=True) + EPS)
    return (y * g.astype(jnp.float32)).astype(x.dtype)

def swa_sink_attention(q, k, v, sinks):
    b, l, _, d = q.shape
    nb = l // BLOCK
    qb = q.reshape(b, nb, BLOCK, SWA_KV_HEADS, SWA_GROUP, d)

    def with_prev(t):
        t = t.reshape(b, nb, BLOCK, SWA_KV_HEADS, d)
        prev = jnp.concatenate([jnp.zeros_like(t[:, :1]), t[:, :-1]], axis=1)
        return jnp.concatenate([prev, t], axis=2)

    kb, vb = with_prev(k), with_prev(v)
    scores = jnp.einsum('bnqhgd,bnkhd->bnhgqk', qb, kb).astype(jnp.float32) * (d ** -0.5)
    qpos = jnp.arange(BLOCK) + BLOCK
    kpos = jnp.arange(2 * BLOCK)
    diff = qpos[:, None] - kpos[None, :]
    band = (diff >= 0) & (diff < WINDOW)
    has_prev = (jnp.arange(nb)[:, None] > 0) | (kpos[None, :] >= BLOCK)
    mask = (band[None, :, :] & has_prev[:, None, :])[None, :, None, None]
    scores = jnp.where(mask, scores, -jnp.inf)
    sink = sinks.astype(jnp.float32).reshape(SWA_KV_HEADS, SWA_GROUP)[None, None, :, :, None, None]
    m = jnp.maximum(scores.max(axis=-1, keepdims=True), sink)
    p = jnp.exp(scores - m)
    probs = p / (p.sum(axis=-1, keepdims=True) + jnp.exp(sink - m))
    o = jnp.einsum('bnhgqk,bnkhd->bnqhgd', probs.astype(v.dtype), vb)
    return o.reshape(b, l, SWA_WIDTH)

def _complex_affine_combine(left, right):
    ar1, ai1, br1, bi1 = left
    ar2, ai2, br2, bi2 = right
    return (ar2 * ar1 - ai2 * ai1,
            ar2 * ai1 + ai2 * ar1,
            ar2 * br1 - ai2 * bi1 + br2,
            ar2 * bi1 + ai2 * br1 + bi2)

def s5_mixer(u, a_re, a_im, b_re, b_im, c_re, c_im, d_skip, log_dt, w_glu, b_glu):
    f32 = jnp.float32
    b, l, _ = u.shape
    uf = u.astype(f32)
    ug = uf.reshape(b, l, SSM_GROUPS, SSM_GROUP_CH)
    a_re, a_im = a_re.astype(f32), a_im.astype(f32)
    b_re, b_im = b_re.astype(f32), b_im.astype(f32)
    c_re, c_im = c_re.astype(f32), c_im.astype(f32)
    dt = jnp.exp(log_dt.astype(f32))[:, None]
    mag = jnp.exp(a_re * dt)
    lam_re = mag * jnp.cos(a_im * dt)
    lam_im = mag * jnp.sin(a_im * dt)
    den = a_re * a_re + a_im * a_im
    w_re = ((lam_re - 1.0) * a_re + lam_im * a_im) / den
    w_im = (lam_im * a_re - (lam_re - 1.0) * a_im) / den
    bb_re = w_re[..., None] * b_re - w_im[..., None] * b_im
    bb_im = w_re[..., None] * b_im + w_im[..., None] * b_re
    bu_re = jnp.einsum('blgp,gnp->blgn', ug, bb_re)
    bu_im = jnp.einsum('blgp,gnp->blgn', ug, bb_im)
    shape = (1, l, SSM_GROUPS, SSM_STATE)
    lr = jnp.broadcast_to(lam_re, shape)
    li = jnp.broadcast_to(lam_im, shape)
    _, _, h_re, h_im = lax.associative_scan(_complex_affine_combine, (lr, li, bu_re, bu_im), axis=1)
    y = jnp.einsum('blgn,gpn->blgp', h_re, c_re) - jnp.einsum('blgn,gpn->blgp', h_im, c_im)
    y = y.reshape(b, l, SSM_WIDTH) + d_skip.astype(f32) * uf
    y = jax.nn.gelu(y)
    out = y * jax.nn.sigmoid(y @ w_glu.astype(f32) + b_glu.astype(f32))
    return out.astype(u.dtype)

def stick_breaking_attention(q, k, v):
    b, l, h, d = q.shape
    nb = l // SB_BLOCK
    qb = q.reshape(b, nb, SB_BLOCK, h, d).transpose(1, 0, 3, 2, 4)
    kt = k.transpose(0, 2, 1, 3)
    vt = v.transpose(0, 2, 1, 3)
    kpos = jnp.arange(l)
    scale = d ** -0.5

    def block(args):
        q_blk, start = args
        z = jnp.einsum('bhqd,bhkd->bhqk', q_blk, kt).astype(jnp.float32) * scale
        qpos = start + jnp.arange(SB_BLOCK)
        mask = kpos[None, :] < qpos[:, None]
        log_keep = jnp.where(mask, jax.nn.log_sigmoid(-z), 0.0)
        log_survive = lax.cumsum(log_keep, axis=3, reverse=True) - log_keep
        weights = jnp.where(mask, jnp.exp(jax.nn.log_sigmoid(z) + log_survive), 0.0)
        return jnp.einsum('bhqk,bhkd->bhqd', weights.astype(vt.dtype), vt)

    starts = jnp.arange(nb, dtype=jnp.int32) * SB_BLOCK
    o = lax.map(block, (qb, starts))
    return o.transpose(1, 0, 3, 2, 4).reshape(b, l, h * d)

def _normal(key, shape, scale):
    return jax.random.normal(key, shape, jnp.float32) * scale

def _gain(key, shape):
    return 1.0 + 0.02 * jax.random.normal(key, shape, jnp.float32)

def first_inputs(seed: int = 0) -> dict:
    key = jax.random.key(seed)
    ks = jax.random.split(key, 26)
    E, O, L = N_EVEN, N_ODD, DEPTH
    G, N, P = SSM_GROUPS, SSM_STATE, SSM_GROUP_CH
    n = jnp.arange(N, dtype=jnp.float32)
    log_dt = jax.random.uniform(ks[13], (E, G), jnp.float32,
                                math.log(DT_MIN), math.log(DT_MAX))
    return {
        "x": _normal(ks[0], (BATCH, SEQ, D_MODEL), 1.0),
        "even_norm": _gain(ks[1], (E, D_MODEL)),
        "even_w_in": _normal(ks[2], (E, D_MODEL, EVEN_IN), D_MODEL ** -0.5),
        "q_norm": _gain(ks[3], (E, HEAD_DIM)),
        "k_norm": _gain(ks[4], (E, HEAD_DIM)),
        "sinks": _normal(ks[5], (E, SWA_Q_HEADS), 0.5),
        "ssm_a_re": -0.5 * jnp.exp(0.02 * jax.random.normal(ks[6], (E, G, N), jnp.float32)),
        "ssm_a_im": jnp.pi * n + 0.01 * jax.random.normal(ks[7], (E, G, N), jnp.float32),
        "ssm_b_re": _normal(ks[8], (E, G, N, P), (2 * P) ** -0.5),
        "ssm_b_im": _normal(ks[9], (E, G, N, P), (2 * P) ** -0.5),
        "ssm_c_re": _normal(ks[10], (E, G, P, N), N ** -0.5),
        "ssm_c_im": _normal(ks[11], (E, G, P, N), N ** -0.5),
        "ssm_d": _normal(ks[12], (E, SSM_WIDTH), 0.5),
        "ssm_log_dt": log_dt,
        "ssm_w_glu": _normal(ks[14], (E, SSM_WIDTH, SSM_WIDTH), SSM_WIDTH ** -0.5),
        "ssm_b_glu": _normal(ks[15], (E, SSM_WIDTH), 0.02),
        "even_w_out": _normal(ks[16], (E, EVEN_MIX, D_MODEL), EVEN_MIX ** -0.5),
        "odd_norm": _gain(ks[17], (O, D_MODEL)),
        "odd_w_in": _normal(ks[18], (O, D_MODEL, 3 * SB_WIDTH), D_MODEL ** -0.5),
        "odd_w_out": _normal(ks[19], (O, SB_WIDTH, D_MODEL), SB_WIDTH ** -0.5),
        "ffn_norm": _gain(ks[20], (L, D_MODEL)),
        "ffn_w_gate": _normal(ks[21], (L, D_MODEL, D_FF), D_MODEL ** -0.5),
        "ffn_w_up": _normal(ks[22], (L, D_MODEL, D_FF), D_MODEL ** -0.5),
        "ffn_w_down": _normal(ks[23], (L, D_FF, D_MODEL), D_FF ** -0.5),
    }

def first_block(x, even_norm, even_w_in, q_norm, k_norm, sinks,
              ssm_a_re, ssm_a_im, ssm_b_re, ssm_b_im, ssm_c_re, ssm_c_im,
              ssm_d, ssm_log_dt, ssm_w_glu, ssm_b_glu, even_w_out,
              odd_norm, odd_w_in, odd_w_out,
              ffn_norm, ffn_w_gate, ffn_w_up, ffn_w_down):
    b, l, _ = x.shape
    for layer in range(DEPTH):
        i = layer // 2
        if layer % 2 == 0:
            hn = rmsnorm(x, even_norm[i])
            proj = hn @ even_w_in[i]
            q, k, v, u = jnp.split(
                proj, [SWA_WIDTH, SWA_WIDTH + KV_WIDTH, SWA_WIDTH + 2 * KV_WIDTH], axis=-1)
            q = rmsnorm(q.reshape(b, l, SWA_Q_HEADS, HEAD_DIM), q_norm[i])
            k = rmsnorm(k.reshape(b, l, SWA_KV_HEADS, HEAD_DIM), k_norm[i])
            v = v.reshape(b, l, SWA_KV_HEADS, HEAD_DIM)
            o_attn = swa_sink_attention(q, k, v, sinks[i])
            o_ssm = s5_mixer(u, ssm_a_re[i], ssm_a_im[i], ssm_b_re[i], ssm_b_im[i],
                             ssm_c_re[i], ssm_c_im[i], ssm_d[i], ssm_log_dt[i],
                             ssm_w_glu[i], ssm_b_glu[i])
            mixed = jnp.concatenate([o_attn, o_ssm], axis=-1) @ even_w_out[i]
        else:
            hn = rmsnorm(x, odd_norm[i])
            q, k, v = jnp.split(hn @ odd_w_in[i], 3, axis=-1)
            q = q.reshape(b, l, SB_HEADS, HEAD_DIM)
            k = k.reshape(b, l, SB_HEADS, HEAD_DIM)
            v = v.reshape(b, l, SB_HEADS, HEAD_DIM)
            mixed = stick_breaking_attention(q, k, v) @ odd_w_out[i]
        x = x + mixed
        hn = rmsnorm(x, ffn_norm[layer])
        x = x + (jax.nn.silu(hn @ ffn_w_gate[layer]) * (hn @ ffn_w_up[layer])) @ ffn_w_down[layer]
    return x


DEPTH_2 = 1

N_MEM = 256
D_MIX = D_MODEL
D_SGU = D_MIX // 2
D_ATT = D_MIX - D_SGU
SGU_GROUPS = 8
SGU_GROUP_DIM = D_SGU // SGU_GROUPS
CHUNK = 128
N_HEADS = 8
HEAD_DIM_2 = D_ATT // N_HEADS
DILATED_CONFIGS = ((128, 1), (512, 4), (2048, 16))
ROPE_THETA = 500000.0
ROPE_DIM = HEAD_DIM_2 // 4
X_HEADS = 4
X_HEAD_DIM = D_MODEL // X_HEADS
D_FF_2 = 2816
D_IN = 2 * D_SGU + 3 * D_ATT
NORM_EPS = 1e-6
LN_EPS = 1e-5
MAX_POS_OFFSET = 4096


F32 = jnp.float32

def rmsnorm_2(t, g):
    tf = t.astype(F32)
    y = tf * lax.rsqrt(jnp.mean(tf * tf, axis=-1, keepdims=True) + NORM_EPS)
    return (y * g.astype(F32)).astype(t.dtype)

def group_layernorm(t, g, b):
    G, C = t.shape[-2], t.shape[-1]
    tf = t.astype(F32)
    mu = jnp.mean(tf, axis=-1, keepdims=True)
    d = tf - mu
    y = d * lax.rsqrt(jnp.mean(d * d, axis=-1, keepdims=True) + LN_EPS)
    return (y * g.astype(F32).reshape(G, C) + b.astype(F32).reshape(G, C)).astype(t.dtype)

def swiglu(h, w_gate, w_up, w_down):
    return (jax.nn.silu(h @ w_gate) * (h @ w_up)) @ w_down

def partial_rotary(t, positions):
    half = ROPE_DIM // 2
    inv_freq = ROPE_THETA ** (-2.0 * jnp.arange(half, dtype=F32) / ROPE_DIM)
    ang = positions.astype(F32)[..., None] * inv_freq
    cos = jnp.cos(ang)[:, :, None, :]
    sin = jnp.sin(ang)[:, :, None, :]
    tf = t.astype(F32)
    x1 = tf[..., :half]
    x2 = tf[..., half:ROPE_DIM]
    out = jnp.concatenate([x1 * cos - x2 * sin, x2 * cos + x1 * sin, tf[..., ROPE_DIM:]], axis=-1)
    return out.astype(t.dtype)

def chunked_spatial_gating(z, ln_g, ln_b, w_s, b_s):
    b, s, _ = z.shape
    u, v = z[..., :D_SGU], z[..., D_SGU:]
    v = group_layernorm(v.reshape(b, s, SGU_GROUPS, SGU_GROUP_DIM), ln_g, ln_b)
    v = v.reshape(b, s // CHUNK, CHUNK, SGU_GROUPS, SGU_GROUP_DIM)
    causal = jnp.tril(jnp.ones((CHUNK, CHUNK), dtype=bool))
    ws = w_s * causal.astype(w_s.dtype)
    mixed = jnp.einsum('gij,bnjgc->bnigc', ws, v) + b_s.T[:, :, None]
    return u * mixed.reshape(b, s, D_SGU)

def dilated_window_attention(q, k, v, window, dilation):
    b, s, h, e = q.shape
    band = window // dilation
    L = s // dilation
    nb = -(-L // band)
    Lp = nb * band
    qs = q.reshape(b, L, dilation, h, e)
    ks = k.reshape(b, L, dilation, h, e)
    vs = v.reshape(b, L, dilation, h, e)
    qb = jnp.pad(qs, ((0, 0), (0, Lp - L), (0, 0), (0, 0), (0, 0))).reshape(b, nb, band, dilation, h, e)

    def kv_blocks(t):
        t = jnp.pad(t, ((0, 0), (band, Lp - L), (0, 0), (0, 0), (0, 0))).reshape(b, nb + 1, band, dilation, h, e)
        return jnp.concatenate([t[:, :-1], t[:, 1:]], axis=2)

    kb, vb = kv_blocks(ks), kv_blocks(vs)
    scores = jnp.einsum('bnqrhe,bnkrhe->bnrhqk', qb.astype(F32), kb.astype(F32)) * (e ** -0.5)
    qi = jnp.arange(band)[:, None]
    kj = jnp.arange(2 * band)[None, :]
    dist = band + qi - kj
    key_pos = (jnp.arange(nb)[:, None, None] - 1) * band + kj[None]
    mask = ((dist >= 0) & (dist <= band))[None] & (key_pos >= 0)
    scores = jnp.where(mask[None, :, None, None], scores, -jnp.inf)
    lse = jax.nn.logsumexp(scores, axis=-1)
    p = jnp.exp(scores - lse[..., None])
    o = jnp.einsum('bnrhqk,bnkrhe->bnqrhe', p.astype(v.dtype), vb)
    o = o.reshape(b, Lp, dilation, h, e)[:, :L].reshape(b, s, h, e)
    lse = jnp.transpose(lse, (0, 1, 4, 2, 3)).reshape(b, Lp, dilation, h)[:, :L].reshape(b, s, h)
    return o, lse

def dilated_mixture_attention(q, k, v):
    outs, lses = [], []
    for window, dilation in DILATED_CONFIGS:
        o, l = dilated_window_attention(q, k, v, window, dilation)
        outs.append(o)
        lses.append(l)
    wts = jax.nn.softmax(jnp.stack(lses, axis=0), axis=0)
    return jnp.einsum('gbsh,gbshe->bshe', wts.astype(q.dtype), jnp.stack(outs, axis=0))

def memory_cross_attention(h, m, wq, wk, wv, wo):
    b, s, _ = h.shape
    nm = m.shape[1]
    q = (h @ wq).reshape(b, s, X_HEADS, X_HEAD_DIM)
    k = (m @ wk).reshape(b, nm, X_HEADS, X_HEAD_DIM)
    v = (m @ wv).reshape(b, nm, X_HEADS, X_HEAD_DIM)
    scores = jnp.einsum('bshe,bmhe->bhsm', q.astype(F32), k.astype(F32)) * (X_HEAD_DIM ** -0.5)
    p = jax.nn.softmax(scores, axis=-1)
    o = jnp.einsum('bhsm,bmhe->bshe', p.astype(v.dtype), v)
    return o.reshape(b, s, D_MODEL) @ wo

def second_inputs(seed: int = 0) -> dict:
    key = jax.random.key(seed)
    ks = jax.random.split(key, 32)

    def w(k, shape, fan_in):
        return jax.random.normal(k, shape, F32) * (fan_in ** -0.5)

    def gain(k, shape):
        return 1.0 + 0.02 * jax.random.normal(k, shape, F32)

    L = DEPTH_2
    x = jax.random.normal(ks[0], (BATCH, SEQ, D_MODEL), F32)
    mem = jax.random.normal(ks[1], (BATCH, N_MEM, D_MODEL), F32)
    start = jax.random.randint(ks[2], (BATCH, 1), 0, MAX_POS_OFFSET, dtype=jnp.int32)
    positions = (start + jnp.arange(SEQ, dtype=jnp.int32)[None, :]).astype(jnp.int32)
    return {
        "x": x,
        "mem": mem,
        "positions": positions,
        "ffn1_norm": gain(ks[3], (L, D_MODEL)),
        "ffn1_w_gate": w(ks[4], (L, D_MODEL, D_FF_2), D_MODEL),
        "ffn1_w_up": w(ks[5], (L, D_MODEL, D_FF_2), D_MODEL),
        "ffn1_w_down": w(ks[6], (L, D_FF_2, D_MODEL), D_FF_2),
        "mix_norm": gain(ks[7], (L, D_MODEL)),
        "w_in": w(ks[8], (L, D_MODEL, D_IN), D_MODEL),
        "sgu_ln_g": gain(ks[9], (L, D_SGU)),
        "sgu_ln_b": 0.02 * jax.random.normal(ks[10], (L, D_SGU), F32),
        "sgu_w_s": w(ks[11], (L, SGU_GROUPS, CHUNK, CHUNK), CHUNK),
        "sgu_b_s": 1.0 + 0.1 * jax.random.normal(ks[12], (L, SGU_GROUPS, CHUNK), F32),
        "out_norm_a": gain(ks[13], (L, D_SGU)),
        "out_norm_b": gain(ks[14], (L, D_ATT)),
        "w_out": w(ks[15], (L, D_MIX, D_MODEL), D_MIX),
        "cross_norm": gain(ks[16], (L, D_MODEL)),
        "mem_norm": gain(ks[17], (L, D_MODEL)),
        "cross_wq": w(ks[18], (L, D_MODEL, D_MODEL), D_MODEL),
        "cross_wk": w(ks[19], (L, D_MODEL, D_MODEL), D_MODEL),
        "cross_wv": w(ks[20], (L, D_MODEL, D_MODEL), D_MODEL),
        "cross_wo": w(ks[21], (L, D_MODEL, D_MODEL), D_MODEL),
        "ffn2_norm": gain(ks[22], (L, D_MODEL)),
        "ffn2_w_gate": w(ks[23], (L, D_MODEL, D_FF_2), D_MODEL),
        "ffn2_w_up": w(ks[24], (L, D_MODEL, D_FF_2), D_MODEL),
        "ffn2_w_down": w(ks[25], (L, D_FF_2, D_MODEL), D_FF_2),
        "final_norm": gain(ks[26], (D_MODEL,)),
    }

def second_block(x, mem, positions, ffn1_norm, ffn1_w_gate, ffn1_w_up, ffn1_w_down,
              mix_norm, w_in, sgu_ln_g, sgu_ln_b, sgu_w_s, sgu_b_s,
              out_norm_a, out_norm_b, w_out, cross_norm, mem_norm,
              cross_wq, cross_wk, cross_wv, cross_wo,
              ffn2_norm, ffn2_w_gate, ffn2_w_up, ffn2_w_down, final_norm):
    b, s, _ = x.shape
    for l in range(DEPTH_2):
        h = rmsnorm_2(x, ffn1_norm[l])
        x = x + 0.5 * swiglu(h, ffn1_w_gate[l], ffn1_w_up[l], ffn1_w_down[l])

        h = rmsnorm_2(x, mix_norm[l])
        z = h @ w_in[l]
        z_sgu = jax.nn.gelu(z[..., :2 * D_SGU], approximate=False)
        o0 = 2 * D_SGU
        q = z[..., o0:o0 + D_ATT].reshape(b, s, N_HEADS, HEAD_DIM_2)
        k = z[..., o0 + D_ATT:o0 + 2 * D_ATT].reshape(b, s, N_HEADS, HEAD_DIM_2)
        v = z[..., o0 + 2 * D_ATT:o0 + 3 * D_ATT].reshape(b, s, N_HEADS, HEAD_DIM_2)
        q = partial_rotary(q, positions)
        k = partial_rotary(k, positions)

        y_a = chunked_spatial_gating(z_sgu, sgu_ln_g[l], sgu_ln_b[l], sgu_w_s[l], sgu_b_s[l])
        y_b = dilated_mixture_attention(q, k, v).reshape(b, s, D_ATT)
        y = jnp.concatenate([rmsnorm_2(y_a, out_norm_a[l]), rmsnorm_2(y_b, out_norm_b[l])], axis=-1)
        x = x + y @ w_out[l]

        h = rmsnorm_2(x, cross_norm[l])
        m = rmsnorm_2(mem, mem_norm[l])
        x = x + memory_cross_attention(h, m, cross_wq[l], cross_wk[l], cross_wv[l], cross_wo[l])

        h = rmsnorm_2(x, ffn2_norm[l])
        x = x + 0.5 * swiglu(h, ffn2_w_gate[l], ffn2_w_up[l], ffn2_w_down[l])
    return rmsnorm_2(x, final_norm)


def setup_inputs(seed=0):
    out = dict(first_inputs(seed))
    for name, value in second_inputs(seed + 1).items():
        if name != "x":
            out[name + "_2"] = value
    return out


def reference(
    x, even_norm, even_w_in, q_norm, k_norm, sinks, ssm_a_re, ssm_a_im, ssm_b_re, ssm_b_im,
    ssm_c_re, ssm_c_im, ssm_d, ssm_log_dt, ssm_w_glu, ssm_b_glu, even_w_out, odd_norm, odd_w_in,
    odd_w_out, ffn_norm, ffn_w_gate, ffn_w_up, ffn_w_down, mem_2, positions_2, ffn1_norm_2,
    ffn1_w_gate_2, ffn1_w_up_2, ffn1_w_down_2, mix_norm_2, w_in_2, sgu_ln_g_2, sgu_ln_b_2,
    sgu_w_s_2, sgu_b_s_2, out_norm_a_2, out_norm_b_2, w_out_2, cross_norm_2, mem_norm_2,
    cross_wq_2, cross_wk_2, cross_wv_2, cross_wo_2, ffn2_norm_2, ffn2_w_gate_2, ffn2_w_up_2,
    ffn2_w_down_2, final_norm_2,
):
    x = first_block(
        x, even_norm, even_w_in, q_norm, k_norm, sinks, ssm_a_re, ssm_a_im, ssm_b_re, ssm_b_im,
        ssm_c_re, ssm_c_im, ssm_d, ssm_log_dt, ssm_w_glu, ssm_b_glu, even_w_out, odd_norm,
        odd_w_in, odd_w_out, ffn_norm, ffn_w_gate, ffn_w_up, ffn_w_down,
    )
    return second_block(
        x, mem_2, positions_2, ffn1_norm_2, ffn1_w_gate_2, ffn1_w_up_2, ffn1_w_down_2,
        mix_norm_2, w_in_2, sgu_ln_g_2, sgu_ln_b_2, sgu_w_s_2, sgu_b_s_2, out_norm_a_2,
        out_norm_b_2, w_out_2, cross_norm_2, mem_norm_2, cross_wq_2, cross_wk_2, cross_wv_2,
        cross_wo_2, ffn2_norm_2, ffn2_w_gate_2, ffn2_w_up_2, ffn2_w_down_2, final_norm_2,
    )


_drawn_inputs = setup_inputs


def setup_inputs(seed=0):
    import zlib

    import numpy as np

    out = dict(_drawn_inputs(seed))
    spreads = {}
    factors = {'even_norm': 6.542,
     'q_norm': 8.0,
     'k_norm': 8.0,
     'sinks': 4.319,
     'ssm_a_re': 8.0,
     'ssm_b_re': 2.947,
     'ssm_b_im': 2.965,
     'ssm_c_re': 2.921,
     'ssm_c_im': 2.913,
     'ssm_b_glu': 8.0,
     'odd_norm': 3.889,
     'ffn1_norm_2': 8.0,
     'mix_norm_2': 3.512,
     'sgu_ln_g_2': 42.641,
     'sgu_ln_b_2': 37.223,
     'out_norm_a_2': 31.146,
     'out_norm_b_2': 31.865,
     'cross_norm_2': 8.0,
     'mem_norm_2': 8.0,
     'ffn2_norm_2': 25.122,
     'final_norm_2': 7.607,
     'sgu_b_s_2': 3.439}
    for name, (base, spread) in spreads.items():
        noise = np.random.default_rng([zlib.crc32(name.encode()), seed]).standard_normal(out[name].shape)
        drawn = base * np.exp(spread * noise) if base else spread * noise
        out[name] = __import__('jax').numpy.asarray(drawn.astype(out[name].dtype))
    for name, factor in factors.items():
        out[name] = (out[name] * factor).astype(out[name].dtype)
    return out
```

```python
from contextlib import ExitStack

import numpy as np
import concourse.bass as bass
from concourse import mybir

F32 = mybir.dt.float32
F32R = mybir.dt.float32r
I32 = mybir.dt.int32
ALU = mybir.AluOpType
ACT = mybir.ActivationFunctionType
AX = mybir.AxisListType.X

P = 128
L = 256
T = L // P
D = 1024
C = D // P
FF = 2816
UW = 256
NF = FF // UW
RAW = 3
NB = 4
EPS = 1e-6
LN_EPS = 1e-5
NEG = -1e30
MAGIC = 1.5 * 2.0 ** 23
TWO_PI = 6.283185
PI_A = 6.28125
PI_B = float(np.float32(np.round((2 * np.pi - PI_A) * 2 ** 20) / 2 ** 20))
PI_C = float(2 * np.pi - PI_A - PI_B)
G, N, PC, S = 32, 64, 16, 8
NC = L // S

CONSTS = dict(ident=128, jt=128, negtri=128, negones=128, tril=128, strict=128, swa=384, dil=384,
              step=36, phase=36, chunk=32, invf=8)
CONST_AT = {}
_at = 0
for _n, _w in CONSTS.items():
    CONST_AT[_n] = _at
    _at += _w
CONST_W = _at
EARLY_W = CONST_AT["negtri"]


def shape_constants():
    q = np.arange(P)[:, None]
    k = np.arange(P)[None, :]
    t = {}
    t["ident"] = (q == k) * 1.0
    j = np.zeros((P, P))
    j[np.arange(N) + N, np.arange(N)] = -1.0
    j[np.arange(N), np.arange(N) + N] = 1.0
    t["jt"] = j
    t["negtri"] = -1.0 * (q >= k)
    t["negones"] = -np.ones((P, P))
    t["tril"] = (q <= k) * 1.0
    t["strict"] = (q < k) * 1.0
    qq = np.concatenate([q, q + P, q + P], 1)

    def blocks(f):
        return np.concatenate([f(q - k), f(q + P - k), f(q - k)], 1)
    t["swa"] = blocks(lambda d: np.where((d >= 0) & (d < 128), 0.0, NEG))

    def count(d):
        n = (((d >= 0) & (d <= 128)) * 1.0 + ((d >= 0) & (d % 4 == 0)) + ((d >= 0) & (d % 16 == 0)))
        return np.where(n > 0, np.log(np.maximum(n, 1)), NEG)
    t["dil"] = blocks(count)
    im = np.arange(P)[:, None] >= N
    kb = np.arange(S - 1, -1, -1)
    kc = np.arange(S + 1)
    t["step"] = np.tile(np.concatenate([kb, kb, kc, kc, [1, 1]]), (P, 1))

    def ph(re, imv, n):
        return np.repeat(np.where(im, imv, re), n, 1)
    t["phase"] = np.concatenate([ph(.25, 0, S), ph(.5, .25, S), ph(.25, .5, S + 1), ph(.5, .75, S + 1),
                                 ph(.25, .25, 1), ph(0, 0, 1)], 1)
    t["chunk"] = np.tile(np.arange(NC), (P, 1))
    f = np.float32(500000.0) ** (np.float32(-2.0) * np.arange(8, dtype=np.float32) / np.float32(16))
    t["invf"] = np.tile(f, (P, 1))
    return np.concatenate([np.asarray(t[n], np.float64) for n in CONSTS], 1).astype(np.float32)


def plan(parts):
    at, out = 0, {}
    for name, n in parts:
        out[name] = at
        at += n
    out["end"] = at
    return out


STAGES = ["even", "ffn0", "odd", "ffn1", "ffn2", "mix", "cross", "ffn3", "final"]


def build(nc, a, out, stop=9):
    UNITS = plan([("even", 10), ("ffn0", 33), ("odd", 16), ("ffn1", 33), ("ffn2", 33), ("mix", 14 + 8),
                  ("cross", 8), ("ffn3", 33)])
    NU = UNITS["end"] if stop >= 8 else UNITS[STAGES[stop]]
    OUT = plan([("even", 5), ("glu", 2), ("even_out", 4), ("ffn0", 22), ("odd", 12), ("odd_pv", 4), ("odd_out", 4),
                ("ffn1", 22), ("ffn2", 22), ("mix", 10), ("mem", 8), ("mix_out", 4), ("cross", 4),
                ("cross_out", 4), ("ffn3", 22)])
    ACC = plan([("norm0", 4), ("prep_a", 1), ("prep_bc", 4), ("uc", 8), ("vt", 8), ("u", 2), ("s", 2), ("js", 2),
                ("k", 8), ("jg", 2), ("qk", 3), ("sc", 6), ("pt0", 3), ("pv0", 1), ("pt1", 3), ("pv1", 1),
                ("y", 2), ("yt", 4),
                ("norm1", 4), ("ffn0", 4), ("norm2", 4), ("sb", 16), ("norm3", 4), ("ffn1", 4),
                ("norm4", 4), ("ffn2", 4), ("norm5", 4), ("ws", 3), ("dqk", 4), ("norm8", 4), ("sgu", 2), ("dsc", 6),
                ("dpt0", 3), ("dpv0", 1), ("dpt1", 3), ("dpv1", 1), ("norm6", 4),
                ("norm7", 4), ("xsc", 4), ("xpt", 4), ("xpv", 4),
                ("norm9", 4), ("ffn3", 4)])
    NORMS = [0, 1, 2, 3, 4, 5, 8, 6, 7, 9, 10]
    GAINS = {0: "even_norm", 1: "ffn_norm", 2: "odd_norm", 3: "ffn_norm", 4: "ffn1_norm_2", 5: "mix_norm_2",
             7: "cross_norm_2", 8: "mem_norm_2", 9: "ffn2_norm_2"}
    SQ = plan([(n, 2 if n == 6 else 1) for n in NORMS])
    NTH = {n: i for i, n in enumerate(NORMS)}

    with ExitStack() as ctx:
        ctx.enter_context(nc.allow_non_contiguous_dma(reason="vectors of a few hundred elements, once"))

        def sb(name, shape, dt=F32):
            return ctx.enter_context(nc.sbuf_tensor(name, shape, dt))

        def sem(name):
            return ctx.enter_context(nc.semaphore(name))

        raw = sb("raw", [P, RAW, 2048])
        w_hi = sb("w_hi", [P, 2, 2048], F32R)
        w_lo = sb("w_lo", [P, 2, 2048], F32R)
        h_hi = sb("h_hi", [P, C, L], F32R)
        h_lo = sb("h_lo", [P, C, L], F32R)
        f_hi = sb("f_hi", [P, 1024], F32R)
        f_lo = sb("f_lo", [P, 1024], F32R)
        x_sb = sb("x_sb", [P, T, D])
        xn = sb("xn", [P, T, D])
        AW = 32460
        arena = sb("arena", [P, AW])
        top = [0]

        def area(n):
            top[0] += n
            assert top[0] <= AW, top[0]
            return top[0] - n

        def view(at, *shape, parts=P):
            n = int(np.prod(shape))
            v = arena[0:parts, at:at + n]
            names = "abcd"[:len(shape)]
            if len(shape) == 1:
                return v
            return v.rearrange(f"p ({' '.join(names)}) -> p {' '.join(names)}", **dict(zip(names, shape)))

        early = view(area(EARLY_W), EARLY_W)
        ident = early[:, 0:P]
        gains = view(area(10 * C), 10, C)
        ss = view(area(64), 16, 4)
        rms = view(area(64), 16, 4)
        half = view(area(32), 32)
        BASE = top[0]
        jt = early[:, CONST_AT["jt"]:CONST_AT["jt"] + P]
        o_swa = area(384)
        swa_mask = view(o_swa, 384)
        steps = view(area(36), 36)
        phase = view(area(36), 36)
        chunk = view(area(32), 32)
        qk_gain = view(area(2), 2)
        sinks = view(area(8), 8)
        b_glu = view(area(4), 4)
        dskip = view(area(512), G, PC)
        log_dt = view(area(32), G)
        REG_A = area(7680)
        b_nat = view(REG_A, 2, 2, 1024, parts=G)
        uc = view(REG_A, G, S * PC, parts=NC)
        kpad = view(REG_A, G, 15 * PC, parts=PC)
        sc = view(REG_A, 2, 1536)
        pt = view(REG_A + 3072, 2, 1536)
        hpad = view(REG_A + 6144, G, NC + 1)
        REG_V = area(4096)
        v_in = view(REG_V, G, S, PC)
        m_in = view(REG_V, G, P)
        REG_T = area(4096)
        tmp_t = view(REG_T, 36, G)
        tmp_u = view(REG_T + 1152, 36, G)
        tmp_n = view(REG_T + 2304, 36, G)
        vt = view(REG_T, G, P)
        g_st = view(REG_T, G, NC)
        y_ch = view(REG_T + 1024, S, C, PC)
        y_f = view(REG_T + 2048, 4, L)
        rho = view(REG_T + 3072, G, NC)
        o_w = area((S + 1) * 512)
        w_out_c = view(o_w, S + 1, G, PC)
        c_nat = view(o_w, 2, PC, 2, N, parts=G)
        tab = view(area(36 * G), 36, G)
        alpha = view(area(2048), 2, G, NC)
        cbr = view(area(512), PC, G)
        cbi = view(area(512), PC, G)
        o_u = area(1024)
        br = view(o_u, PC, G)
        bi = view(o_u + 512, PC, G)
        u_ch = view(o_u, G, NC)
        o_qkv = area(1536)
        qkv = view(o_qkv, T, 768)
        u_t = view(o_qkv, 4, L)
        o_qt = area(1280)
        q_t = view(o_qt, 4, L)
        k_t = view(o_qt + 1024, L)
        cr = view(o_qt, PC, G)
        ci = view(o_qt + 512, PC, G)
        st = view(area(200), 200)
        a_t = view(area(64), 2, G)
        small = view(area(16 * G), 16, G)
        a_raw = view(area(4 * N), 2, 2, N, parts=G)
        bst = view(area(512), PC, G)
        pool_tmp = view(area(512), G, PC)
        sig = u_t
        s_ch = xn[:, 0, :]
        t_ch = xn[:, 1, :]
        EVEN_TOP = top[0]
        top[0] = BASE
        late = view(area(CONST_W - EARLY_W), CONST_W - EARLY_W)
        silu = view(area(1024), 2, 512)
        hf = view(area(1024), 2, 512)
        BASE2 = top[0]

        def const(name):
            o = CONST_AT[name] - EARLY_W
            return late[:, o:o + CONSTS[name]]
        sq_t = view(area(2048), C, L)
        sk_t = view(area(2048), C, L)
        sv = view(area(2048), T, D)
        sb_e = view(area(4 * 384), 4, 384)
        sb_sp = view(area(4 * 384), 4, 384)
        sb_w = view(area(4 * 384), 4, 384)
        top[0] = BASE2
        zu = view(area(1024), T, 512)
        zv = view(area(1024), T, 512)
        zs = view(area(1024), T, 512)
        dqk = view(area(2048), T, 16, 64)
        dv = view(area(1024), T, 512)
        dq_t = view(area(1024), 4, L)
        dk_t = view(area(1024), 4, L)
        dsc = view(area(3072), 2, 1536)
        dpt = view(area(3072), 2, 1536)
        km_t = view(area(2048), C, L)
        vm = view(area(2048), T, D)
        mem_sb = view(area(2048), T, D)
        y_nat = view(area(2048), T, D)
        ws_nat = view(area(1024), 8, P)
        ws_t = view(area(1024), 8, P)
        bs_nat = view(area(128), P, parts=8)
        bs_t = view(area(8), 8)
        ln_g = view(area(512), 512)
        ln_b = view(area(512), 512)
        g_ab = view(area(8), C)
        rot = view(area(8 * 16), 8, T, 8)
        pos_f = view(area(2), 2)
        dst_ = view(area(128), 128)
        ropet = view(area(4 * 256), 4, T, 16, 8)
        pos_i = sb("pos_i", [P, T], I32)
        xq_t = dsc_q = view(BASE2, C, L)
        xs = view(BASE2 + 2048, T, 4, L)
        xpt = view(BASE2 + 4096, T, 4, L)
        fin_g = view(BASE2 + 6144, D)

        acc = ctx.enter_context(nc.psum_tensor("acc", [P, NB, 512], F32))
        outp = ctx.enter_context(nc.psum_tensor("outp", [P, NB, 512], F32))

        raw_landed = [sem(f"raw_landed{i}") for i in range(RAW)]
        w_hi_ready, w_lo_ready, w_used = sem("w_hi_ready"), sem("w_lo_ready"), sem("w_used")
        acc_ready = sem("acc_ready")
        acc_free = [sem(f"acc_free{i}") for i in range(NB)]
        out_free = [sem(f"out_free{i}") for i in range(NB)]
        x_loaded, consts_in, late_in, late2_in, mem_in, fin_in = (sem("x_loaded"), sem("consts_in"), sem("late_in"),
                                                                  sem("late2_in"), sem("mem_in"), sem("fin_in"))
        small_in, gain0_in = sem("small_in"), sem("gain0_in")
        act_step, dve_step, pool_step = sem("act_step"), sem("dve_step"), sem("pool_step")
        half_ready = sem("half_ready")
        sq_v, sq_a, rms_ready, xn_v, xn_a, h_hi_ready = (sem("sq_v"), sem("sq_a"), sem("rms_ready"), sem("xn_v"),
                                                         sem("xn_a"), sem("h_hi_ready"))
        f_hi_done, f_lo_done = sem("f_hi_done"), sem("f_lo_done")
        dt_ready, lam_mag, lam_exp, lam_frac, lam_sin = (sem("dt_ready"), sem("lam_mag"), sem("lam_exp"),
                                                         sem("lam_frac"), sem("lam_sin"))
        al_frac, al_sin, tab_ready, bb_ready, v_ready, wc_ready = (
            sem("al_frac"), sem("al_sin"), sem("tab_ready"), sem("bb_ready"), sem("v_ready"), sem("wc_ready"))
        decay_ready, rho_ready, g_ready, h_ready, kz_ready, k_ready, m_in_done = (
            sem("decay_ready"), sem("rho_ready"), sem("g_ready"), sem("h_ready"), sem("kz_ready"), sem("k_ready"),
            sem("m_in_done"))
        qk_sq, qk_rms, qk_ready = sem("qk_sq"), sem("qk_rms"), sem("qk_ready")
        yf_done, yhi_ready, ylo_ready, sig_done, glu_done, glu_hi, glu_lo = (
            sem("yf_done"), sem("yhi_ready"), sem("ylo_ready"), sem("sig_done"), sem("glu_done"), sem("glu_hi"),
            sem("glu_lo"))
        sub_done, exp_done, p_ready, mix_hi = sem("sub_done"), sem("exp_done"), sem("p_ready"), sem("mix_hi")
        sb_ln, sb_sp_done, sb_cum, sb_w_done, pv_ready = (sem("sb_ln"), sem("sb_sp_done"), sem("sb_cum"),
                                                          sem("sb_w_done"), sem("pv_ready"))
        rope_frac, rope_sin, rot_done, ln_v, ln_rms, ln_ready = (
            sem("rope_frac"), sem("rope_sin"), sem("rot_done"), sem("ln_v"), sem("ln_rms"), sem("ln_ready"))
        stored = sem("stored")

        block = ctx.enter_context(nc.Block())

        class Own:

            def __init__(self, eng, s):
                self.eng, self.s, self.n = eng, s, 0

            def link(self, ins):
                self.n += 1
                ins.then_inc(self.s, 1)
                self.eng.wait_ge(self.s, self.n)

        def acc_taken(pe, k):
            if k >= NB:
                pe.wait_ge(acc_free[k % NB], k // NB)

        def out_taken(pe, k, it=0):
            if k >= NB:
                pe.wait_ge(out_free[k % NB], k // NB + it)

        def written(eng, k):
            eng.wait_ge(acc_ready, k + 1 - NB * sum(ACC[f] < k for f in FFN))

        def emptied(eng, k, n=1):
            for j in range(k + max(0, n - NB), k + n):
                eng.wait_ge(acc_free[j % NB], j // NB + 1)

        def out_emptied(eng, k, n=1, it=0):
            for j in range(k + max(0, n - NB), k + n):
                eng.wait_ge(out_free[j % NB], j // NB + 1 + it)

        def x_whole(eng, what):
            ring, k = what
            (emptied if ring == "acc" else out_emptied)(eng, k, NB)

        X_FROM = {1: ("out", OUT["even_out"]), 2: ("acc", ACC["ffn0"]), 3: ("out", OUT["odd_out"]),
                  4: ("acc", ACC["ffn1"]), 5: ("acc", ACC["ffn2"]), 7: ("out", OUT["mix_out"]),
                  9: ("out", OUT["cross_out"]), 10: ("acc", ACC["ffn3"])}
        FFNS = [("ffn0", 0, a["ffn_w_gate"][0], a["ffn_w_up"][0], a["ffn_w_down"][0], 1.0, 1),
                ("ffn1", 1, a["ffn_w_gate"][1], a["ffn_w_up"][1], a["ffn_w_down"][1], 1.0, 3),
                ("ffn2", 2, a["ffn1_w_gate_2"][0], a["ffn1_w_up_2"][0], a["ffn1_w_down_2"][0], 0.5, 4),
                ("ffn3", 3, a["ffn2_w_gate_2"][0], a["ffn2_w_up_2"][0], a["ffn2_w_down_2"][0], 0.5, 9)]
        FFN = {f[0]: f for f in FFNS}
        running = STAGES[:stop]

        def const_in(name):
            return a["consts"][:, CONST_AT[name]:CONST_AT[name] + CONSTS[name]]

        def flat(v):
            return v.rearrange("p a b -> p (a b)")

        def uc_part(j, q):
            return uc[:, 16 * j:16 * j + 16, 2 * q * PC:(2 * q + 2) * PC].rearrange("p g (s c) -> p s g c", c=PC)

        def uc_bank(k):
            return acc[0:NC, k % NB, :].rearrange("p (s g c) -> p s g c", s=2, c=PC)

        def row(v):
            return v.rearrange("(a n) -> a n", a=1)
        small_loads = [(a_raw[:, j, h, :], a[n][0]) for j, n in enumerate(["ssm_a_re", "ssm_a_im"]) for h in range(2)]
        small_loads += [(log_dt, row(a["ssm_log_dt"][0]).to_broadcast([P, G]))]
        small_loads += [(b_nat[:, j, h, :], a[n][0].rearrange("g n p -> g (n p)"))
                        for j, n in enumerate(["ssm_b_re", "ssm_b_im"]) for h in range(2)]
        small_loads += [(c_nat[:, j, :, h, :], a[n][0]) for j, n in enumerate(["ssm_c_re", "ssm_c_im"])
                        for h in range(2)]
        small_loads += [(steps, const_in("step")), (phase, const_in("phase")), (chunk, const_in("chunk")),
                        (swa_mask, const_in("swa"))]
        small_loads += [(qk_gain[64 * j:64 * j + 64, i:i + 1], a[n][0].rearrange("(d a) -> d a", a=1))
                        for i, n in enumerate(["q_norm", "k_norm"]) for j in range(2)]
        small_loads += [(sinks, row(a["sinks"][0]).to_broadcast([P, 8])),
                        (b_glu, a["ssm_b_glu"][0].rearrange("(c p) -> p c", p=P)),
                        (dskip[0:PC, :, :].rearrange("p g c -> p (g c)"), row(a["ssm_d"][0]).to_broadcast([PC, 512]))]
        small_loads += [(gains[:, n, :], a[g][1 if n == 3 else 0].rearrange("(p c) -> p c", c=C))
                        for n, g in GAINS.items() if n > 0]
        SMALL = len(small_loads)
        late_loads = [(ws_nat, a["sgu_w_s_2"][0].rearrange("g i j -> i g j")), (bs_nat, a["sgu_b_s_2"][0]),
                      (ln_g, row(a["sgu_ln_g_2"][0]).to_broadcast([P, 512])),
                      (ln_b, row(a["sgu_ln_b_2"][0]).to_broadcast([P, 512])),
                      (pos_i[:, :], a["positions_2"][0].rearrange("(t p) -> p t", p=P))]
        late_loads += [(g_ab[64 * j:64 * j + 64, :], a[n][0].rearrange("(p c) -> p c", c=C))
                       for j, n in enumerate(["out_norm_a_2", "out_norm_b_2"])]
        LATE2 = len(late_loads)

        @block.sync
        def _(sp):
            sp.dma_start(x_sb[:, :, :], a["x"][0].rearrange("(t p) f -> p t f", p=P)).then_inc(x_loaded, 16)
            sp.dma_start(early, a["consts"][:, 0:EARLY_W]).then_inc(consts_in, 16)
            sp.dma_start(gains[:, 0, :], a["even_norm"][0].rearrange("(p c) -> p c", c=C)).then_inc(gain0_in, 16)

            def load(u, src, cols=UW, it=0):
                if u >= RAW:
                    sp.wait_ge(w_lo_ready, u - RAW + 1 + 6 * it)
                dst = raw[:, u % RAW, :].rearrange("p (c n) -> p c n", n=cols)
                sp.dma_start(dst, src).then_inc(raw_landed[u % RAW], 16)

            def by_p(w):
                return w.rearrange("(p c) n -> p c n", p=P)

            def by_c(w):
                return w.rearrange("(c p) n -> p c n", p=P)

            def cols(w, n):
                return w[:, :, n * UW:(n + 1) * UW]

            def ffn(name):
                _, _, wg, wu, wd, _, _ = FFN[name]
                wg, wu, wd = by_p(wg), by_p(wu), by_c(wd)
                u0 = UNITS[name]
                load(u0, cols(wg, 0))
                load(u0 + 1, cols(wu, 0))
                load(u0 + 2, cols(wg, 1))
                if name == "ffn0":
                    x_whole(sp, X_FROM[1])
                    sp.dma_start(late, a["consts"][:, EARLY_W:CONST_W]).then_inc(late_in, 16)
                if name == "ffn1":
                    x_whole(sp, X_FROM[3])
                    for dst, src in late_loads:
                        sp.dma_start(dst, src).then_inc(late2_in, 16)
                    sp.dma_start(mem_sb, a["mem_2"][0].rearrange("(t p) f -> p t f", p=P)).then_inc(mem_in, 16)
                if name == "ffn3":
                    x_whole(sp, X_FROM[9])
                    sp.dma_start(fin_g, row(a["final_norm_2"]).to_broadcast([P, D])).then_inc(fin_in, 16)

                def turn(i, it=0):
                    if i > 0:
                        load(u0 + 2 + 3 * i, wg[:, :, bass.ds((i + 1 + 2 * it) * UW, UW)], it=it)
                    load(u0 + 3 + 3 * i, wu[:, :, bass.ds((i + 1 + 2 * it) * UW, UW)], it=it)
                    load(u0 + 4 + 3 * i, wd[:, bass.ds((i + 2 * it) * 2, 2), :], D, it=it)
                turn(0)
                with sp.Fori(0, 4) as it:
                    turn(1, it)
                    turn(2, it)
                turn(9)
                load(u0 + 32, wd[:, 20:22, :], D)

            if "even" in running:
                u0 = UNITS["even"]
                w = by_p(a["even_w_in"][0])
                for j, n in enumerate([3, 4, 0, 1, 2]):
                    load(u0 + j, cols(w, n))
                    if j == 1:
                        for dst, src in small_loads:
                            sp.dma_start(dst, src).then_inc(small_in, 16)
                load(u0 + 5, by_c(a["ssm_w_glu"][0]), 512)
                for j in range(4):
                    load(u0 + 6 + j, cols(by_c(a["even_w_out"][0]), j))
                    if j == 1:
                        sp.wait_ge(kz_ready, 1)
                        sp.wait_ge(k_ready, 1)
                        for s in range(S):
                            o = (S - 1 - s) * PC
                            sp.dma_start(m_in[s * PC:(s + 1) * PC, :, :], kpad[:, :, o:o + P]).then_inc(m_in_done, 16)
            if "ffn0" in running:
                ffn("ffn0")
            if "odd" in running:
                u0 = UNITS["odd"]
                for j in range(12):
                    load(u0 + j, cols(by_p(a["odd_w_in"][0]), j))
                for j in range(4):
                    load(u0 + 12 + j, cols(by_c(a["odd_w_out"][0]), j))
            if "ffn1" in running:
                ffn("ffn1")
            if "ffn2" in running:
                ffn("ffn2")
            if "mix" in running:
                u0 = UNITS["mix"]
                for j, n in enumerate([4, 5, 6, 7, 8, 9, 0, 1, 2, 3]):
                    load(u0 + j, cols(by_p(a["w_in_2"][0]), n))
                for j in range(4):
                    load(u0 + 10 + j, cols(by_p(a["cross_wk_2"][0]), j))
                for j in range(4):
                    load(u0 + 14 + j, cols(by_p(a["cross_wv_2"][0]), j))
                for j in range(4):
                    load(u0 + 18 + j, cols(by_p(a["w_out_2"][0]), j))
            if "cross" in running:
                u0 = UNITS["cross"]
                for j in range(4):
                    load(u0 + j, cols(by_p(a["cross_wq_2"][0]), j))
                for j in range(4):
                    load(u0 + 4 + j, cols(by_c(a["cross_wo_2"][0]), j))
            if "ffn3" in running:
                ffn("ffn3")
            if stop == 9:
                sp.wait_ge(xn_v, NTH[10] + 1)
                sp.wait_ge(xn_a, NTH[10] + 1)
                src = xn
            else:
                n = {1: 1, 2: 2, 3: 3, 4: 4, 5: 5, 6: 7, 7: 9, 8: 10}[stop]
                x_whole(sp, X_FROM[n])
                src = x_sb
            sp.dma_start(out[0].rearrange("(t p) f -> p t f", p=P), src[:, :, :]).then_inc(stored, 16)
            sp.wait_ge(stored, 16)

        @block.tensor
        def _(pe):
            def mm3(dst, w_pair, a_pair, start, stop_, act_first=False):
                passes = ((0, 0), (0, 1), (1, 0))
                for n, (i, j) in enumerate(passes):
                    lhs, rhs = (a_pair[j], w_pair[i]) if act_first else (w_pair[i], a_pair[j])
                    ins = nc.tensor.matmul(dst, lhs, rhs, start=start and n == 0, stop=stop_ and n == 2)
                return ins

            def w_unit(u, n, it=0):
                pe.wait_ge(w_lo_ready, u + 1 + 6 * it)
                return [w[:, u % 2, :].rearrange("p (c n) -> p c n", n=n) for w in (w_hi, w_lo)]

            def proj_t(u, k, it=0):
                w = w_unit(u, UW, it)
                out_taken(pe, k, it)
                for m in range(2):
                    for c in range(C):
                        ins = mm3(outp[:, k % NB, m * L:(m + 1) * L], [x[:, c, m * P:(m + 1) * P] for x in w],
                                  [x[:, c, :] for x in (h_hi, h_lo)], c == 0, c == C - 1)
                ins.then_inc(w_used, 1)

            def proj_n(u, k):
                w = w_unit(u, UW)
                out_taken(pe, k)
                for t in range(T):
                    for c in range(C):
                        ins = mm3(outp[:, k % NB, t * UW:(t + 1) * UW], [x[:, c, :] for x in w],
                                  [x[:, c, t * P:(t + 1) * P] for x in (h_hi, h_lo)], c == 0, c == C - 1, True)
                ins.then_inc(w_used, 1)

            def flip(dst, src, rows=P, base=0):
                return nc.tensor.transpose(dst, src, ident[base:base + rows, base:base + rows])

            def norm(n):
                k = ACC[f"norm{n}"]
                for t in range(T):
                    pe.wait_ge(*((xn_v, NTH[n] + 1) if t == 0 else (xn_a, NTH[n] + 1)))
                    for q in range(4):
                        if t == 0:
                            acc_taken(pe, k + q)
                        for c in range(2):
                            ins = flip(acc[:, (k + q) % NB, c * L + t * P:c * L + (t + 1) * P],
                                       xn[:, t, 2 * q + c::C])
                        if t == 1:
                            ins.then_inc(acc_ready, 1)

            def h_whole(n):
                emptied(pe, ACC[f"norm{n}"], 4)

            def ffn(name):
                _, f, _, _, _, _, n = FFN[name]
                u0, k0, d0 = UNITS[name], OUT[name], ACC[name]
                norm(n)
                h_whole(n)
                proj_t(u0, k0)
                proj_t(u0 + 1, k0 + 1)

                def down(u, i, it, start, stop_):
                    w = w_unit(u, D, it)
                    pe.wait_ge(f_lo_done, NF * f + i + 1 + 2 * it)
                    b = (NF * f + i) % 2
                    for t in range(T):
                        for h in range(2):
                            for m in range(2):
                                o = b * 512 + m * L + t * P
                                ins = mm3(acc[:, (d0 + 2 * t + h) % NB, :], [x[:, m, h * 512:(h + 1) * 512] for x in w],
                                          [x[:, o:o + P] for x in (f_hi, f_lo)], start and m == 0,
                                          stop_ and m == 1, True)
                    ins.then_inc(w_used, 1)

                def turn(i, it=0):
                    proj_t(u0 + 2 + 3 * i, k0 + 2 * (i + 1), it)
                    proj_t(u0 + 3 + 3 * i, k0 + 2 * (i + 1) + 1, it)
                    down(u0 + 4 + 3 * i, i, it, i == 0, False)
                for j in range(4):
                    acc_taken(pe, d0 + j)
                turn(0)
                with pe.Fori(0, 4) as it:
                    turn(1, it)
                    turn(2, it)
                turn(9)
                down(u0 + 32, 10, 0, False, True)

            def scores(k, b, lhs, rhs):
                acc_taken(pe, k)
                for h in range(4):
                    ins = nc.tensor.matmul(acc[:, k % NB, h * P:(h + 1) * P], lhs(b, h)[:, 0:P], rhs(b, h)[:, 0:P],
                                           start=True, stop=True)
                ins.then_inc(acc_ready, 1)
                for j in range(2):
                    acc_taken(pe, k + 1 + j)
                    for h in range(2 * j, 2 * j + 2):
                        ins = nc.tensor.matmul(acc[:, (k + 1 + j) % NB, (h % 2) * L:(h % 2 + 1) * L],
                                               lhs(b, h)[:, P:L], rhs(b, h), start=True, stop=True)
                    ins.then_inc(acc_ready, 1)

            def probs_t(k, b, s, first):
                for j in range(2):
                    acc_taken(pe, k + j)
                    pe.wait_ge(p_ready, first + (3 * b + 2 + j))
                    for h in range(2 * j, 2 * j + 2):
                        o = (h % 2) * L
                        flip(acc[:, (k + j) % NB, o:o + P], s[:, b, h * P:(h + 1) * P])
                        ins = flip(acc[:, (k + j) % NB, o + P:o + L], s[:, b, 512 + h * L:512 + h * L + P])
                    ins.then_inc(acc_ready, 1)
                acc_taken(pe, k + 2)
                for h in range(4):
                    ins = flip(acc[:, (k + 2) % NB, h * P:(h + 1) * P], s[:, b, 512 + h * L + P:512 + (h + 1) * L])
                ins.then_inc(acc_ready, 1)

            def even():
                u0, k0 = UNITS["even"], OUT["even"]
                pe.wait_ge(consts_in, 16)
                norm(0)
                k = ACC["prep_a"]
                acc_taken(pe, k)
                pe.wait_ge(small_in, 16 * SMALL)
                for j in range(2):
                    ins = flip(acc[:, k % NB, j * G:(j + 1) * G], flat(a_raw[:, j, :, :]), G)
                ins.then_inc(acc_ready, 1)
                for j in range(4):
                    k = ACC["prep_bc"] + j
                    acc_taken(pe, k)
                    for p in range(PC):
                        src = flat(b_nat[:, j, :, :])[:, p::PC] if j < 2 else flat(c_nat[:, j - 2, p, :, :])
                        ins = flip(acc[:, k % NB, p * G:(p + 1) * G], src, G)
                    ins.then_inc(acc_ready, 1)
                h_whole(0)
                proj_t(u0, k0)
                proj_t(u0 + 1, k0 + 1)
                for j in range(2):
                    out_emptied(pe, k0 + j)
                    for q in range(4):
                        k = ACC["uc"] + 4 * j + q
                        acc_taken(pe, k)
                        for s in range(2):
                            for m in range(2):
                                o = s * 256 + m * P
                                ins = flip(acc[0:NC, k % NB, o:o + P], u_t[:, 2 * j + m, 2 * q + s::S])
                        ins.then_inc(acc_ready, 1)
                for j in range(3):
                    proj_n(u0 + 2 + j, k0 + 2 + j)
                pe.wait_ge(v_ready, 1)
                for j in range(8):
                    k = ACC["vt"] + j
                    acc_taken(pe, k)
                    for g in range(4):
                        ins = flip(acc[:, k % NB, g * P:(g + 1) * P],
                                   v_in[:, 4 * j + g, :, :].rearrange("p s c -> p (s c)"))
                    ins.then_inc(acc_ready, 1)
                emptied(pe, ACC["uc"], 8)
                for j in range(2):
                    k = ACC["u"] + j
                    acc_taken(pe, k)
                    for g in range(16):
                        ins = flip(acc[:, k % NB, g * NC:(g + 1) * NC], uc[:, 16 * j + g, :], NC)
                    ins.then_inc(acc_ready, 1)
                emptied(pe, ACC["u"], 2)
                emptied(pe, ACC["vt"], 8)
                for j in range(2):
                    k = ACC["s"] + j
                    acc_taken(pe, k)
                    for g in range(16):
                        gg = 16 * j + g
                        ins = nc.tensor.matmul(acc[:, k % NB, g * NC:(g + 1) * NC], vt[:, gg, :], u_ch[:, gg, :],
                                               start=True, stop=True)
                    ins.then_inc(acc_ready, 1)
                for j in range(2):
                    k = ACC["js"] + j
                    acc_taken(pe, k)
                    emptied(pe, ACC["s"] + j)
                    nc.tensor.matmul(acc[:, k % NB, :], jt, s_ch[:, j * 512:(j + 1) * 512],
                                     start=True, stop=True).then_inc(acc_ready, 1)
                pe.wait_ge(wc_ready, 1)
                pe.wait_ge(bb_ready, 1)
                for j in range(8):
                    k = ACC["k"] + j
                    acc_taken(pe, k)
                    for g in range(4):
                        gg = 4 * j + g
                        ins = nc.tensor.matmul(acc[0:PC, k % NB, g * P:(g + 1) * P], bst[:, :, gg],
                                               w_out_c[:, 0:S, gg, :], start=True, stop=True)
                    ins.then_inc(acc_ready, 1)
                for j in range(2):
                    k = ACC["jg"] + j
                    acc_taken(pe, k)
                    pe.wait_ge(g_ready, 1)
                    nc.tensor.matmul(acc[:, k % NB, :], jt,
                                     g_st[:, 16 * j:16 * (j + 1), :].rearrange("p g c -> p (g c)"),
                                     start=True, stop=True).then_inc(acc_ready, 1)
                k = ACC["qk"]
                pe.wait_ge(qk_ready, 1)
                for j in range(2):
                    acc_taken(pe, k + j)
                    for h in range(2):
                        for t in range(T):
                            ins = flip(acc[:, (k + j) % NB, h * L + t * P:h * L + (t + 1) * P],
                                       qkv[:, t, (2 * j + h) * P:(2 * j + h + 1) * P])
                    ins.then_inc(acc_ready, 1)
                acc_taken(pe, k + 2)
                for t in range(T):
                    ins = flip(acc[:, (k + 2) % NB, t * P:(t + 1) * P], qkv[:, t, 512:640])
                ins.then_inc(acc_ready, 1)
                emptied(pe, ACC["qk"], 3)

                def q_of(b, h):
                    return q_t[64 * b:64 * b + 64, h, :]

                def k_of(b, h):
                    return k_t[64 * b:64 * b + 64, :]
                for b in range(2):
                    scores(ACC["sc"] + 3 * b, b, q_of, k_of)

                def values_t(k, b):
                    emptied(pe, ACC[f"pt{b}"], 3)
                    acc_taken(pe, k)
                    for h in range(4):
                        po = (h % 2) * 64
                        dst = acc[po:po + 64, k % NB, (h // 2) * L:(h // 2 + 1) * L]
                        vs = [qkv[:, t, 640 + 64 * b:704 + 64 * b] for t in range(T)]
                        nc.tensor.matmul(dst, vs[0], pt[:, b, h * L:(h + 1) * L], start=True, stop=False)
                        ins = nc.tensor.matmul(dst[:, P:L], vs[1], pt[:, b, 1024 + h * P:1024 + (h + 1) * P],
                                               start=False, stop=True)
                    ins.then_inc(acc_ready, 1)
                for b in range(2):
                    probs_t(ACC[f"pt{b}"], b, sc, 0)
                    values_t(ACC[f"pv{b}"], b)
                pe.wait_ge(m_in_done, 16 * S)
                pe.wait_ge(h_ready, 3)
                for j in range(2):
                    k = ACC["y"] + j
                    acc_taken(pe, k)
                    for cc in range(4):
                        for g4 in range(4):
                            gg = cc * 8 + j * 4 + g4
                            dst = acc[NC * cc:NC * (cc + 1), k % NB, g4 * P:(g4 + 1) * P]
                            nc.tensor.matmul(dst, u_ch[:, gg, :], m_in[:, gg, :], start=True, stop=False)
                            ins = nc.tensor.matmul(dst, hpad[:, gg, 0:NC], w_out_c[:, 1:S + 1, gg, :],
                                                   start=False, stop=True)
                    ins.then_inc(acc_ready, 1)
                emptied(pe, ACC["y"], 2)
                for cc in range(4):
                    k = ACC["yt"] + cc
                    acc_taken(pe, k)
                    for s in range(S):
                        ins = flip(acc[:, k % NB, s * NC:(s + 1) * NC], flat(y_ch[NC * cc:NC * (cc + 1), s, :, :]),
                                   NC, NC * cc)
                    ins.then_inc(acc_ready, 1)
                w = w_unit(u0 + 5, 512)
                pe.wait_ge(ylo_ready, 4)
                yv = [x[:, :].rearrange("p (c l) -> p c l", l=L) for x in (f_hi, f_lo)]
                for j in range(2):
                    out_taken(pe, OUT["glu"] + j)
                    for m in range(2):
                        for c in range(4):
                            ins = mm3(outp[:, (OUT["glu"] + j) % NB, m * L:(m + 1) * L],
                                      [x[:, c, (2 * j + m) * P:(2 * j + m + 1) * P] for x in w],
                                      [x[:, c, :] for x in yv], c == 0, c == 3)
                ins.then_inc(w_used, 1)
                for b in range(2):
                    emptied(pe, ACC[f"pv{b}"])
                pe.wait_ge(glu_lo, 4)
                for j in range(4):
                    proj_n(u0 + 6 + j, OUT["even_out"] + j)

            def odd():
                u0, k0 = UNITS["odd"], OUT["odd"]
                norm(2)
                h_whole(2)
                for j in range(8):
                    proj_t(u0 + j, k0 + j)
                for j in range(4):
                    proj_n(u0 + 8 + j, k0 + 8 + j)
                pe.wait_ge(late_in, 16)
                out_emptied(pe, k0, 12)

                def z_of(h):
                    k = ACC["sb"] + h
                    acc_taken(pe, k)
                    po = (h % 2) * 64
                    kk, qq = sk_t[po:po + 64, h // 2, :], sq_t[po:po + 64, h // 2, :]
                    nc.tensor.matmul(acc[:, k % NB, 0:L], kk[:, 0:P], qq, start=True, stop=False,
                                     skip_group_check=True)
                    nc.tensor.matmul(acc[:, k % NB, L:384], kk[:, P:L], qq[:, P:L], start=False, stop=False,
                                     skip_group_check=True).then_inc(acc_ready, 1)

                def survive(h):
                    k = ACC["sb"] + h
                    pe.wait_ge(sb_sp_done, h + 1)
                    sp_ = sb_sp[:, h % 4, :]
                    nc.tensor.matmul(acc[:, k % NB, 0:L], const("negtri"), sp_[:, 0:L], start=False, stop=False,
                                     skip_group_check=True)
                    nc.tensor.matmul(acc[:, k % NB, P:L], const("negones"), sp_[:, L:384], start=False, stop=False,
                                     skip_group_check=True)
                    nc.tensor.matmul(acc[:, k % NB, L:384], const("negtri"), sp_[:, L:384], start=False, stop=True,
                                     skip_group_check=True).then_inc(sb_cum, 1)

                def values(h):
                    k = OUT["odd_pv"] + h // 4
                    if h % 4 == 0:
                        out_taken(pe, k)
                    pe.wait_ge(sb_w_done, h + 1)
                    po = (h % 2) * 64
                    dst = outp[po:po + 64, k % NB, ((h % 4) // 2) * L:((h % 4) // 2 + 1) * L]
                    w = sb_w[:, h % 4, :]
                    nc.tensor.matmul(dst, sv[:, 0, h * 64:(h + 1) * 64], w[:, 0:L], start=True, stop=False)
                    nc.tensor.matmul(dst[:, P:L], sv[:, 1, h * 64:(h + 1) * 64], w[:, L:384], start=False,
                                     stop=True).then_inc(pv_ready, 1)
                z_of(0)
                z_of(1)
                for h in range(17):
                    if h + 2 < 16:
                        z_of(h + 2)
                    if h < 16:
                        survive(h)
                    if h >= 1:
                        values(h - 1)
                out_emptied(pe, OUT["odd_pv"], 4)
                for j in range(4):
                    proj_n(u0 + 12 + j, OUT["odd_out"] + j)

            def mix():
                u0, k0 = UNITS["mix"], OUT["mix"]
                norm(5)
                h_whole(5)
                for j in range(6):
                    proj_n(u0 + j, k0 + j)
                pe.wait_ge(late2_in, 16 * LATE2)
                for j in range(2):
                    k = ACC["ws"] + j
                    acc_taken(pe, k)
                    for g in range(4):
                        ins = flip(acc[:, k % NB, g * P:(g + 1) * P], ws_nat[:, 4 * j + g, :])
                    ins.then_inc(acc_ready, 1)
                k = ACC["ws"] + 2
                acc_taken(pe, k)
                flip(acc[:, k % NB, 0:8], bs_nat, 8).then_inc(acc_ready, 1)
                for j in range(6, 10):
                    proj_n(u0 + j, k0 + j)
                pe.wait_ge(rot_done, 1)
                for j in range(4):
                    k = ACC["dqk"] + j
                    acc_taken(pe, k)
                    for m in range(2):
                        for t in range(T):
                            ins = flip(acc[:, k % NB, m * L + t * P:m * L + (t + 1) * P],
                                       dqk[:, t, 4 * j + 2 * m:4 * j + 2 * m + 2, :].rearrange("p h d -> p (h d)"))
                    ins.then_inc(acc_ready, 1)
                norm(8)
                h_whole(8)
                for j in range(4):
                    proj_t(u0 + 10 + j, OUT["mem"] + j)
                pe.wait_ge(ln_ready, 1)
                emptied(pe, ACC["ws"], 3)
                for j in range(2):
                    k = ACC["sgu"] + j
                    acc_taken(pe, k)
                    for g in range(4):
                        gg = 4 * j + g
                        ins = nc.tensor.matmul(acc[:, k % NB, g * P:(g + 1) * P], ws_t[:, gg, :],
                                               zv[:, :, gg * 64:(gg + 1) * 64], start=True, stop=True)
                    ins.then_inc(acc_ready, 1)
                emptied(pe, ACC["dqk"], 4)

                def q_of(b, h):
                    return dq_t[64 * b:64 * b + 64, h, :]

                def k_of(b, h):
                    return dk_t[64 * b:64 * b + 64, h, :]
                for b in range(2):
                    scores(ACC["dsc"] + 3 * b, b, q_of, k_of)
                for j in range(4):
                    proj_n(u0 + 14 + j, OUT["mem"] + 4 + j)
                for b in range(2):
                    probs_t(ACC[f"dpt{b}"], b, dsc, 6)
                    emptied(pe, ACC[f"dpt{b}"], 3)
                    k = ACC[f"dpv{b}"]
                    acc_taken(pe, k)
                    for h in range(4):
                        vs = [dv[:, t, (2 * h + b) * 64:(2 * h + b + 1) * 64] for t in range(T)]
                        dst = [acc[:, k % NB, t * 256 + h * 64:t * 256 + (h + 1) * 64] for t in range(T)]
                        p0 = dpt[:, b, h * L:(h + 1) * L]
                        nc.tensor.matmul(dst[0], p0[:, 0:P], vs[0], start=True, stop=True)
                        nc.tensor.matmul(dst[1], p0[:, P:L], vs[0], start=True, stop=False)
                        ins = nc.tensor.matmul(dst[1], dpt[:, b, 1024 + h * P:1024 + (h + 1) * P], vs[1],
                                               start=False, stop=True)
                    ins.then_inc(acc_ready, 1)
                norm(6)
                h_whole(6)
                for j in range(4):
                    proj_n(u0 + 18 + j, OUT["mix_out"] + j)

            def cross():
                u0 = UNITS["cross"]
                norm(7)
                h_whole(7)
                for j in range(4):
                    proj_t(u0 + j, OUT["cross"] + j)
                out_emptied(pe, OUT["mem"], 8)
                out_emptied(pe, OUT["cross"], 4)
                for t in range(T):
                    for j in range(2):
                        k = ACC["xsc"] + 2 * t + j
                        acc_taken(pe, k)
                        for h in range(2):
                            hh = 2 * j + h
                            for c in range(2):
                                ins = nc.tensor.matmul(acc[:, k % NB, h * L:(h + 1) * L],
                                                       xq_t[:, 2 * hh + c, t * P:(t + 1) * P], km_t[:, 2 * hh + c, :],
                                                       start=c == 0, stop=c == 1)
                        ins.then_inc(acc_ready, 1)
                for kt in range(T):
                    for j in range(2):
                        k = ACC["xpt"] + 2 * kt + j
                        acc_taken(pe, k)
                        pe.wait_ge(p_ready, 12 + 3 + j)
                        for h in range(2):
                            for t in range(T):
                                ins = flip(acc[:, k % NB, h * L + t * P:h * L + (t + 1) * P],
                                           xs[:, t, 2 * j + h, kt * P:(kt + 1) * P])
                        ins.then_inc(acc_ready, 1)
                emptied(pe, ACC["xpt"], 4)
                for h in range(4):
                    k = ACC["xpv"] + h
                    acc_taken(pe, k)
                    for c in range(2):
                        for kt in range(T):
                            ins = nc.tensor.matmul(acc[:, k % NB, c * L:(c + 1) * L],
                                                   vm[:, kt, h * 256 + c * P:h * 256 + (c + 1) * P],
                                                   xpt[:, kt, h, :], start=kt == 0, stop=kt == 1)
                    ins.then_inc(acc_ready, 1)
                emptied(pe, ACC["xpv"], 4)
                for j in range(4):
                    proj_n(u0 + 4 + j, OUT["cross_out"] + j)

            if "even" in running:
                even()
            if "ffn0" in running:
                ffn("ffn0")
            if "odd" in running:
                odd()
            if "ffn1" in running:
                ffn("ffn1")
            if "ffn2" in running:
                ffn("ffn2")
            if "mix" in running:
                mix()
            if "cross" in running:
                cross()
            if "ffn3" in running:
                ffn("ffn3")

        @block.gpsimd
        def _(pool):
            own = Own(pool, pool_step)
            gp = nc.gpsimd
            gp.memset(half, -0.5).then_inc(half_ready, 1)
            pool.wait_ge(half_ready, 1)

            def norm(n):
                hs = 2 if n == 6 else 1
                pool.wait_ge(sq_v, SQ[n] + hs)
                pool.wait_ge(sq_a, SQ[n] + hs)
                i = NTH[n]
                cols = slice(0, 4, 2 // hs)
                own.link(gp.tensor_scalar(rms[:, i, cols], ss[:, i, cols], hs / D, EPS, ALU.mult, ALU.add))
                gp.tensor_tensor(rms[:, i, cols], rms[:, i, cols], half[:, 0:2 * hs], ALU.pow).then_inc(rms_ready, 1)

            def root(x, n, scale, eps, done):
                own.link(gp.tensor_scalar(x, x, scale, eps, ALU.mult, ALU.add))
                gp.tensor_tensor(x, x, half[:, 0:n], ALU.pow).then_inc(done, 1)

            def even():
                norm(0)
                emptied(pool, ACC["prep_bc"], 4)
                pool.wait_ge(tab_ready, 1)
                for k in range(S + 1):
                    q1 = tab[:, 2 * S + k, :].unsqueeze(2).to_broadcast([P, G, PC])
                    q2 = tab[:, 3 * S + 1 + k, :].unsqueeze(2).to_broadcast([P, G, PC])
                    dst = w_out_c[:, k, :, :]
                    own.link(gp.tensor_tensor(pool_tmp, q2, ci.rearrange("p c g -> p g c"), ALU.mult))
                    own.link(gp.tensor_tensor(dst, q1, cr.rearrange("p c g -> p g c"), ALU.mult))
                    ins = gp.tensor_tensor(dst, dst, pool_tmp, ALU.add)
                    if k < S:
                        own.link(ins)
                ins.then_inc(wc_ready, 1)
                written(pool, ACC["u"] + 1)
                gp.memset(kpad[:, :, 0:(S - 1) * PC], 0.0).then_inc(kz_ready, 1)
                for t in range(T):
                    pool.wait_ge(qk_sq, t + 1)
                    root(st[:, 80 + 10 * t:90 + 10 * t], 10, 1 / 64, EPS, qk_rms)
                written(pool, ACC["s"] + 1)
                pool.wait_ge(decay_ready, 1)
                own.link(gp.tensor_copy(rho, small[:, 12, :].unsqueeze(2).to_broadcast([P, G, NC])))
                gp.memset(rho[:, :, 0:1], 0.0).then_inc(rho_ready, 1)
                dsk = dskip[0:PC, :, :]
                own.link(gp.tensor_tensor(dsk, dsk, ident[0:PC, 0:PC].unsqueeze(1).to_broadcast([PC, G, PC]),
                                          ALU.mult))
                emptied(pool, ACC["k"], 8)
                lag0 = kpad[:, :, (S - 1) * PC:S * PC]
                gp.tensor_tensor(lag0, lag0, dsk, ALU.add).then_inc(k_ready, 1)

            if "even" in running:
                even()
            if "ffn0" in running:
                norm(1)
            if "odd" in running:
                norm(2)
                for h in range(16):
                    k = ACC["sb"] + h
                    emptied(pool, k)
                    w = sb_w[:, h % 4, :].rearrange("p (a b) -> p a b", b=P)[:, 0:3:2, :]
                    gp.affine_select(out=w, in_=w, compare_op=ALU.is_gt, fill=0.0, base=0,
                                     pattern=[[0, 2], [1, P]], channel_multiplier=-1).then_inc(sb_w_done, 1)
            if "ffn1" in running:
                norm(3)
            if "ffn2" in running:
                norm(4)
            if "mix" in running:
                norm(5)
                norm(8)
                pool.wait_ge(ln_v, 1)
                root(dst_[:, 16:32], 16, 1 / 64, LN_EPS, ln_rms)
                norm(6)
            if "cross" in running:
                norm(7)
            if "ffn3" in running:
                norm(9)
            if "final" in running:
                norm(10)

        @block.scalar
        def _(act):
            own = Own(act, act_step)
            A = nc.scalar.activation

            def split(u, it=0, n=1):
                for u in range(u, u + n):
                    if u >= NU:
                        return
                    act.wait_ge(raw_landed[u % RAW], 16 * (u // RAW + 1) + 32 * it)
                    if u >= 2:
                        act.wait_ge(w_used, u - 1 + 6 * it)
                    A(w_hi[:, u % 2, :], raw[:, u % RAW, :], ACT.Copy).then_inc(w_hi_ready, 1)

            def norm(n, src, gain):
                hs = 2 if n == 6 else 1
                W = D // hs
                for h in range(hs):
                    A(xn[:, 1, h * W:(h + 1) * W], src[:, 1, h * W:(h + 1) * W], ACT.Square,
                      accum_out=ss[:, NTH[n], 2 + h:3 + h]).then_inc(sq_a, 1)
                if n == 10:
                    return
                act.wait_ge(rms_ready, NTH[n] + 1)
                act.wait_ge(sq_a, SQ[n] + hs)
                for h in range(hs):
                    ins = A(xn[:, 1, h * W:(h + 1) * W], src[:, 1, h * W:(h + 1) * W], ACT.Copy,
                            scale=rms[:, NTH[n], 2 + h:3 + h])
                ins.then_inc(xn_a, 1)
                for q in range(4):
                    k = ACC[f"norm{n}"] + q
                    written(act, k)
                    for c in range(2):
                        A(h_hi[:, 2 * q + c, :], acc[:, k % NB, c * L:(c + 1) * L], ACT.Copy,
                          scale=gain[:, 2 * q + c:2 * q + c + 1]).then_inc(h_hi_ready, 1)

            def ffn(name):
                _, f, _, _, _, _, n = FFN[name]
                u0, k0 = UNITS[name], OUT[name]
                x_whole(act, X_FROM[n])
                norm(n, x_sb, gains[:, n, :])
                split(u0 + 2, n=2)

                def gate(i, it=0):
                    j, k = NF * f + i, k0 + 2 * i
                    act.wait_ge(w_used, (u0 + 1 if i == 0 else u0 + 3 * i) + 6 * it)
                    if i >= 1:
                        act.wait_ge(out_free[(k + 1) % NB], (k + 1) // NB + it)
                    A(silu[:, j % 2, :], outp[:, k % NB, :], ACT.Silu).then_inc(out_free[k % NB], 1)
                    out_emptied(act, k + 1, it=it)
                    if i >= 1:
                        act.wait_ge(w_used, u0 + 3 * i - 1 + 6 * it)
                    A(f_hi[:, (j % 2) * 512:(j % 2 + 1) * 512], hf[:, j % 2, :], ACT.Copy).then_inc(f_hi_done, 1)

                def turn(i, it=0):
                    gate(i, it)
                    split(u0 + 4 + 3 * i, it, 3)
                turn(0)
                with act.Fori(0, 4) as it:
                    turn(1, it)
                    turn(2, it)
                turn(9)
                gate(10)
                split(u0 + 34)

            def even():
                u0, k0 = UNITS["even"], OUT["even"]
                act.wait_ge(x_loaded, 16)
                split(0, n=2)
                act.wait_ge(gain0_in, 16)
                norm(0, x_sb, gains[:, 0, :])
                act.wait_ge(small_in, 16 * SMALL)
                A(small[:, 0, :], log_dt, ACT.Exp).then_inc(dt_ready, 1)
                for j, dst in enumerate([br, bi, cr, ci]):
                    k = ACC["prep_bc"] + j
                    written(act, k)
                    A(dst.rearrange("p c g -> p (c g)"), acc[:, k % NB, :], ACT.Copy).then_inc(acc_free[k % NB], 1)
                act.wait_ge(lam_mag, 1)
                A(tmp_u, tmp_u, ACT.Exp).then_inc(lam_exp, 1)
                A(small[:, 12, :], small[:, 1, :], ACT.Exp, scale=float(S)).then_inc(decay_ready, 1)
                act.wait_ge(lam_frac, 1)
                A(tmp_t, tmp_t, ACT.Sin, scale=TWO_PI).then_inc(lam_sin, 1)
                act.wait_ge(al_frac, 1)
                A(alpha, alpha, ACT.Sin, scale=TWO_PI).then_inc(al_sin, 1)

                for j in range(2):
                    act.wait_ge(w_used, u0 + j + 1)
                    k = k0 + j
                    A(flat(u_t[:, 2 * j:2 * j + 2, :]), outp[:, k % NB, :], ACT.Copy).then_inc(out_free[k % NB], 1)
                    split(u0 + 2 + j)
                for j in range(2):
                    for q in range(0, 4, 2):
                        k = ACC["uc"] + 4 * j + q
                        written(act, k)
                        A(uc_part(j, q), uc_bank(k), ACT.Copy).then_inc(acc_free[k % NB], 1)
                for j in range(3):
                    act.wait_ge(w_used, u0 + 2 + j + 1)
                    k = k0 + 2 + j
                    src = outp[:, k % NB, :].rearrange("p (t n) -> p t n", n=UW)
                    if j < 2:
                        for t in range(T):
                            ins = A(qkv[:, t, 0:512].rearrange("p (h b d) -> p h b d", b=2, d=64)[:, :, j, :],
                                    src[:, t, :].rearrange("p (h d) -> p h d", d=64), ACT.Copy)
                    else:
                        ins = A(qkv[:, :, 512:768], src, ACT.Copy)
                    ins.then_inc(out_free[k % NB], 1)
                    split(u0 + 4 + j)
                for j in range(8):
                    acc_copy(ACC["vt"] + j, flat(vt[:, 4 * j:4 * j + 4, :]))
                for j in range(2):
                    acc_copy(ACC["s"] + j, s_ch[:, j * 512:(j + 1) * 512])
                for j in range(8):
                    acc_copy(ACC["k"] + j, kpad[:, 4 * j:4 * j + 4, (S - 1) * PC:], PC, P)
                for j in range(3):
                    k = ACC["qk"] + j
                    written(act, k)
                    dst, w = (flat(q_t[:, 2 * j:2 * j + 2, :]), 512) if j < 2 else (k_t, L)
                    A(dst, acc[:, k % NB, 0:w], ACT.Copy,
                      scale=qk_gain[:, (j == 2) * 1:(j == 2) * 1 + 1]).then_inc(acc_free[k % NB], 1)
                for n in range(6):
                    act.wait_ge(sub_done, n + 1)
                    sk = st[:, 24 + 4 * n:24 + 4 * n + (2 if n % 3 else 4)]
                    A(sk, sk, ACT.Exp).then_inc(exp_done, 1)
                    tile = sc[:, n // 3, (n % 3) * 512:(n % 3 + 1) * 512]
                    A(tile, tile, ACT.Exp).then_inc(exp_done, 1)
                for b in range(2):
                    for j in range(3):
                        acc_copy(ACC[f"pt{b}"] + j, pt[:, b, j * 512:(j + 1) * 512])
                    mix_part(ACC[f"pv{b}"], 2 * b)
                for j in range(2):
                    k = ACC["y"] + j
                    written(act, k)
                    A(y_ch[:, :, 4 * j:4 * j + 4, :].rearrange("p s g c -> p g s c"),
                      acc[:, k % NB, :].rearrange("p (g s c) -> p g s c", g=4, c=PC),
                      ACT.Copy).then_inc(acc_free[k % NB], 1)
                for cc in range(4):
                    k = ACC["yt"] + cc
                    written(act, k)
                    A(y_f[:, cc, :].rearrange("p (c s) -> p s c", s=S),
                      acc[:, k % NB, 0:L].rearrange("p (s c) -> p s c", c=NC),
                      ACT.Gelu_apprx_tanh).then_inc(acc_free[k % NB], 1)
                for cc in range(4):
                    emptied(act, ACC["yt"] + cc)
                    A(f_hi[:, cc * L:(cc + 1) * L], y_f[:, cc, :], ACT.Copy).then_inc(yhi_ready, 1)
                act.wait_ge(w_used, u0 + 6)
                for j in range(2):
                    k = OUT["glu"] + j
                    for m in range(2):
                        cc = 2 * j + m
                        ins = A(sig[:, cc, :], outp[:, k % NB, m * L:(m + 1) * L], ACT.Sigmoid,
                                bias=b_glu[:, cc:cc + 1])
                        if m == 1:
                            ins.then_inc(out_free[k % NB], 1)
                split(u0 + 7)
                for cc in range(4):
                    act.wait_ge(glu_done, cc + 1)
                    A(h_hi[:, 4 + cc, :], sig[:, cc, :], ACT.Copy).then_inc(glu_hi, 1)
                for j in range(4):
                    split(u0 + 8 + j)

            def acc_copy(k, dst, parts=P, inner=512):
                written(act, k)
                src = acc[0:parts, k % NB, :]
                if inner < 512:
                    src = src.rearrange("p (a b) -> p a b", b=inner)
                A(dst, src, ACT.Copy).then_inc(acc_free[k % NB], 1)

            def mix_part(k, c):
                written(act, k)
                A(flat(h_hi[:, c:c + 2, :]), acc[:, k % NB, :], ACT.Copy).then_inc(mix_hi, 1)

            def odd():
                u0, k0 = UNITS["odd"], OUT["odd"]
                x_whole(act, X_FROM[2])
                norm(2, x_sb, gains[:, 2, :])
                for j in range(12):
                    if not 4 <= j < 8:
                        act.wait_ge(w_used, u0 + j + 1)
                        k = k0 + j
                        if j < 4:
                            A(flat(sq_t[:, 2 * j:2 * j + 2, :]), outp[:, k % NB, :], ACT.Copy,
                              scale=0.125).then_inc(out_free[k % NB], 1)
                        else:
                            A(sv[:, :, (j - 8) * UW:(j - 7) * UW], outp[:, k % NB, :].rearrange("p (t n) -> p t n", n=UW),
                              ACT.Copy).then_inc(out_free[k % NB], 1)
                    split(u0 + 2 + j)

                def softplus(h):
                    k = ACC["sb"] + h
                    written(act, k)
                    if h >= 4:
                        act.wait_ge(sb_sp_done, h - 3)
                    e = sb_e[:, h % 4, :]
                    own.link(A(e, acc[:, k % NB, 0:384], ACT.Abs))
                    own.link(A(e, e, ACT.Exp, scale=-1.0))
                    A(e, e, ACT.Ln, bias=1.0).then_inc(sb_ln, 1)

                def weigh(h):
                    k = ACC["sb"] + h
                    act.wait_ge(sb_cum, h + 1)
                    if h >= 4:
                        act.wait_ge(pv_ready, h - 3)
                    A(sb_w[:, h % 4, :], acc[:, k % NB, 0:384], ACT.Exp).then_inc(acc_free[k % NB], 1)

                def pv(j):
                    k = OUT["odd_pv"] + j
                    act.wait_ge(pv_ready, 4 * j + 4)
                    A(flat(h_hi[:, 2 * j:2 * j + 2, :]), outp[:, k % NB, :], ACT.Copy).then_inc(mix_hi, 1)
                softplus(0)
                for h in range(16):
                    if h + 1 < 16:
                        softplus(h + 1)
                    weigh(h)
                    if h % 4 == 1 and h > 4:
                        pv(h // 4 - 1)
                pv(3)
                for j in range(4):
                    split(u0 + 14 + j)

            def mix():
                u0, k0 = UNITS["mix"], OUT["mix"]
                x_whole(act, X_FROM[5])
                norm(5, x_sb, gains[:, 5, :])
                act.wait_ge(rope_frac, 1)
                own.link(A(rot[:, 2, :, :], rot[:, 1, :, :], ACT.Sin, scale=0.5))
                A(rot[:, 3, :, :], rot[:, 1, :, :], ACT.Sin).then_inc(rope_sin, 1)
                for j in range(10):
                    act.wait_ge(w_used, u0 + j + 1)
                    k = k0 + j
                    src = outp[:, k % NB, :].rearrange("p (t n) -> p t n", n=UW)
                    if j < 4:
                        A(dqk[:, :, 4 * j:4 * j + 4, :].rearrange("p t h d -> p t (h d)"), src,
                          ACT.Copy).then_inc(out_free[k % NB], 1)
                    elif j < 6:
                        A(dv[:, :, (j - 4) * UW:(j - 3) * UW], src, ACT.Copy).then_inc(out_free[k % NB], 1)
                    else:
                        dst = (zu if j < 8 else zv)[:, :, (j % 2) * UW:(j % 2 + 1) * UW]
                        A(dst, src, ACT.Gelu).then_inc(out_free[k % NB], 1)
                    split(u0 + 2 + j)
                for j in range(4):
                    acc_copy(ACC["dqk"] + j, flat((dq_t if j < 2 else dk_t)[:, 2 * (j % 2):2 * (j % 2) + 2, :]))
                act.wait_ge(mem_in, 16)
                norm(8, mem_sb, gains[:, 8, :])
                for j in range(4):
                    act.wait_ge(w_used, u0 + 10 + j + 1)
                    k = OUT["mem"] + j
                    A(flat(km_t[:, 2 * j:2 * j + 2, :]), outp[:, k % NB, :], ACT.Copy).then_inc(out_free[k % NB], 1)
                    split(u0 + 12 + j)
                for n in range(6):
                    act.wait_ge(sub_done, 6 + n + 1)
                    tile = dsc[:, n // 3, (n % 3) * 512:(n % 3 + 1) * 512]
                    A(tile, tile, ACT.Exp).then_inc(exp_done, 1)
                for j in range(4):
                    act.wait_ge(w_used, u0 + 14 + j + 1)
                    k = OUT["mem"] + 4 + j
                    A(vm[:, :, j * UW:(j + 1) * UW], outp[:, k % NB, :].rearrange("p (t n) -> p t n", n=UW),
                      ACT.Copy).then_inc(out_free[k % NB], 1)
                    split(u0 + 16 + j)
                for b in range(2):
                    for j in range(3):
                        acc_copy(ACC[f"dpt{b}"] + j, dpt[:, b, j * 512:(j + 1) * 512])
                    k = ACC[f"dpv{b}"]
                    written(act, k)
                    for t in range(T):
                        ins = A(y_nat[:, t, 512:].rearrange("p (h b d) -> p h b d", b=2, d=64)[:, :, b, :],
                                acc[:, k % NB, t * 256:(t + 1) * 256].rearrange("p (h d) -> p h d", d=64), ACT.Copy)
                    ins.then_inc(acc_free[k % NB], 1)
                emptied(act, ACC["sgu"], 2)
                for b in range(2):
                    emptied(act, ACC[f"dpv{b}"])
                norm(6, y_nat, g_ab)
                for j in range(4):
                    split(u0 + 20 + j)

            def cross():
                u0 = UNITS["cross"]
                x_whole(act, X_FROM[7])
                norm(7, x_sb, gains[:, 7, :])
                for j in range(4):
                    act.wait_ge(w_used, u0 + j + 1)
                    k = OUT["cross"] + j
                    A(flat(xq_t[:, 2 * j:2 * j + 2, :]), outp[:, k % NB, :], ACT.Copy).then_inc(out_free[k % NB], 1)
                    split(u0 + 2 + j)
                for n in range(4):
                    act.wait_ge(sub_done, 12 + n + 1)
                    tile = flat(xs[:, n // 2, 2 * (n % 2):2 * (n % 2) + 2, :])
                    A(tile, tile, ACT.Exp).then_inc(exp_done, 1)
                for kt in range(T):
                    for j in range(2):
                        acc_copy(ACC["xpt"] + 2 * kt + j, flat(xpt[:, kt, 2 * j:2 * j + 2, :]))
                for h in range(4):
                    mix_part(ACC["xpv"] + h, 2 * h)
                for j in range(4):
                    split(u0 + 6 + j)

            if "even" in running:
                even()
            if "ffn0" in running:
                ffn("ffn0")
            if "odd" in running:
                odd()
            if "ffn1" in running:
                ffn("ffn1")
            if "ffn2" in running:
                ffn("ffn2")
            if "mix" in running:
                mix()
            if "cross" in running:
                cross()
            if "ffn3" in running:
                ffn("ffn3")
            if "final" in running:
                x_whole(act, X_FROM[10])
                norm(10, x_sb, None)

        @block.vector
        def _(dve):
            own = Own(dve, dve_step)
            V = nc.vector
            tt, ts, stt = V.tensor_tensor, V.tensor_scalar, V.scalar_tensor_tensor
            link = own.link

            def split(u, it=0, n=1):
                for u in range(u, u + n):
                    if u >= NU:
                        return
                    dve.wait_ge(w_hi_ready, u + 1 + 6 * it)
                    tt(w_lo[:, u % 2, :], raw[:, u % RAW, :], w_hi[:, u % 2, :].bitcast(F32),
                       ALU.subtract).then_inc(w_lo_ready, 1)

            def norm_front(n, src):
                hs = 2 if n == 6 else 1
                W = D // hs
                for h in range(hs):
                    V.tensor_tensor_reduce(out=xn[:, 0, h * W:(h + 1) * W], in0=src[:, 0, h * W:(h + 1) * W],
                                           in1=src[:, 0, h * W:(h + 1) * W], scale=1.0, scalar=0.0, op0=ALU.mult,
                                           op1=ALU.add, accum_out=ss[:, NTH[n], h:h + 1]).then_inc(sq_v, 1)
                dve.wait_ge(rms_ready, NTH[n] + 1)
                dve.wait_ge(sq_v, SQ[n] + hs)
                if n == 10:
                    dve.wait_ge(fin_in, 16)
                    for t in range(T):
                        stt(xn[:, t, :], src[:, t, :], rms[:, NTH[n], 2 * t:2 * t + 1], fin_g, ALU.mult,
                            ALU.mult).then_inc([xn_v, xn_a][t], 1)
                    return
                for h in range(hs):
                    ins = ts(xn[:, 0, h * W:(h + 1) * W], src[:, 0, h * W:(h + 1) * W], rms[:, NTH[n], h:h + 1], None,
                             ALU.mult)
                ins.then_inc(xn_v, 1)

            def norm_back(n, gain):
                for q in range(4):
                    k = ACC[f"norm{n}"] + q
                    dve.wait_ge(h_hi_ready, 8 * NTH[n] + 2 * q + 2)
                    for c in range(2):
                        ch = 2 * q + c
                        ins = stt(h_lo[:, ch, :], acc[:, k % NB, c * L:(c + 1) * L], gain[:, ch:ch + 1],
                                  h_hi[:, ch, :].bitcast(F32), ALU.mult, ALU.subtract)
                    ins.then_inc(acc_free[k % NB], 1)

            def ffn(name):
                _, f, _, _, _, scale, n = FFN[name]
                u0, k0, d0 = UNITS[name], OUT[name], ACC[name]
                x_whole(dve, X_FROM[n])
                norm_front(n, x_sb)
                norm_back(n, gains[:, n, :])
                split(u0 + 2, n=2)

                def product(i, it=0):
                    j, k = NF * f + i, k0 + 2 * i
                    out_emptied(dve, k, it=it)
                    dve.wait_ge(w_used, (u0 + 2 if i == 0 else u0 + 3 * i + 1) + 6 * it)
                    if j >= 2:
                        dve.wait_ge(f_hi_done, j - 1 + 2 * it)
                        dve.wait_ge(f_lo_done, j - 1 + 2 * it)
                    b = j % 2
                    tt(hf[:, b, :], silu[:, b, :], outp[:, (k + 1) % NB, :], ALU.mult).then_inc(out_free[(k + 1) % NB], 1)
                    out_emptied(dve, k + 1, it=it)
                    dve.wait_ge(f_hi_done, j + 1 + 2 * it)
                    tt(f_lo[:, b * 512:(b + 1) * 512], hf[:, b, :], f_hi[:, b * 512:(b + 1) * 512].bitcast(F32),
                       ALU.subtract).then_inc(f_lo_done, 1)

                def turn(i, it=0):
                    product(i, it)
                    split(u0 + 4 + 3 * i, it, 3)
                turn(0)
                with dve.Fori(0, 4) as it:
                    turn(1, it)
                    turn(2, it)
                turn(9)
                product(10)
                split(u0 + 34)
                dve.wait_ge(w_used, u0 + 33)
                for t in range(T):
                    for h in range(2):
                        k = d0 + 2 * t + h
                        xs_ = x_sb[:, t, h * 512:(h + 1) * 512]
                        stt(xs_, acc[:, k % NB, :], scale, xs_, ALU.mult, ALU.add).then_inc(acc_free[k % NB], 1)

            def add_out(u, k):
                for j in range(4):
                    dve.wait_ge(w_used, u + j + 1)
                    xs_ = x_sb[:, :, j * UW:(j + 1) * UW]
                    tt(xs_, xs_, outp[:, (k + j) % NB, :].rearrange("p (t n) -> p t n", n=UW),
                       ALU.add).then_inc(out_free[(k + j) % NB], 1)
                    split(u + j + 2)

            def softmax(tiles, scale, k, done, exps, sink=False):
                per = 2 if sink else 1

                def front(n):
                    s, mask, sk = tiles[n]
                    _, h, w = s.shape
                    written(dve, k + n)
                    src = acc[:, (k + n) % NB, :].rearrange("p (h w) -> p h w", w=w)
                    if mask is None:
                        ins = ts(s, src, scale, None, ALU.mult)
                    else:
                        for i in range(h):
                            ins = stt(s[:, i, :], src[:, i, :], scale, mask, ALU.mult, ALU.add)
                    ins.then_inc(acc_free[(k + n) % NB], 1)
                    emptied(dve, k + n)
                    mx = st[:, 4 * n:4 * n + h]
                    link(V.reduce_max(mx, s, AX))
                    if sink:
                        link(tt(mx, mx, sk, ALU.max))
                        link(tt(st[:, 24 + 4 * n:24 + 4 * n + h], sk, mx, ALU.subtract))
                    tt(s, s, mx.unsqueeze(2).to_broadcast([P, h, w]), ALU.subtract).then_inc(sub_done, 1)

                def back(n):
                    s = tiles[n][0]
                    _, h, w = s.shape
                    dve.wait_ge(exp_done, exps + per * (n + 1))
                    sm = st[:, 48 + 4 * n:48 + 4 * n + h]
                    link(V.reduce_sum(sm, s, AX))
                    if sink:
                        link(tt(sm, sm, st[:, 24 + 4 * n:24 + 4 * n + h], ALU.add))
                    link(V.reciprocal(sm, sm))
                    tt(s, s, sm.unsqueeze(2).to_broadcast([P, h, w]), ALU.mult).then_inc(p_ready, 1)
                front(0)
                for n in range(len(tiles)):
                    if n + 1 < len(tiles):
                        front(n + 1)
                    back(n)

            def mix_low(n, k, c):
                dve.wait_ge(mix_hi, n + 1)
                tt(flat(h_lo[:, c:c + 2, :]), acc[:, k % NB, :], flat(h_hi[:, c:c + 2, :]).bitcast(F32),
                   ALU.subtract).then_inc(acc_free[k % NB], 1)

            def turns_off(x, n):
                link(ts(n, x, MAGIC, MAGIC, ALU.add, ALU.subtract))
                return tt(x, x, n, ALU.subtract)

            def radians_off(r, x, n):
                link(ts(n, x, float(1 / (2 * np.pi)), MAGIC, ALU.mult, ALU.add))
                link(ts(n, n, MAGIC, None, ALU.subtract))
                link(stt(r, n, -PI_A, x, ALU.mult, ALU.add))
                link(stt(r, n, -PI_B, r, ALU.mult, ALU.add))
                return stt(r, n, -PI_C, r, ALU.mult, ALU.add)

            def even():
                u0, k0 = UNITS["even"], OUT["even"]
                dve.wait_ge(x_loaded, 16)
                split(0, n=2)
                norm_front(0, x_sb)
                norm_back(0, gains[:, 0, :])
                k = ACC["prep_a"]
                written(dve, k)
                V.tensor_copy(flat(a_t), acc[:, k % NB, 0:2 * G]).then_inc(acc_free[k % NB], 1)
                emptied(dve, k)
                dve.wait_ge(dt_ready, 1)
                are, aim = a_t[:, 0, :], a_t[:, 1, :]
                sm = [small[:, j, :] for j in range(16)]
                link(tt(sm[1], are, sm[0], ALU.mult))
                link(tt(sm[2], aim, sm[0], ALU.mult))
                tt(tmp_u, steps.unsqueeze(2).to_broadcast([P, 36, G]), sm[1].unsqueeze(1).to_broadcast([P, 36, G]),
                   ALU.mult).then_inc(lam_mag, 1)
                link(radians_off(sm[4], sm[2], sm[3]))
                link(ts(sm[5], sm[4], float(1 / (2 * np.pi)), None, ALU.mult))
                link(tt(tmp_t, steps.unsqueeze(2).to_broadcast([P, 36, G]),
                        sm[5].unsqueeze(1).to_broadcast([P, 36, G]), ALU.mult))
                link(tt(tmp_t, tmp_t, phase.unsqueeze(2).to_broadcast([P, 36, G]), ALU.add))
                turns_off(tmp_t, tmp_n).then_inc(lam_frac, 1)
                link(ts(sm[6], sm[5], float(S), None, ALU.mult))
                link(turns_off(sm[6], sm[3]))
                link(tt(alpha[:, 1, :, :], sm[6].unsqueeze(2).to_broadcast([P, G, NC]),
                        chunk.unsqueeze(1).to_broadcast([P, G, NC]), ALU.mult))
                link(ts(alpha[:, 0, :, :], alpha[:, 1, :, :], 0.25, None, ALU.add))
                turns_off(alpha.rearrange("p a g c -> p (a g c)"), flat(xn[:, :, :])).then_inc(al_frac, 1)
                dve.wait_ge(lam_exp, 1)
                dve.wait_ge(lam_sin, 1)
                tt(tab, tmp_t, tmp_u, ALU.mult).then_inc(tab_ready, 1)
                dve.wait_ge(tab_ready, 1)
                split(u0 + 2)
                lre, lim = tab[:, 34, :], tab[:, 35, :]
                link(tt(sm[7], are, are, ALU.mult))
                link(tt(sm[8], aim, aim, ALU.mult))
                link(tt(sm[7], sm[7], sm[8], ALU.add))
                link(V.reciprocal(sm[8], sm[7]))
                link(ts(sm[11], lre, -1.0, None, ALU.add))
                link(tt(sm[9], sm[11], are, ALU.mult))
                link(tt(sm[10], lim, aim, ALU.mult))
                link(tt(sm[9], sm[9], sm[10], ALU.add))
                link(tt(sm[10], lim, are, ALU.mult))
                link(tt(sm[13], sm[11], aim, ALU.mult))
                link(tt(sm[10], sm[10], sm[13], ALU.subtract))
                link(tt(sm[9], sm[9], sm[8], ALU.mult))
                link(tt(sm[10], sm[10], sm[8], ALU.mult))
                emptied(dve, ACC["prep_bc"], 4)
                wr = sm[9].unsqueeze(1).to_broadcast([P, PC, G])
                wi = sm[10].unsqueeze(1).to_broadcast([P, PC, G])
                scr = view(REG_V, PC, G)
                link(tt(scr, wi, bi, ALU.mult))
                link(tt(cbr, wr, br, ALU.mult))
                link(tt(cbr, cbr, scr, ALU.subtract))
                link(tt(scr, wi, br, ALU.mult))
                link(tt(cbi, wr, bi, ALU.mult))
                link(tt(cbi, cbi, scr, ALU.add))
                V.tensor_copy(bst[0:N, :, :], cbr[0:N, :, :]).then_inc(bb_ready, 1)
                V.tensor_copy(bst[N:P, :, :], cbi[N:P, :, :]).then_inc(bb_ready, 1)
                split(u0 + 3)

                def carry_in(s0):
                    n = S // 2
                    dst = v_in[:, :, s0:s0 + n, :].rearrange("p g s c -> p s g c")
                    scr = flat(xn[:, :, :]).rearrange("p (s g c) -> p s g c", s=n, c=PC)
                    shape = [P, n, G, PC]
                    p1 = tab[:, s0:s0 + n, :].unsqueeze(3).to_broadcast(shape)
                    p2 = tab[:, S + s0:S + s0 + n, :].unsqueeze(3).to_broadcast(shape)
                    link(tt(scr, p2, cbi.rearrange("p c g -> p g c").unsqueeze(1).to_broadcast(shape), ALU.mult))
                    link(tt(dst, p1, cbr.rearrange("p c g -> p g c").unsqueeze(1).to_broadcast(shape), ALU.mult))
                    return tt(dst, dst, scr, ALU.add)

                def uc_copy(j):
                    for q in range(1, 4, 2):
                        k = ACC["uc"] + 4 * j + q
                        written(dve, k)
                        V.tensor_copy(uc_part(j, q), uc_bank(k)).then_inc(acc_free[k % NB], 1)
                uc_copy(0)
                uc_copy(1)
                link(carry_in(0))
                split(u0 + 4)
                carry_in(S // 2).then_inc(v_ready, 1)
                split(u0 + 5)
                split(u0 + 6)
                out_emptied(dve, k0 + 2, 3)
                for t in range(T):
                    qk = qkv[:, t, 0:640]
                    scr = arena[:, o_u:o_u + 640]
                    if t:
                        dve.wait_ge(qk_sq, t)
                    link(tt(scr, qk, qk, ALU.mult))
                    V.reduce_sum(st[:, 80 + 10 * t:90 + 10 * t], scr.rearrange("p (h d) -> p h d", d=64),
                                 AX).then_inc(qk_sq, 1)
                for t in range(T):
                    qk = qkv[:, t, 0:640].rearrange("p (h d) -> p h d", d=64)
                    dve.wait_ge(qk_rms, t + 1)
                    ins = tt(qk, qk, st[:, 80 + 10 * t:90 + 10 * t].unsqueeze(2).to_broadcast([P, 10, 64]), ALU.mult)
                    if t == 0:
                        link(ins)
                ins.then_inc(qk_ready, 1)
                for j in range(2):
                    k = ACC["u"] + j
                    written(dve, k)
                    V.tensor_copy(flat(u_ch[:, 16 * j:16 * j + 16, :]), acc[:, k % NB, :]).then_inc(acc_free[k % NB], 1)
                dve.wait_ge(al_sin, 1)
                cos_, sin_ = [alpha[:, j, :, :].rearrange("p g c -> p (g c)") for j in range(2)]
                gf = flat(g_st)
                for j in range(2):
                    k = ACC["js"] + j
                    o = slice(j * 512, (j + 1) * 512)
                    written(dve, k)
                    tt(t_ch[:, o], sin_[:, o], acc[:, k % NB, :], ALU.mult).then_inc(acc_free[k % NB], 1)
                    link(tt(gf[:, o], cos_[:, o], s_ch[:, o], ALU.mult))
                    emptied(dve, k)
                    link(tt(gf[:, o], gf[:, o], t_ch[:, o], ALU.subtract))
                dve.wait_ge(rho_ready, 1)
                V.tensor_tensor_scan(gf, flat(rho), gf, 0.0, ALU.mult, ALU.add).then_inc(g_ready, 1)
                dve.wait_ge(m_in_done, 16 * S)
                dve.wait_ge(g_ready, 1)
                V.memset(hpad[:, :, 0:1], 0.0).then_inc(h_ready, 1)
                for j in range(2):
                    k = ACC["jg"] + j
                    o = slice(j * 512, (j + 1) * 512)
                    written(dve, k)
                    tt(t_ch[:, o], sin_[:, o], acc[:, k % NB, :], ALU.mult).then_inc(acc_free[k % NB], 1)
                    link(tt(s_ch[:, o], cos_[:, o], gf[:, o], ALU.mult))
                    emptied(dve, k)
                    tt(hpad[:, 16 * j:16 * j + 16, 1:], s_ch[:, o].rearrange("p (g c) -> p g c", c=NC),
                       t_ch[:, o].rearrange("p (g c) -> p g c", c=NC), ALU.add).then_inc(h_ready, 1)
                tiles = []
                for b in range(2):
                    tiles.append((sc[:, b, 0:512].rearrange("p (h w) -> p h w", w=P), swa_mask[:, 0:P],
                                  sinks[:, 4 * b:4 * b + 4]))
                    for j in range(2):
                        tiles.append((sc[:, b, 512 * (j + 1):512 * (j + 2)].rearrange("p (h w) -> p h w", w=L),
                                      swa_mask[:, P:384], sinks[:, 4 * b + 2 * j:4 * b + 2 * j + 2]))
                softmax(tiles, 0.125, ACC["sc"], 0, 0, sink=True)
                for b in range(2):
                    mix_low(b, ACC[f"pv{b}"], 2 * b)
                for cc in range(4):
                    dve.wait_ge(yhi_ready, cc + 1)
                    tt(f_lo[:, cc * L:(cc + 1) * L], y_f[:, cc, :], f_hi[:, cc * L:(cc + 1) * L].bitcast(F32),
                       ALU.subtract).then_inc(ylo_ready, 1)
                out_emptied(dve, OUT["glu"], 2)
                for cc in range(4):
                    tt(sig[:, cc, :], sig[:, cc, :], y_f[:, cc, :], ALU.mult).then_inc(glu_done, 1)
                split(u0 + 7)
                for cc in range(4):
                    dve.wait_ge(glu_hi, cc + 1)
                    tt(h_lo[:, 4 + cc, :], sig[:, cc, :], h_hi[:, 4 + cc, :].bitcast(F32),
                       ALU.subtract).then_inc(glu_lo, 1)
                add_out(u0 + 6, OUT["even_out"])

            def odd():
                u0, k0 = UNITS["odd"], OUT["odd"]
                x_whole(dve, X_FROM[2])
                norm_front(2, x_sb)
                norm_back(2, gains[:, 2, :])
                for j in range(12):
                    if 4 <= j < 8:
                        dve.wait_ge(w_used, u0 + j + 1)
                        k = k0 + j
                        V.tensor_copy(flat(sk_t[:, 2 * (j - 4):2 * (j - 4) + 2, :]),
                                      outp[:, k % NB, :]).then_inc(out_free[k % NB], 1)
                    split(u0 + 2 + j)
                dve.wait_ge(late_in, 16)
                for h in range(16):
                    k = ACC["sb"] + h
                    dve.wait_ge(sb_ln, h + 1)
                    if h >= 4:
                        dve.wait_ge(sb_cum, h - 3)
                    b = sb_sp[:, h % 4, :]
                    link(stt(b, acc[:, k % NB, 0:384], 0.0, sb_e[:, h % 4, :], ALU.max, ALU.add))
                    d = b.rearrange("p (a b) -> p a b", b=P)[:, 0:3:2, :]
                    tt(d, d, const("strict").unsqueeze(1).to_broadcast([P, 2, P]), ALU.mult).then_inc(sb_sp_done, 1)
                for j in range(4):
                    k = OUT["odd_pv"] + j
                    dve.wait_ge(mix_hi, 2 + j + 1)
                    tt(flat(h_lo[:, 2 * j:2 * j + 2, :]), outp[:, k % NB, :],
                       flat(h_hi[:, 2 * j:2 * j + 2, :]).bitcast(F32), ALU.subtract).then_inc(out_free[k % NB], 1)
                add_out(u0 + 12, OUT["odd_out"])

            def mix():
                u0, k0 = UNITS["mix"], OUT["mix"]
                x_whole(dve, X_FROM[5])
                norm_front(5, x_sb)
                norm_back(5, gains[:, 5, :])
                dve.wait_ge(late2_in, 16 * LATE2)
                link(V.tensor_copy(pos_f, pos_i[:, :]))
                link(tt(rot[:, 0, :, :], pos_f.unsqueeze(2).to_broadcast([P, T, 8]),
                        const("invf").unsqueeze(1).to_broadcast([P, T, 8]), ALU.mult))
                r1 = flat(rot[:, 1, :, :])
                link(radians_off(r1, flat(rot[:, 0, :, :]), flat(rot[:, 2, :, :])))
                ts(r1, r1, 3.1415925, -3.1415925, ALU.min, ALU.max).then_inc(rope_frac, 1)
                for j in range(4):
                    split(u0 + 2 + j)
                dve.wait_ge(rope_sin, 1)
                link(tt(rot[:, 4, :, :], rot[:, 2, :, :], rot[:, 2, :, :], ALU.mult))
                link(ts(rot[:, 4, :, :], rot[:, 4, :, :], -2.0, 1.0, ALU.mult, ALU.add))
                out_emptied(dve, k0, 4)
                cosb = rot[:, 4, :, :].unsqueeze(2).to_broadcast([P, T, 16, 8])
                sinb = rot[:, 3, :, :].unsqueeze(2).to_broadcast([P, T, 16, 8])
                x1, x2 = dqk[:, :, :, 0:8], dqk[:, :, :, 8:16]
                r = [ropet[:, j, :, :, :] for j in range(4)]
                link(tt(r[0], x1, cosb, ALU.mult))
                link(tt(r[1], x2, sinb, ALU.mult))
                link(tt(r[2], x2, cosb, ALU.mult))
                link(tt(r[3], x1, sinb, ALU.mult))
                link(tt(x1, r[0], r[1], ALU.subtract))
                tt(x2, r[2], r[3], ALU.add).then_inc(rot_done, 1)
                split(u0 + 6)
                split(u0 + 7)
                for j in range(2):
                    k = ACC["ws"] + j
                    written(dve, k)
                    tt(ws_t[:, 4 * j:4 * j + 4, :], acc[:, k % NB, :].rearrange("p (g i) -> p g i", i=P),
                       const("tril").unsqueeze(1).to_broadcast([P, 4, P]), ALU.mult).then_inc(acc_free[k % NB], 1)
                k = ACC["ws"] + 2
                written(dve, k)
                V.tensor_copy(bs_t, acc[:, k % NB, 0:8]).then_inc(acc_free[k % NB], 1)
                for j in range(4):
                    split(u0 + 8 + j)
                dve.wait_ge(mem_in, 16)
                norm_front(8, mem_sb)
                norm_back(8, gains[:, 8, :])
                out_emptied(dve, k0 + 8, 2)
                z = zv.rearrange("p t (g c) -> p (t g) c", c=64)
                zq = zs.rearrange("p t (g c) -> p (t g) c", c=64)
                mean, var = dst_[:, 0:16], dst_[:, 16:32]
                wide = [P, 16, 64]
                link(V.reduce_sum(mean, z, AX))
                link(ts(mean, mean, 1 / 64, None, ALU.mult))
                link(tt(z, z, mean.unsqueeze(2).to_broadcast(wide), ALU.subtract))
                split(u0 + 12)
                link(tt(zq, z, z, ALU.mult))
                V.reduce_sum(var, zq, AX).then_inc(ln_v, 1)
                dve.wait_ge(ln_rms, 1)
                link(tt(z, z, var.unsqueeze(2).to_broadcast(wide), ALU.mult))
                split(u0 + 13)
                link(tt(zv, zv, ln_g.unsqueeze(1).to_broadcast([P, T, 512]), ALU.mult))
                tt(zv, zv, ln_b.unsqueeze(1).to_broadcast([P, T, 512]), ALU.add).then_inc(ln_ready, 1)
                split(u0 + 14)
                split(u0 + 15)
                for j in range(2):
                    k = ACC["sgu"] + j
                    written(dve, k)
                    for g in range(4):
                        gg = 4 * j + g
                        c = slice(gg * 64, (gg + 1) * 64)
                        ins = stt(y_nat[:, :, c], acc[:, k % NB, g * P:(g + 1) * P].rearrange("p (t c) -> p t c", c=64),
                                  bs_t[:, gg:gg + 1], zu[:, :, c], ALU.add, ALU.mult)
                    ins.then_inc(acc_free[k % NB], 1)
                tiles = []
                dm = const("dil")
                for b in range(2):
                    tiles.append((dsc[:, b, 0:512].rearrange("p (h w) -> p h w", w=P), dm[:, 0:P], None))
                    for j in range(2):
                        tiles.append((dsc[:, b, 512 * (j + 1):512 * (j + 2)].rearrange("p (h w) -> p h w", w=L),
                                      dm[:, P:384], None))
                softmax(tiles, 0.125, ACC["dsc"], 6, 12)
                for j in range(4):
                    split(u0 + 16 + j)
                emptied(dve, ACC["sgu"], 2)
                for b in range(2):
                    emptied(dve, ACC[f"dpv{b}"])
                norm_front(6, y_nat)
                norm_back(6, g_ab)
                add_out(u0 + 18, OUT["mix_out"])

            def cross():
                u0 = UNITS["cross"]
                x_whole(dve, X_FROM[7])
                norm_front(7, x_sb)
                norm_back(7, gains[:, 7, :])
                for j in range(4):
                    split(u0 + 2 + j)
                tiles = [(xs[:, t, 2 * j:2 * j + 2, :], None, None) for t in range(T) for j in range(2)]
                softmax(tiles, 1 / 16, ACC["xsc"], 12, 18)
                for h in range(4):
                    mix_low(6 + h, ACC["xpv"] + h, 2 * h)
                add_out(u0 + 4, OUT["cross_out"])

            if "even" in running:
                even()
            if "ffn0" in running:
                ffn("ffn0")
            if "odd" in running:
                odd()
            if "ffn1" in running:
                ffn("ffn1")
            if "ffn2" in running:
                ffn("ffn2")
            if "mix" in running:
                mix()
            if "cross" in running:
                cross()
            if "ffn3" in running:
                ffn("ffn3")
            if "final" in running:
                x_whole(dve, X_FROM[10])
                norm_front(10, x_sb)


_INS = ["x", "even_norm", "even_w_in", "q_norm", "k_norm", "sinks", "ssm_a_re", "ssm_a_im", "ssm_b_re", "ssm_b_im",
        "ssm_c_re", "ssm_c_im", "ssm_d", "ssm_log_dt", "ssm_w_glu", "ssm_b_glu", "even_w_out", "odd_norm",
        "odd_w_in", "odd_w_out", "ffn_norm", "ffn_w_gate", "ffn_w_up", "ffn_w_down", "mem_2", "positions_2",
        "ffn1_norm_2", "ffn1_w_gate_2", "ffn1_w_up_2", "ffn1_w_down_2", "mix_norm_2", "w_in_2", "sgu_ln_g_2",
        "sgu_ln_b_2", "sgu_w_s_2", "sgu_b_s_2", "out_norm_a_2", "out_norm_b_2", "w_out_2", "cross_norm_2",
        "mem_norm_2", "cross_wq_2", "cross_wk_2", "cross_wv_2", "cross_wo_2", "ffn2_norm_2", "ffn2_w_gate_2",
        "ffn2_w_up_2", "ffn2_w_down_2", "final_norm_2"]


def kernel(**inputs):
    import concourse.bacc as _bacc
    from concourse.bass_utils import run_bass_kernel_spmd as _run

    nc = _bacc.Bacc("TRN2", target_bir_lowering=False, num_devices=1, dynamic_dma_scratch_size=1024)
    arrays, args = {}, {}
    for name in _INS:
        v = np.ascontiguousarray(inputs[name])
        arrays[f"in_{name}_dram"] = v
        args[name] = nc.dram_tensor(f"in_{name}_dram", v.shape, mybir.dt.from_np(v.dtype), kind="ExternalInput").ap()
    v = shape_constants()
    arrays["in_consts_dram"] = v
    args["consts"] = nc.dram_tensor("in_consts_dram", v.shape, F32, kind="ExternalInput").ap()
    out = nc.dram_tensor("out_0_dram", (1, L, D), F32, kind="ExternalOutput").ap()
    build(nc, args, out)
    r = _run(nc, [arrays], core_ids=[0])
    return r.results[0]["out_0_dram"]
```

```python
from contextlib import ExitStack

import numpy as np
import concourse.bass as bass
from concourse import mybir

F32 = mybir.dt.float32
F32R = mybir.dt.float32r
I32 = mybir.dt.int32
ALU = mybir.AluOpType
ACT = mybir.ActivationFunctionType
AX = mybir.AxisListType.X

P = 128
L = 256
T = L // P
D = 1024
C = D // P
FF = 2816
UW = 256
NF = FF // UW
RAW = 3
NB = 4
EPS = 1e-6
LN_EPS = 1e-5
NEG = -1e30
MAGIC = 1.5 * 2.0 ** 23
TWO_PI = 6.283185
PI_A = 6.28125
PI_B = float(np.float32(np.round((2 * np.pi - PI_A) * 2 ** 20) / 2 ** 20))
PI_C = float(2 * np.pi - PI_A - PI_B)
G, N, PC, S = 32, 64, 16, 8
NC = L // S

CONSTS = dict(ident=128, jt=128, negtri=128, negones=128, tril=128, strict=128, swa=384, dil=384,
              step=36, phase=36, chunk=32, invf=8)
CONST_AT = {}
_at = 0
for _n, _w in CONSTS.items():
    CONST_AT[_n] = _at
    _at += _w
CONST_W = _at
EARLY_W = CONST_AT["negtri"]


def shape_constants():
    q = np.arange(P)[:, None]
    k = np.arange(P)[None, :]
    t = {}
    t["ident"] = (q == k) * 1.0
    j = np.zeros((P, P))
    j[np.arange(N) + N, np.arange(N)] = -1.0
    j[np.arange(N), np.arange(N) + N] = 1.0
    t["jt"] = j
    t["negtri"] = -1.0 * (q >= k)
    t["negones"] = -np.ones((P, P))
    t["tril"] = (q <= k) * 1.0
    t["strict"] = (q < k) * 1.0
    qq = np.concatenate([q, q + P, q + P], 1)

    def blocks(f):
        return np.concatenate([f(q - k), f(q + P - k), f(q - k)], 1)
    t["swa"] = blocks(lambda d: np.where((d >= 0) & (d < 128), 0.0, NEG))

    def count(d):
        n = (((d >= 0) & (d <= 128)) * 1.0 + ((d >= 0) & (d % 4 == 0)) + ((d >= 0) & (d % 16 == 0)))
        return np.where(n > 0, np.log(np.maximum(n, 1)), NEG)
    t["dil"] = blocks(count)
    im = np.arange(P)[:, None] >= N
    kb = np.arange(S - 1, -1, -1)
    kc = np.arange(S + 1)
    t["step"] = np.tile(np.concatenate([kb, kb, kc, kc, [1, 1]]), (P, 1))

    def ph(re, imv, n):
        return np.repeat(np.where(im, imv, re), n, 1)
    t["phase"] = np.concatenate([ph(.25, 0, S), ph(.5, .25, S), ph(.25, .5, S + 1), ph(.5, .75, S + 1),
                                 ph(.25, .25, 1), ph(0, 0, 1)], 1)
    t["chunk"] = np.tile(np.arange(NC), (P, 1))
    f = np.float32(500000.0) ** (np.float32(-2.0) * np.arange(8, dtype=np.float32) / np.float32(16))
    t["invf"] = np.tile(f, (P, 1))
    return np.concatenate([np.asarray(t[n], np.float64) for n in CONSTS], 1).astype(np.float32)


def plan(parts):
    at, out = 0, {}
    for name, n in parts:
        out[name] = at
        at += n
    out["end"] = at
    return out


STAGES = ["even", "ffn0", "odd", "ffn1", "ffn2", "mix", "cross", "ffn3", "final"]


def build(nc, a, out, stop=9):
    UNITS = plan([("even", 10), ("ffn0", 33), ("mem_k0", 1), ("odd", 12), ("mem_k1", 1), ("odd_out", 4),
                  ("mem_k2", 1), ("ffn1", 33), ("mem_k3", 1), ("ffn2", 33), ("mem_v0", 1), ("mix", 10),
                  ("mem_v1", 1), ("mem_v2", 1), ("mix_out", 4), ("mem_v3", 1), ("cross", 8), ("ffn3", 33)])
    BEGINS = dict(ffn0="ffn0", odd="mem_k0", ffn1="mem_k2", ffn2="mem_k3", mix="mem_v0", cross="mem_v3",
                  ffn3="ffn3")
    NU = UNITS["end"] if stop >= 8 else UNITS[BEGINS[STAGES[stop]]]
    ODD_ORDER = []
    for s_ in range(24):
        ODD_ORDER.append(("half", s_))
        if s_ > 6 and s_ % 6 in (1, 2, 4, 5):
            ODD_ORDER.append(("head", (s_ // 6 - 1) * 4 + (1, 2, 4, 5).index(s_ % 6)))
    ODD_ORDER += [("fill", 0), ("head", 12), ("fill", 1)] + [("head", i) for i in range(13, 19)]
    ODD_BANKS = [("unit", i // 2) if what == "half" else ("pv", (i - 3) // 2) if what == "head" else ("fill", 0)
                 for what, i in ODD_ORDER
                 if (what == "half" and i % 2 == 0) or (what == "head" and i >= 3 and i % 2 == 1) or
                 (what == "fill" and i == 0)]
    OUT = plan([("even", 5), ("glu", 2), ("even_out", 5), ("ffn0", 22), ("mem_k0", 1), ("odd", len(ODD_BANKS)),
                ("odd_out", 5), ("mem_k2", 1), ("ffn1", 22), ("mem_k3", 1), ("ffn2", 22), ("mem_v0", 1), ("mix", 10),
                ("mem_v1", 1), ("mem_v2", 1), ("mix_out", 5), ("mem_v3", 1), ("cross", 4), ("cross_out", 5),
                ("ffn3", 22)])
    ODD_BANK = {what: OUT["odd"] + i for i, what in enumerate(ODD_BANKS)}
    OUT["mem_k1"] = ODD_BANK["fill", 0]
    ACC = plan([("norm0", 4), ("prep_a", 1), ("prep_bc", 4), ("uc", 8), ("vt", 8), ("qk", 3), ("u", 2), ("sc0", 3),
                ("s", 2), ("js", 2), ("sc1", 3), ("k", 8), ("jg", 2), ("pt0", 3), ("pv0", 1), ("pt1", 3), ("pv1", 1),
                ("y", 2), ("yt", 4), ("norm8", 4),
                ("norm1", 4), ("ffn0", 4), ("norm2", 4), ("sb", 16), ("norm3", 4), ("ffn1", 4),
                ("norm4", 4), ("ffn2", 4), ("norm5", 4), ("ws", 3), ("dqk", 4), ("dsc", 6), ("sgu", 2),
                ("dpt0", 3), ("dpv0", 1), ("dpt1", 3), ("dpv1", 1), ("norm6", 4),
                ("norm7", 4), ("xsc", 4), ("xpt", 4), ("xpv", 4),
                ("norm9", 4), ("ffn3", 4)])
    NORMS = [0, 8, 1, 2, 3, 4, 5, 6, 7, 9, 10]
    GAINS = {0: "even_norm", 1: "ffn_norm", 2: "odd_norm", 3: "ffn_norm", 4: "ffn1_norm_2", 5: "mix_norm_2",
             7: "cross_norm_2", 8: "mem_norm_2", 9: "ffn2_norm_2"}
    SQ_V = plan([(n, 2 if n in (0, 8) else 0) for n in NORMS])
    SQ_A = plan([(n, 2 if n in (0, 8) else 4) for n in NORMS])
    RMS = plan([(n, 4 if n == 6 else 2) for n in NORMS])
    SUMS = plan([("even", 1), ("ffn0", 3), ("odd", 1), ("ffn1", 3), ("ffn2", 3), ("mix", 1), ("cross", 1), ("ffn3", 3)])
    NTH = {n: i for i, n in enumerate(NORMS)}

    with ExitStack() as ctx:
        ctx.enter_context(nc.allow_non_contiguous_dma(reason="vectors of a few hundred elements, once"))

        def sb(name, shape, dt=F32):
            return ctx.enter_context(nc.sbuf_tensor(name, shape, dt))

        def sem(name):
            return ctx.enter_context(nc.semaphore(name))

        raw = sb("raw", [P, RAW, 2048])
        w_hi = sb("w_hi", [P, 2, 2048], F32R)
        w_lo = sb("w_lo", [P, 2, 2048], F32R)
        h_hi = sb("h_hi", [P, C, L], F32R)
        h_lo = sb("h_lo", [P, C, L], F32R)
        f_hi = sb("f_hi", [P, 1024], F32R)
        f_lo = sb("f_lo", [P, 1024], F32R)
        x_sb = sb("x_sb", [P, T, D])
        xn = sb("xn", [P, T, D])
        AW = 32460
        M_AT = AW - 2 * C * L
        arena = sb("arena", [P, M_AT])
        with nc.sbuf_tensor("arena_end", [P, 2 * C * L], F32) as arena_end:
            pass
        m_pair = sb("m_pair", [P, 2, C, L], F32R)
        m_hi, m_lo = m_pair[:, 0, :, :], m_pair[:, 1, :, :]
        top = [0]

        def flat(v):
            return v.rearrange("p a b -> p (a b)")

        def area(n):
            if top[0] < M_AT < top[0] + n:
                top[0] = M_AT
            top[0] += n
            assert top[0] <= AW, top[0]
            return top[0] - n

        def view(at, *shape, parts=P):
            n = int(np.prod(shape))
            v = arena[0:parts, at:at + n] if at < M_AT else arena_end[0:parts, at - M_AT:at - M_AT + n]
            names = "abcd"[:len(shape)]
            if len(shape) == 1:
                return v
            return v.rearrange(f"p ({' '.join(names)}) -> p {' '.join(names)}", **dict(zip(names, shape)))

        early = view(area(EARLY_W), EARLY_W)
        ident = early[:, 0:P]
        gains = view(area(10 * C), 10, C)
        ss = view(area(64), 16, 4)
        rms = view(area(64), 16, 4)
        half = view(area(32), 32)
        st = view(area(200), 200)
        BASE = top[0]
        jt = early[:, CONST_AT["jt"]:CONST_AT["jt"] + P]
        o_swa = area(384)
        swa_mask = view(o_swa, 384)
        steps = view(area(36), 36)
        phase = view(area(36), 36)
        chunk = view(area(32), 32)
        qk_gain = view(area(2), 2)
        sinks = view(area(8), 8)
        b_glu = view(area(4), 4)
        dskip = view(area(512), G, PC)
        log_dt = view(area(32), G)
        a_t = view(area(64), 2, G)
        small = view(area(16 * G), 16, G)
        REG_T = area(4096)
        tmp_t = view(REG_T, 36, G)
        tmp_u = view(REG_T + 1152, 36, G)
        tmp_n = view(REG_T + 2304, 36, G)
        vt = view(REG_T, G, P)
        g_st = view(REG_T, G, NC)
        y_ch = view(REG_T + 1024, S, C, PC)
        y_f = view(REG_T + 2048, 4, L)
        rho = view(REG_T + 3072, G, NC)
        o_u = area(1024)
        br = view(o_u, PC, G)
        bi = view(o_u + 512, PC, G)
        u_ch = view(o_u, G, NC)
        o_qkv = area(1536)
        qkv = view(o_qkv, T, 768)
        u_t = view(o_qkv, 4, L)
        REG_A = area(4096)
        uc = view(REG_A, G, S * PC, parts=NC)
        lags = view(REG_A, G, P, parts=PC)
        b_nat = view(REG_A, 2, 2, 1024, parts=G)
        o_sc = area(3072)
        sc = [view(o_sc, 1536), view(o_sc + 1536, 1536)]
        REG_V = area(4096)
        v_in = view(REG_V, G, S, PC)
        m_in = view(REG_V, G, P)
        o_w = area((S + 1) * 512)
        w_out_c = view(o_w, S + 1, G, PC)
        c_nat = view(o_w, 2, PC, 2, N, parts=G)
        o_alpha = area(2048)
        alpha = view(o_alpha, 2, G, NC)
        hpad = view(o_alpha, G, NC + 1)
        k_t = view(area(L), L)
        cr = view(area(512), PC, G)
        ci = view(area(512), PC, G)
        o_tab = area(36 * G)
        tab = view(o_tab, 36, G)
        o_qt = area(1024)
        cbr = view(o_qt, PC, G)
        cbi = view(o_qt + 512, PC, G)
        q_t = [view(o_qt + 512 * i, 2, L) for i in range(2)]
        pool_tmp = view(area(512), G, PC)
        a_raw = view(area(4 * N), 2, 2, N, parts=G)
        area(128)
        pt = view(o_tab, 2, 1536)
        bst = view(area(512), PC, G)
        sig = u_t
        s_ch = xn[:, 0, :]
        t_ch = xn[:, 1, :]
        MEM = M_AT - 4096
        assert MEM - 2048 >= REG_A
        km_t = view(MEM, C, L)
        vm = view(MEM + 2048, T, D)
        mem_sb = view(MEM - 2048, T, D)
        top[0] = BASE
        late = view(area(CONST_W - EARLY_W), CONST_W - EARLY_W)
        silu = view(area(1024), 2, 512)
        hf = view(area(1024), 2, 512)
        BASE2 = top[0]

        def const(name):
            o = CONST_AT[name] - EARLY_W
            return late[:, o:o + CONSTS[name]]
        sq_t = view(area(2048), C, L)
        sk_t = view(area(2048), C, L)
        sv = view(area(2048), T, D)
        sb_e = view(area(4 * 384), 4, 384)
        sb_sp = view(area(4 * 384), 4, 384)
        sb_w = view(area(4 * 384), 4, 384)
        sb_o = view(area(2048), C, L)
        assert top[0] <= MEM
        top[0] = BASE2
        zu = view(area(1024), T, 512)
        zv = view(area(1024), T, 512)
        zs = view(area(1024), T, 512)
        dqk = view(area(2048), T, 16, 64)
        dv = view(area(1024), T, 512)
        dq_t = view(area(1024), 4, L)
        dk_t = view(area(1024), 4, L)
        dsc = view(area(3072), 2, 1536)
        o_dpt = area(3072)
        dpt = view(o_dpt, 2, 1536)
        y_nat = view(area(2048), T, D)
        ws_nat = view(area(1024), 8, P)
        ws_t = view(area(1024), 8, P)
        bs_nat = view(area(128), P, parts=8)
        bs_t = view(area(8), 8)
        ln_g = view(area(512), 512)
        ln_b = view(area(512), 512)
        g_ab = view(area(8), C)
        rot = view(area(8 * 16), 8, T, 8)
        pos_f = view(area(2), 2)
        dst_ = view(area(128), 128)
        ropet = view(o_dpt, 4, T, 16, 8)
        assert top[0] <= MEM
        pos_i = sb("pos_i", [P, T], I32)
        xq_t = view(BASE2, C, L)
        xs = view(BASE2 + 2048, T, 4, L)
        xpt = view(BASE2 + 4096, T, 4, L)
        fin_g = view(BASE2 + 6144, D)
        MEM_UNITS = {f"mem_{w}{j}": (w, j) for w in "kv" for j in range(4)}

        acc = ctx.enter_context(nc.psum_tensor("acc", [P, NB, 512], F32))
        outp = ctx.enter_context(nc.psum_tensor("outp", [P, NB, 512], F32))

        raw_landed = [sem(f"raw_landed{i}") for i in range(RAW)]
        w_hi_ready, w_lo_ready, w_used = sem("w_hi_ready"), sem("w_lo_ready"), sem("w_used")
        acc_ready = sem("acc_ready")
        acc_free = [sem(f"acc_free{i}") for i in range(NB)]
        out_free = [sem(f"out_free{i}") for i in range(NB)]
        x_loaded, consts_in, late_in, late2_in, mem_in, fin_in = (sem("x_loaded"), sem("consts_in"), sem("late_in"),
                                                                  sem("late2_in"), sem("mem_in"), sem("fin_in"))
        ssm_in, small_in, gain0_in = sem("ssm_in"), sem("small_in"), sem("gain0_in")
        sum_ready, result_ready = sem("sum_ready"), sem("result_ready")
        act_step, dve_step, pool_step = sem("act_step"), sem("dve_step"), sem("pool_step")
        half_ready = sem("half_ready")
        sq_v, sq_a, rms_ready, xn_v, xn_a, h_hi_ready = (sem("sq_v"), sem("sq_a"), sem("rms_ready"), sem("xn_v"),
                                                         sem("xn_a"), sem("h_hi_ready"))
        f_hi_done, f_lo_done = sem("f_hi_done"), sem("f_lo_done")
        dt_ready, lam_mag, lam_exp, lam_frac, lam_sin = (sem("dt_ready"), sem("lam_mag"), sem("lam_exp"),
                                                         sem("lam_frac"), sem("lam_sin"))
        al_frac, al_sin, tab_ready, bb_ready, v_ready, wc_ready = (
            sem("al_frac"), sem("al_sin"), sem("tab_ready"), sem("bb_ready"), sem("v_ready"), sem("wc_ready"))
        decay_ready, rho_ready, g_ready, h_ready, kz_ready, k_ready, m_in_done = (
            sem("decay_ready"), sem("rho_ready"), sem("g_ready"), sem("h_ready"), sem("kz_ready"), sem("k_ready"),
            sem("m_in_done"))
        qk_sq, qk_rms, qk_ready = sem("qk_sq"), sem("qk_rms"), sem("qk_ready")
        yhi_ready, ylo_ready, glu_done, glu_hi, glu_lo = (
            sem("yhi_ready"), sem("ylo_ready"), sem("glu_done"), sem("glu_hi"), sem("glu_lo"))
        sub_done, exp_done, p_ready, mix_hi = sem("sub_done"), sem("exp_done"), sem("p_ready"), sem("mix_hi")
        sb_ln, sb_sp_done, sb_cum, sb_w_done, pv_ready, o_lo_done = (sem("sb_ln"), sem("sb_sp_done"), sem("sb_cum"),
                                                          sem("sb_w_done"), sem("pv_ready"), sem("o_lo_done"))
        rope_frac, rope_sin, rot_done, ln_v, ln_rms, ln_ready = (
            sem("rope_frac"), sem("rope_sin"), sem("rot_done"), sem("ln_v"), sem("ln_rms"), sem("ln_ready"))
        stored = sem("stored")

        block = ctx.enter_context(nc.Block())

        class Own:

            def __init__(self, eng, s):
                self.eng, self.s, self.n = eng, s, 0

            def link(self, ins):
                self.n += 1
                ins.then_inc(self.s, 1)
                self.eng.wait_ge(self.s, self.n)

        def acc_taken(pe, k):
            if k >= NB:
                pe.wait_ge(acc_free[k % NB], k // NB)

        def out_taken(pe, k, it=0):
            if k >= NB:
                pe.wait_ge(out_free[k % NB], k // NB + it)

        def written(eng, k):
            eng.wait_ge(acc_ready, k + 1 - NB * sum(ACC[f] < k for f in FFN))

        def emptied(eng, k, n=1):
            for j in range(k + max(0, n - NB), k + n):
                eng.wait_ge(acc_free[j % NB], j // NB + 1)

        def out_emptied(eng, k, n=1, it=0):
            for j in range(k + max(0, n - NB), k + n):
                eng.wait_ge(out_free[j % NB], j // NB + 1 + it)

        def x_whole(eng, what):
            ring, k = what
            if ring == "acc":
                emptied(eng, k, 4)
            else:
                out_emptied(eng, k, 5)

        def x_piece(n, t, h):
            if X_FROM.get(n, ("acc",))[0] == "out":
                return slice(0, 3 * UW) if h == 0 else slice(3 * UW, D)
            return slice(h * 512, (h + 1) * 512)

        def x_order(n):
            if X_FROM.get(n, ("acc",))[0] == "out":
                return [(0, 0), (1, 0), (0, 1), (1, 1)]
            return [(0, 0), (0, 1), (1, 0), (1, 1)]

        def x_piece_ready(eng, n, t, h):
            if n not in X_FROM:
                return
            ring, k = X_FROM[n]
            if ring == "acc":
                emptied(eng, k + 2 * t + h)
            else:
                out_emptied(eng, k + 2 if h == 0 else k + 3 + t)

        X_FROM = {1: ("out", OUT["even_out"]), 2: ("acc", ACC["ffn0"]), 3: ("out", OUT["odd_out"]),
                  4: ("acc", ACC["ffn1"]), 5: ("acc", ACC["ffn2"]), 7: ("out", OUT["mix_out"]),
                  9: ("out", OUT["cross_out"]), 10: ("acc", ACC["ffn3"])}
        FFNS = [("ffn0", 0, a["ffn_w_gate"][0], a["ffn_w_up"][0], a["ffn_w_down"][0], 1.0, 1),
                ("ffn1", 1, a["ffn_w_gate"][1], a["ffn_w_up"][1], a["ffn_w_down"][1], 1.0, 3),
                ("ffn2", 2, a["ffn1_w_gate_2"][0], a["ffn1_w_up_2"][0], a["ffn1_w_down_2"][0], 0.5, 4),
                ("ffn3", 3, a["ffn2_w_gate_2"][0], a["ffn2_w_up_2"][0], a["ffn2_w_down_2"][0], 0.5, 9)]
        FFN = {f[0]: f for f in FFNS}
        running = STAGES[:stop]

        def const_in(name):
            return a["consts"][:, CONST_AT[name]:CONST_AT[name] + CONSTS[name]]

        def uc_part(j, q):
            return uc[:, 16 * j:16 * j + 16, 2 * q * PC:(2 * q + 2) * PC].rearrange("p g (s c) -> p s g c", c=PC)

        def uc_bank(k):
            return acc[0:NC, k % NB, :].rearrange("p (s g c) -> p s g c", s=2, c=PC)

        def row(v):
            return v.rearrange("(a n) -> a n", a=1)
        small_loads = [(a_raw[:, j, h, :], a[n][0]) for j, n in enumerate(["ssm_a_re", "ssm_a_im"]) for h in range(2)]
        small_loads += [(log_dt, row(a["ssm_log_dt"][0]).to_broadcast([P, G]))]
        small_loads += [(b_nat[:, j, h, :], a[n][0].rearrange("g n p -> g (n p)"))
                        for j, n in enumerate(["ssm_b_re", "ssm_b_im"]) for h in range(2)]
        small_loads += [(c_nat[:, j, :, h, :], a[n][0]) for j, n in enumerate(["ssm_c_re", "ssm_c_im"])
                        for h in range(2)]
        small_loads += [(steps, const_in("step")), (phase, const_in("phase")), (chunk, const_in("chunk"))]
        ssm_loads, small_loads = small_loads, [(swa_mask, const_in("swa"))]
        SSM = len(ssm_loads)
        small_loads += [(qk_gain[64 * j:64 * j + 64, i:i + 1], a[n][0].rearrange("(d a) -> d a", a=1))
                        for i, n in enumerate(["q_norm", "k_norm"]) for j in range(2)]
        small_loads += [(sinks, row(a["sinks"][0]).to_broadcast([P, 8])),
                        (b_glu, a["ssm_b_glu"][0].rearrange("(c p) -> p c", p=P)),
                        (dskip[0:PC, :, :].rearrange("p g c -> p (g c)"), row(a["ssm_d"][0]).to_broadcast([PC, 512]))]
        small_loads += [(gains[:, n, :], a[g][1 if n == 3 else 0].rearrange("(p c) -> p c", c=C))
                        for n, g in GAINS.items() if n > 0]
        SMALL = len(small_loads)
        late_loads = [(ws_nat, a["sgu_w_s_2"][0].rearrange("g i j -> i g j")), (bs_nat, a["sgu_b_s_2"][0]),
                      (ln_g, row(a["sgu_ln_g_2"][0]).to_broadcast([P, 512])),
                      (ln_b, row(a["sgu_ln_b_2"][0]).to_broadcast([P, 512])),
                      (pos_i[:, :], a["positions_2"][0].rearrange("(t p) -> p t", p=P))]
        late_loads += [(g_ab[64 * j:64 * j + 64, :], a[n][0].rearrange("(p c) -> p c", c=C))
                       for j, n in enumerate(["out_norm_a_2", "out_norm_b_2"])]
        LATE2 = len(late_loads)

        def tiles_of(s):
            return [t for b in range(2) for t in
                    [s[b][:, 0:512].rearrange("p (h w) -> p h w", w=P)] +
                    [s[b][:, 512 * (j + 1):512 * (j + 2)].rearrange("p (h w) -> p h w", w=L) for j in range(2)]]
        sc_tiles = tiles_of(sc)
        dsc_tiles = tiles_of([dsc[:, b, :] for b in range(2)])
        xs_tiles = [xs[:, t, 2 * j:2 * j + 2, :] for t in range(T) for j in range(2)]

        def stat_at(n, before):
            return 2 * n if before == 12 else 8 * (n // 3) + (0, 4, 6)[n % 3]

        @block.sync
        def _(sp):
            sp.dma_start(x_sb[:, :, :], a["x"][0].rearrange("(t p) f -> p t f", p=P)).then_inc(x_loaded, 16)
            sp.dma_start(early, a["consts"][:, 0:EARLY_W]).then_inc(consts_in, 16)
            sp.dma_start(gains[:, 0, :], a["even_norm"][0].rearrange("(p c) -> p c", c=C)).then_inc(gain0_in, 16)

            def load(u, src, cols=UW, it=0):
                if u >= RAW:
                    sp.wait_ge(w_lo_ready, u - RAW + 1 + 6 * it)
                dst = raw[:, u % RAW, :].rearrange("p (c n) -> p c n", n=cols)
                sp.dma_start(dst, src).then_inc(raw_landed[u % RAW], 16)

            def by_p(w):
                return w.rearrange("(p c) n -> p c n", p=P)

            def by_c(w):
                return w.rearrange("(c p) n -> p c n", p=P)

            def cols(w, n):
                return w[:, :, n * UW:(n + 1) * UW]

            def ffn(name, mem=None):
                _, _, wg, wu, wd, _, _ = FFN[name]
                wg, wu, wd = by_p(wg), by_p(wu), by_c(wd)
                u0 = UNITS[name]
                load(u0, cols(wg, 0))
                load(u0 + 1, cols(wu, 0))
                load(u0 + 2, cols(wg, 1))
                if name == "ffn0":
                    x_whole(sp, X_FROM[1])
                    sp.dma_start(late, a["consts"][:, EARLY_W:CONST_W]).then_inc(late_in, 16)
                if name == "ffn1":
                    x_whole(sp, X_FROM[3])
                    for dst, src in late_loads:
                        sp.dma_start(dst, src).then_inc(late2_in, 16)
                if name == "ffn3":
                    x_whole(sp, X_FROM[9])
                    sp.dma_start(fin_g, row(a["final_norm_2"]).to_broadcast([P, D])).then_inc(fin_in, 16)

                def turn(i, it=0):
                    if i > 0:
                        load(u0 + 2 + 3 * i, wg[:, :, bass.ds((i + 1 + 2 * it) * UW, UW)], it=it)
                    load(u0 + 3 + 3 * i, wu[:, :, bass.ds((i + 1 + 2 * it) * UW, UW)], it=it)
                    load(u0 + 4 + 3 * i, wd[:, bass.ds((i + 2 * it) * 2, 2), :], D, it=it)
                turn(0)
                with sp.Fori(0, 4) as it:
                    turn(1, it)
                    turn(2, it)
                turn(9)
                load(u0 + 32, wd[:, 20:22, :], D)

            if "even" in running:
                u0 = UNITS["even"]
                w = by_p(a["even_w_in"][0])
                for j, n in enumerate([3, 4, 0, 1, 2]):
                    load(u0 + j, cols(w, n))
                    if j == 0:
                        for dst, src in ssm_loads:
                            sp.dma_start(dst, src).then_inc(ssm_in, 16)
                    if j == 1:
                        for dst, src in small_loads:
                            sp.dma_start(dst, src).then_inc(small_in, 16)
                load(u0 + 5, by_c(a["ssm_w_glu"][0]), 512)
                for j in range(4):
                    load(u0 + 6 + j, cols(by_c(a["even_w_out"][0]), j))
                    if j == 1:
                        sp.wait_ge(kz_ready, 1)
                        sp.wait_ge(k_ready, 1)
                        for s in range(S):
                            sp.dma_start(m_in[s * PC:(s + 1) * PC, :, s * PC:],
                                         lags[:, :, 0:P - s * PC]).then_inc(m_in_done, 16)
                written(sp, ACC["y"] + 1)
                sp.dma_start(mem_sb, a["mem_2"][0].rearrange("(t p) f -> p t f", p=P)).then_inc(mem_in, 16)

            def load_mem(name):
                w, j = MEM_UNITS[name]
                load(UNITS[name], cols(by_p(a[f"cross_w{w}_2"][0]), j))
            if "ffn0" in running:
                ffn("ffn0")
            if "odd" in running:
                load_mem("mem_k0")
                for j in range(12):
                    load(UNITS["odd"] + j, cols(by_p(a["odd_w_in"][0]), 4 * (j % 3) + j // 3))
                load_mem("mem_k1")
                for j in range(4):
                    load(UNITS["odd_out"] + j, cols(by_c(a["odd_w_out"][0]), j))
            if "ffn1" in running:
                load_mem("mem_k2")
                ffn("ffn1")
            if "ffn2" in running:
                load_mem("mem_k3")
                ffn("ffn2")
            if "mix" in running:
                u0 = UNITS["mix"]
                load_mem("mem_v0")
                for j, n in enumerate([4, 5, 6, 7, 2, 3, 0, 1, 8, 9]):
                    load(u0 + j, cols(by_p(a["w_in_2"][0]), n))
                load_mem("mem_v1")
                load_mem("mem_v2")
                for j in range(4):
                    load(UNITS["mix_out"] + j, cols(by_p(a["w_out_2"][0]), j))
            if "cross" in running:
                u0 = UNITS["cross"]
                load_mem("mem_v3")
                for j in range(4):
                    load(u0 + j, cols(by_p(a["cross_wq_2"][0]), j))
                for j in range(4):
                    load(u0 + 4 + j, cols(by_c(a["cross_wo_2"][0]), j))
            if "ffn3" in running:
                ffn("ffn3")
            if stop in (4, 5):
                sp.wait_ge(late2_in, 16 * LATE2)
            if stop < 9:
                x_whole(sp, X_FROM[{1: 1, 2: 2, 3: 3, 4: 4, 5: 5, 6: 7, 7: 9, 8: 10}[stop]])
            for t in range(T):
                if stop == 9:
                    sp.wait_ge(result_ready, t + 1)
                sp.dma_start(out[0, t * P:(t + 1) * P, :],
                             (xn if stop == 9 else x_sb)[:, t, :]).then_inc(stored, 16)
            sp.wait_ge(stored, 16 * T)

        @block.tensor
        def _(pe):
            def mm3(dst, w_pair, a_pair, start, stop_, act_first=False):
                passes = ((0, 0), (0, 1), (1, 0))
                for n, (i, j) in enumerate(passes):
                    lhs, rhs = (a_pair[j], w_pair[i]) if act_first else (w_pair[i], a_pair[j])
                    ins = nc.tensor.matmul(dst, lhs, rhs, start=start and n == 0, stop=stop_ and n == 2)
                return ins

            def w_unit(u, n, it=0):
                pe.wait_ge(w_lo_ready, u + 1 + 6 * it)
                return [w[:, u % 2, :].rearrange("p (c n) -> p c n", n=n) for w in (w_hi, w_lo)]

            def proj_t(u, k, it=0, fresh=None, x=(h_hi, h_lo), halves=(0, 1)):
                w = w_unit(u, UW, it)
                if 0 in halves:
                    out_taken(pe, k, it)
                for m in halves:
                    for c in range(C):
                        if fresh and m == 0 and c % 2 == 0:
                            fresh(c // 2)
                        ins = mm3(outp[:, k % NB, m * L:(m + 1) * L], [v[:, c, m * P:(m + 1) * P] for v in w],
                                  [v[:, c, :] for v in x], c == 0, c == C - 1)
                if 1 in halves:
                    ins.then_inc(w_used, 1)

            def proj_n(u, k, fresh=None, x=(h_hi, h_lo), halves=(0, 1), last=False):
                w = w_unit(u, UW)
                for t in halves:
                    kt = k + t if last else k
                    if t == 0 or last:
                        out_taken(pe, kt)
                    o = 0 if last else t * UW
                    for c in range(C):
                        if fresh and t == 0 and c % 2 == 0:
                            fresh(c // 2)
                        ins = mm3(outp[:, kt % NB, o:o + UW], [v[:, c, :] for v in w],
                                  [v[:, c, t * P:(t + 1) * P] for v in x], c == 0, c == C - 1, True)
                    if t == 0 and last:
                        ins.then_inc(sum_ready, 1)
                if 1 in halves:
                    ins.then_inc(w_used, 1)

            def proj_out(u, k, fresh=None, x=(h_hi, h_lo)):
                for j in range(4):
                    proj_n(u + j, k + j, fresh if j == 0 else None, x, last=j == 3)

            def mem_half(name, half):
                (proj_t if MEM_UNITS[name][0] == "k" else proj_n)(UNITS[name], OUT[name], x=(m_hi, m_lo),
                                                                  halves=(half,))

            def flip(dst, src, rows=P, base=0):
                return nc.tensor.transpose(dst, src, ident[base:base + rows, base:base + rows])

            def norm(n):
                k = ACC[f"norm{n}"]
                for t in range(T):
                    pe.wait_ge(xn_v, 2 * NTH[n] + 1 + t)
                    if t == 1:
                        pe.wait_ge(xn_a, NTH[n] + 1)
                    for q in range(4):
                        if t == 0:
                            acc_taken(pe, k + q)
                        for c in range(2):
                            ins = flip(acc[:, (k + q) % NB, c * L + t * P:c * L + (t + 1) * P],
                                       xn[:, t, 2 * q + c::C])
                        if t == 1:
                            ins.then_inc(acc_ready, 1)

            def h_whole(n):
                emptied(pe, ACC[f"norm{n}"], 4)

            def chunks(n):
                return lambda q: emptied(pe, ACC[f"norm{n}"] + q)

            def ffn(name, mem=None):
                _, f, _, _, _, _, n = FFN[name]
                u0, k0, d0 = UNITS[name], OUT[name], ACC[name]
                if mem:
                    mem_half(mem, 0)
                norm(n)
                if mem:
                    mem_half(mem, 1)
                proj_t(u0, k0, fresh=chunks(n))
                proj_t(u0 + 1, k0 + 1)

                def down(u, i, it, start, stop_):
                    w = w_unit(u, D, it)
                    pe.wait_ge(f_lo_done, NF * f + i + 1 + 2 * it)
                    b = (NF * f + i) % 2
                    for t in range(T):
                        for h in range(2):
                            for m in range(2):
                                o = b * 512 + m * L + t * P
                                ins = mm3(acc[:, (d0 + 2 * t + h) % NB, :], [x[:, m, h * 512:(h + 1) * 512] for x in w],
                                          [x[:, o:o + P] for x in (f_hi, f_lo)], start and m == 0,
                                          stop_ and m == 1, True)
                            if stop_ and t + h < 2:
                                ins.then_inc(sum_ready, 1)
                    ins.then_inc(w_used, 1)

                def turn(i, it=0):
                    proj_t(u0 + 2 + 3 * i, k0 + 2 * (i + 1), it)
                    proj_t(u0 + 3 + 3 * i, k0 + 2 * (i + 1) + 1, it)
                    down(u0 + 4 + 3 * i, i, it, i == 0, False)
                for j in range(4):
                    acc_taken(pe, d0 + j)
                turn(0)
                with pe.Fori(0, 4) as it:
                    turn(1, it)
                    turn(2, it)
                turn(9)
                down(u0 + 32, 10, 0, False, True)

            def scores(k, b, lhs, rhs):
                acc_taken(pe, k)
                for h in range(4):
                    ins = nc.tensor.matmul(acc[:, k % NB, h * P:(h + 1) * P], lhs(b, h)[:, 0:P], rhs(b, h)[:, 0:P],
                                           start=True, stop=True)
                ins.then_inc(acc_ready, 1)
                for j in range(2):
                    acc_taken(pe, k + 1 + j)
                    for h in range(2 * j, 2 * j + 2):
                        ins = nc.tensor.matmul(acc[:, (k + 1 + j) % NB, (h % 2) * L:(h % 2 + 1) * L],
                                               lhs(b, h)[:, P:L], rhs(b, h), start=True, stop=True)
                    ins.then_inc(acc_ready, 1)

            def probs_t(k, b, s, done, first):
                for j in range(2):
                    acc_taken(pe, k + j)
                    pe.wait_ge(done, first + (3 * b + 2 + j))
                    for h in range(2 * j, 2 * j + 2):
                        o = (h % 2) * L
                        flip(acc[:, (k + j) % NB, o:o + P], s[b][:, h * P:(h + 1) * P])
                        ins = flip(acc[:, (k + j) % NB, o + P:o + L], s[b][:, 512 + h * L:512 + h * L + P])
                    ins.then_inc(acc_ready, 1)
                acc_taken(pe, k + 2)
                for h in range(4):
                    ins = flip(acc[:, (k + 2) % NB, h * P:(h + 1) * P], s[b][:, 512 + h * L + P:512 + (h + 1) * L])
                ins.then_inc(acc_ready, 1)

            def even():
                u0, k0 = UNITS["even"], OUT["even"]
                pe.wait_ge(consts_in, 16)
                norm(0)
                proj_t(u0, k0, fresh=chunks(0), halves=(0,))
                k = ACC["prep_a"]
                acc_taken(pe, k)
                pe.wait_ge(ssm_in, 16 * SSM)
                for j in range(2):
                    ins = flip(acc[:, k % NB, j * G:(j + 1) * G], flat(a_raw[:, j, :, :]), G)
                ins.then_inc(acc_ready, 1)
                for j in range(4):
                    k = ACC["prep_bc"] + j
                    acc_taken(pe, k)
                    for p in range(PC):
                        src = flat(b_nat[:, j, :, :])[:, p::PC] if j < 2 else flat(c_nat[:, j - 2, p, :, :])
                        ins = flip(acc[:, k % NB, p * G:(p + 1) * G], src, G)
                    ins.then_inc(acc_ready, 1)
                proj_t(u0, k0, halves=(1,))
                proj_t(u0 + 1, k0 + 1)
                for j in range(2):
                    out_emptied(pe, k0 + j)
                    for q in range(4):
                        k = ACC["uc"] + 4 * j + q
                        acc_taken(pe, k)
                        for s in range(2):
                            for m in range(2):
                                o = s * 256 + m * P
                                ins = flip(acc[0:NC, k % NB, o:o + P], u_t[:, 2 * j + m, 2 * q + s::S])
                        ins.then_inc(acc_ready, 1)
                for j in range(3):
                    proj_n(u0 + 2 + j, k0 + 2 + j)
                pe.wait_ge(v_ready, 1)
                for j in range(8):
                    k = ACC["vt"] + j
                    acc_taken(pe, k)
                    for g in range(4):
                        ins = flip(acc[:, k % NB, g * P:(g + 1) * P],
                                   v_in[:, 4 * j + g, :, :].rearrange("p s c -> p (s c)"))
                    ins.then_inc(acc_ready, 1)
                k = ACC["qk"]
                pe.wait_ge(qk_ready, 1)
                for j in range(2):
                    acc_taken(pe, k + j)
                    for h in range(2):
                        for t in range(T):
                            ins = flip(acc[:, (k + j) % NB, h * L + t * P:h * L + (t + 1) * P],
                                       qkv[:, t, (2 * j + h) * P:(2 * j + h + 1) * P])
                    ins.then_inc(acc_ready, 1)
                acc_taken(pe, k + 2)
                for t in range(T):
                    ins = flip(acc[:, (k + 2) % NB, t * P:(t + 1) * P], qkv[:, t, 512:640])
                ins.then_inc(acc_ready, 1)
                emptied(pe, ACC["uc"], 8)
                for j in range(2):
                    k = ACC["u"] + j
                    acc_taken(pe, k)
                    for g in range(16):
                        ins = flip(acc[:, k % NB, g * NC:(g + 1) * NC], uc[:, 16 * j + g, :], NC)
                    ins.then_inc(acc_ready, 1)
                def q_of(b, h):
                    return q_t[h // 2][64 * b:64 * b + 64, h % 2, :]

                def k_of(b, h):
                    return k_t[64 * b:64 * b + 64, :]
                emptied(pe, ACC["qk"], 3)
                scores(ACC["sc0"], 0, q_of, k_of)
                emptied(pe, ACC["u"], 2)
                emptied(pe, ACC["vt"], 8)
                for j in range(2):
                    k = ACC["s"] + j
                    acc_taken(pe, k)
                    for g in range(16):
                        gg = 16 * j + g
                        ins = nc.tensor.matmul(acc[:, k % NB, g * NC:(g + 1) * NC], vt[:, gg, :], u_ch[:, gg, :],
                                               start=True, stop=True)
                    ins.then_inc(acc_ready, 1)
                for j in range(2):
                    k = ACC["js"] + j
                    acc_taken(pe, k)
                    emptied(pe, ACC["s"] + j)
                    nc.tensor.matmul(acc[:, k % NB, :], jt, s_ch[:, j * 512:(j + 1) * 512],
                                     start=True, stop=True).then_inc(acc_ready, 1)
                scores(ACC["sc1"], 1, q_of, k_of)
                pe.wait_ge(wc_ready, 1)
                pe.wait_ge(bb_ready, 1)
                for j in range(8):
                    k = ACC["k"] + j
                    acc_taken(pe, k)
                    for g in range(4):
                        gg = 4 * j + g
                        ins = nc.tensor.matmul(acc[0:PC, k % NB, g * P:(g + 1) * P], bst[:, :, gg],
                                               w_out_c[:, 0:S, gg, :], start=True, stop=True)
                    ins.then_inc(acc_ready, 1)
                for j in range(2):
                    k = ACC["jg"] + j
                    acc_taken(pe, k)
                    pe.wait_ge(g_ready, 1)
                    nc.tensor.matmul(acc[:, k % NB, :], jt,
                                     g_st[:, 16 * j:16 * (j + 1), :].rearrange("p g c -> p (g c)"),
                                     start=True, stop=True).then_inc(acc_ready, 1)
                def values_t(k, b):
                    emptied(pe, ACC[f"pt{b}"], 3)
                    acc_taken(pe, k)
                    for h in range(4):
                        po = (h % 2) * 64
                        dst = acc[po:po + 64, k % NB, (h // 2) * L:(h // 2 + 1) * L]
                        vs = [qkv[:, t, 640 + 64 * b:704 + 64 * b] for t in range(T)]
                        nc.tensor.matmul(dst, vs[0], pt[:, b, h * L:(h + 1) * L], start=True, stop=False)
                        ins = nc.tensor.matmul(dst[:, P:L], vs[1], pt[:, b, 1024 + h * P:1024 + (h + 1) * P],
                                               start=False, stop=True)
                    ins.then_inc(acc_ready, 1)
                for b in range(2):
                    probs_t(ACC[f"pt{b}"], b, sc, p_ready, 0)
                    values_t(ACC[f"pv{b}"], b)
                pe.wait_ge(m_in_done, 16 * S)
                pe.wait_ge(h_ready, 1)
                for j in range(2):
                    k = ACC["y"] + j
                    acc_taken(pe, k)
                    for cc in range(4):
                        for g4 in range(4):
                            gg = cc * 8 + j * 4 + g4
                            dst = acc[NC * cc:NC * (cc + 1), k % NB, g4 * P:(g4 + 1) * P]
                            nc.tensor.matmul(dst, u_ch[:, gg, :], m_in[:, gg, :], start=True, stop=False)
                            ins = nc.tensor.matmul(dst, hpad[:, gg, 0:NC], w_out_c[:, 1:S + 1, gg, :],
                                                   start=False, stop=True)
                    ins.then_inc(acc_ready, 1)
                emptied(pe, ACC["y"], 2)
                for cc in range(4):
                    k = ACC["yt"] + cc
                    acc_taken(pe, k)
                    for s in range(S):
                        ins = flip(acc[:, k % NB, s * NC:(s + 1) * NC], flat(y_ch[NC * cc:NC * (cc + 1), s, :, :]),
                                   NC, NC * cc)
                    ins.then_inc(acc_ready, 1)
                w = w_unit(u0 + 5, 512)
                pe.wait_ge(ylo_ready, 4)
                yv = [x[:, :].rearrange("p (c l) -> p c l", l=L) for x in (f_hi, f_lo)]
                for j in range(2):
                    out_taken(pe, OUT["glu"] + j)
                    for m in range(2):
                        for c in range(4):
                            ins = mm3(outp[:, (OUT["glu"] + j) % NB, m * L:(m + 1) * L],
                                      [x[:, c, (2 * j + m) * P:(2 * j + m + 1) * P] for x in w],
                                      [x[:, c, :] for x in yv], c == 0, c == 3)
                ins.then_inc(w_used, 1)
                norm(8)
                proj_out(u0 + 6, OUT["even_out"], lambda q: (
                    emptied(pe, ACC[f"pv{q}"]) if q < 2 else pe.wait_ge(glu_lo, 2 * (q - 1))))

            def odd():
                u0, k0 = UNITS["odd"], OUT["odd"]
                mem_half("mem_k0", 0)
                norm(2)
                mem_half("mem_k0", 1)
                pe.wait_ge(late_in, 16)

                def z_of(h):
                    k = ACC["sb"] + h
                    acc_taken(pe, k)
                    po = (h % 2) * 64
                    if h % 4 == 0:
                        for j in range(3):
                            out_emptied(pe, ODD_BANK["unit", 3 * (h // 4) + j])
                    kk, qq = sk_t[po:po + 64, h // 2, :], sq_t[po:po + 64, h // 2, :]
                    nc.tensor.matmul(acc[:, k % NB, 0:L], kk[:, 0:P], qq, start=True, stop=False,
                                     skip_group_check=True)
                    nc.tensor.matmul(acc[:, k % NB, L:384], kk[:, P:L], qq[:, P:L], start=False, stop=False,
                                     skip_group_check=True).then_inc(acc_ready, 1)

                def survive(h):
                    k = ACC["sb"] + h
                    pe.wait_ge(sb_sp_done, h + 1)
                    sp_ = sb_sp[:, h % 4, :]
                    nc.tensor.matmul(acc[:, k % NB, 0:L], const("negtri"), sp_[:, 0:L], start=False, stop=False,
                                     skip_group_check=True)
                    nc.tensor.matmul(acc[:, k % NB, P:L], const("negones"), sp_[:, L:384], start=False, stop=False,
                                     skip_group_check=True)
                    nc.tensor.matmul(acc[:, k % NB, L:384], const("negtri"), sp_[:, L:384], start=False, stop=True,
                                     skip_group_check=True).then_inc(sb_cum, 1)

                def values(h):
                    k = ODD_BANK["pv", h // 2]
                    if h % 2 == 0:
                        out_taken(pe, k)
                    pe.wait_ge(sb_w_done, h + 1)
                    po = (h % 2) * 64
                    dst = outp[po:po + 64, k % NB, 0:L]
                    w = sb_w[:, h % 4, :]
                    nc.tensor.matmul(dst, sv[:, 0, h * 64:(h + 1) * 64], w[:, 0:L], start=True, stop=False)
                    nc.tensor.matmul(dst[:, P:L], sv[:, 1, h * 64:(h + 1) * 64], w[:, L:384], start=False,
                                     stop=True).then_inc(pv_ready, 1)
                for what, i in ODD_ORDER:
                    if what == "half":
                        j = i // 2
                        (proj_n if j % 3 == 2 else proj_t)(u0 + j, ODD_BANK["unit", j],
                                                           fresh=chunks(2) if i == 0 else None, halves=(i % 2,))
                    elif what == "fill":
                        mem_half("mem_k1", i)
                    else:
                        if i < 16:
                            z_of(i)
                        if 2 <= i < 18:
                            survive(i - 2)
                        if i >= 3:
                            values(i - 3)
                proj_out(UNITS["odd_out"], OUT["odd_out"], lambda q: pe.wait_ge(o_lo_done, 2 * q + 2))

            def mix():
                u0, k0 = UNITS["mix"], OUT["mix"]
                mem_half("mem_v0", 0)
                norm(5)
                mem_half("mem_v0", 1)
                def q_of(b, h):
                    return dq_t[64 * b:64 * b + 64, h, :]

                def k_of(b, h):
                    return dk_t[64 * b:64 * b + 64, h, :]
                for j in range(10):
                    proj_n(u0 + j, k0 + j, chunks(5) if j == 0 else None)
                    if j == 2:
                        pe.wait_ge(late2_in, 16 * LATE2)
                        for i in range(2):
                            k = ACC["ws"] + i
                            acc_taken(pe, k)
                            for g in range(4):
                                ins = flip(acc[:, k % NB, g * P:(g + 1) * P], ws_nat[:, 4 * i + g, :])
                            ins.then_inc(acc_ready, 1)
                        k = ACC["ws"] + 2
                        acc_taken(pe, k)
                        flip(acc[:, k % NB, 0:8], bs_nat, 8).then_inc(acc_ready, 1)
                    if j == 4:
                        pe.wait_ge(rot_done, 1)
                        for i in range(4):
                            k = ACC["dqk"] + i
                            acc_taken(pe, k)
                            for m in range(2):
                                for t in range(T):
                                    ins = flip(acc[:, k % NB, m * L + t * P:m * L + (t + 1) * P],
                                               dqk[:, t, 4 * i + 2 * m:4 * i + 2 * m + 2, :].rearrange("p h d -> p (h d)"))
                            ins.then_inc(acc_ready, 1)
                    if j == 5:
                        emptied(pe, ACC["dqk"], 4)
                        scores(ACC["dsc"], 0, q_of, k_of)
                    if j == 6:
                        scores(ACC["dsc"] + 3, 1, q_of, k_of)
                    if j == 8:
                        pe.wait_ge(ln_ready, 1)
                        emptied(pe, ACC["ws"], 3)
                        for i in range(2):
                            k = ACC["sgu"] + i
                            acc_taken(pe, k)
                            for g in range(4):
                                gg = 4 * i + g
                                ins = nc.tensor.matmul(acc[:, k % NB, g * P:(g + 1) * P], ws_t[:, gg, :],
                                                       zv[:, :, gg * 64:(gg + 1) * 64], start=True, stop=True)
                            ins.then_inc(acc_ready, 1)
                out_emptied(pe, k0 + 8, 2)
                for b in range(2):
                    probs_t(ACC[f"dpt{b}"], b, [dsc[:, i, :] for i in range(2)], exp_done, 6)
                    emptied(pe, ACC[f"dpt{b}"], 3)
                    k = ACC[f"dpv{b}"]
                    acc_taken(pe, k)
                    for h in range(4):
                        vs = [dv[:, t, (2 * h + b) * 64:(2 * h + b + 1) * 64] for t in range(T)]
                        dst = [acc[:, k % NB, t * 256 + h * 64:t * 256 + (h + 1) * 64] for t in range(T)]
                        p0 = dpt[:, b, h * L:(h + 1) * L]
                        nc.tensor.matmul(dst[0], p0[:, 0:P], vs[0], start=True, stop=True)
                        nc.tensor.matmul(dst[1], p0[:, P:L], vs[0], start=True, stop=False)
                        ins = nc.tensor.matmul(dst[1], dpt[:, b, 1024 + h * P:1024 + (h + 1) * P], vs[1],
                                               start=False, stop=True)
                    ins.then_inc(acc_ready, 1)
                for half_ in range(2):
                    mem_half("mem_v1", half_)
                norm(6)
                for half_ in range(2):
                    mem_half("mem_v2", half_)
                proj_out(UNITS["mix_out"], OUT["mix_out"], chunks(6))

            def cross():
                u0 = UNITS["cross"]
                mem_half("mem_v3", 0)
                norm(7)
                mem_half("mem_v3", 1)
                for j in range(4):
                    proj_t(u0 + j, OUT["cross"] + j, fresh=chunks(7) if j == 0 else None)
                out_emptied(pe, OUT["mem_v3"])
                out_emptied(pe, OUT["cross"], 4)
                for t in range(T):
                    for j in range(2):
                        k = ACC["xsc"] + 2 * t + j
                        acc_taken(pe, k)
                        for h in range(2):
                            hh = 2 * j + h
                            for c in range(2):
                                ins = nc.tensor.matmul(acc[:, k % NB, h * L:(h + 1) * L],
                                                       xq_t[:, 2 * hh + c, t * P:(t + 1) * P], km_t[:, 2 * hh + c, :],
                                                       start=c == 0, stop=c == 1)
                        ins.then_inc(acc_ready, 1)
                for kt in range(T):
                    for j in range(2):
                        k = ACC["xpt"] + 2 * kt + j
                        acc_taken(pe, k)
                        pe.wait_ge(p_ready, 6 + 3 + j)
                        for h in range(2):
                            for t in range(T):
                                ins = flip(acc[:, k % NB, h * L + t * P:h * L + (t + 1) * P],
                                           xs[:, t, 2 * j + h, kt * P:(kt + 1) * P])
                        ins.then_inc(acc_ready, 1)
                emptied(pe, ACC["xpt"], 4)
                for h in range(4):
                    k = ACC["xpv"] + h
                    acc_taken(pe, k)
                    for c in range(2):
                        for kt in range(T):
                            ins = nc.tensor.matmul(acc[:, k % NB, c * L:(c + 1) * L],
                                                   vm[:, kt, h * 256 + c * P:h * 256 + (c + 1) * P],
                                                   xpt[:, kt, h, :], start=kt == 0, stop=kt == 1)
                    ins.then_inc(acc_ready, 1)
                proj_out(u0 + 4, OUT["cross_out"], lambda q: emptied(pe, ACC["xpv"] + q))

            if "even" in running:
                even()
            if "ffn0" in running:
                ffn("ffn0")
            if "odd" in running:
                odd()
            if "ffn1" in running:
                ffn("ffn1", "mem_k2")
            if "ffn2" in running:
                ffn("ffn2", "mem_k3")
            if "mix" in running:
                mix()
            if "cross" in running:
                cross()
            if "ffn3" in running:
                ffn("ffn3")

        @block.gpsimd
        def _(pool):
            own = Own(pool, pool_step)
            gp = nc.gpsimd
            gp.memset(half, -0.5).then_inc(half_ready, 1)
            pool.wait_ge(half_ready, 1)

            def norm(n):
                i = NTH[n]
                for t in range(T):
                    for h in range(2):
                        if t == 0 and n in (0, 8):
                            pool.wait_ge(sq_v, SQ_V[n] + h + 1)
                        else:
                            at = [p for p in x_order(n) if p[0] == 1 or n not in (0, 8)].index((t, h))
                            pool.wait_ge(sq_a, SQ_A[n] + at + 1)
                        r, q = [v[:, i, 2 * t + h:2 * t + h + 1] for v in (rms, ss)]
                        if n == 6:
                            own.link(gp.tensor_scalar(r, q, 2 / D, EPS, ALU.mult, ALU.add))
                            gp.tensor_tensor(r, r, half[:, 0:1], ALU.pow).then_inc(rms_ready, 1)
                        elif h == 0:
                            own.link(gp.tensor_scalar(r, q, 1 / D, EPS, ALU.mult, ALU.add))
                            first = r
                        else:
                            own.link(gp.tensor_scalar(r, q, 1 / D, None, ALU.mult))
                            own.link(gp.tensor_tensor(first, first, r, ALU.add))
                            gp.tensor_tensor(first, first, half[:, 0:1], ALU.pow).then_inc(rms_ready, 1)

            def root(x, n, scale, eps, done):
                own.link(gp.tensor_scalar(x, x, scale, eps, ALU.mult, ALU.add))
                gp.tensor_tensor(x, x, half[:, 0:n], ALU.pow).then_inc(done, 1)

            def even():
                norm(0)
                emptied(pool, ACC["prep_bc"], 4)
                pool.wait_ge(tab_ready, 1)
                for k in range(S + 1):
                    q1 = tab[:, 2 * S + k, :].unsqueeze(2).to_broadcast([P, G, PC])
                    q2 = tab[:, 3 * S + 1 + k, :].unsqueeze(2).to_broadcast([P, G, PC])
                    dst = w_out_c[:, k, :, :]
                    own.link(gp.tensor_tensor(pool_tmp, q2, ci.rearrange("p c g -> p g c"), ALU.mult))
                    own.link(gp.tensor_tensor(dst, q1, cr.rearrange("p c g -> p g c"), ALU.mult))
                    ins = gp.tensor_tensor(dst, dst, pool_tmp, ALU.add)
                    if k < S:
                        own.link(ins)
                    if k == 6:
                        pool.wait_ge(qk_sq, 2)
                        root(st[:, 80:100], 20, 1 / 64, EPS, qk_rms)
                ins.then_inc(wc_ready, 1)
                written(pool, ACC["vt"] + 7)
                gp.memset(m_in, 0.0).then_inc(kz_ready, 1)
                pool.wait_ge(small_in, 16 * SMALL)
                written(pool, ACC["s"] + 1)
                pool.wait_ge(decay_ready, 1)
                own.link(gp.tensor_copy(rho, small[:, 12, :].unsqueeze(2).to_broadcast([P, G, NC])))
                gp.memset(rho[:, :, 0:1], 0.0).then_inc(rho_ready, 1)
                dsk = dskip[0:PC, :, :]
                own.link(gp.tensor_tensor(dsk, dsk, ident[0:PC, 0:PC].unsqueeze(1).to_broadcast([PC, G, PC]),
                                          ALU.mult))
                emptied(pool, ACC["k"], 8)
                lag0 = lags[:, :, 0:PC]
                gp.tensor_tensor(lag0, lag0, dsk, ALU.add).then_inc(k_ready, 1)
                norm(8)

            if "even" in running:
                even()
            if "ffn0" in running:
                norm(1)
            if "odd" in running:
                norm(2)
                for h in range(16):
                    k = ACC["sb"] + h
                    emptied(pool, k)
                    w = sb_w[:, h % 4, :].rearrange("p (a b) -> p a b", b=P)[:, 0:3:2, :]
                    gp.affine_select(out=w, in_=w, compare_op=ALU.is_gt, fill=0.0, base=0,
                                     pattern=[[0, 2], [1, P]], channel_multiplier=-1).then_inc(sb_w_done, 1)
            if "ffn1" in running:
                norm(3)
            if "ffn2" in running:
                norm(4)
            if "mix" in running:
                norm(5)
                pool.wait_ge(ln_v, 1)
                root(dst_[:, 16:32], 16, 1 / 64, LN_EPS, ln_rms)
                norm(6)
            if "cross" in running:
                norm(7)
            if "ffn3" in running:
                norm(9)
            if "final" in running:
                norm(10)

        @block.scalar
        def _(act):
            own = Own(act, act_step)
            A = nc.scalar.activation

            def split(u, it=0, n=1):
                for u in range(u, u + n):
                    if u >= NU:
                        return
                    act.wait_ge(raw_landed[u % RAW], 16 * (u // RAW + 1) + 32 * it)
                    if u >= 2:
                        act.wait_ge(w_used, u - 1 + 6 * it)
                    A(w_hi[:, u % 2, :], raw[:, u % RAW, :], ACT.Copy).then_inc(w_hi_ready, 1)

            def squares(n, src):
                for t, h in x_order(n):
                    if t == 0 and n in (0, 8):
                        continue
                    x_piece_ready(act, n, t, h)
                    c = x_piece(n, t, h)
                    A(xn[:, t, c], src[:, t, c], ACT.Square,
                      accum_out=ss[:, NTH[n], 2 * t + h:2 * t + h + 1]).then_inc(sq_a, 1)

            def norm_rows(n, src):
                act.wait_ge(rms_ready, RMS[n] + (4 if n == 6 else 2))
                c = slice(512, D)
                r = 3 if n == 6 else 2
                A(xn[:, 1, c], src[:, 1, c], ACT.Copy, scale=rms[:, NTH[n], r:r + 1]).then_inc(xn_a, 1)

            def norm_parts(n, gain, dst=h_hi):
                for q in range(4):
                    k = ACC[f"norm{n}"] + q
                    written(act, k)
                    for c in range(2):
                        A(dst[:, 2 * q + c, :], acc[:, k % NB, c * L:(c + 1) * L], ACT.Copy,
                          scale=gain[:, 2 * q + c:2 * q + c + 1]).then_inc(h_hi_ready, 1)

            def norm(n, src, gain, u):
                squares(n, src)
                norm_rows(n, src)
                if u is not None:
                    split(u)
                norm_parts(n, gain)

            def mem_copy(name):
                w, j = MEM_UNITS[name]
                act.wait_ge(w_used, UNITS[name] + 1)
                k = OUT[name]
                if w == "k":
                    A(flat(km_t[:, 2 * j:2 * j + 2, :]), outp[:, k % NB, :], ACT.Copy).then_inc(out_free[k % NB], 1)
                else:
                    A(vm[:, :, j * UW:(j + 1) * UW], outp[:, k % NB, :].rearrange("p (t n) -> p t n", n=UW),
                      ACT.Copy).then_inc(out_free[k % NB], 1)

            def ffn(name, mem=None):
                _, f, _, _, _, _, n = FFN[name]
                u0, k0 = UNITS[name], OUT[name]
                norm(n, x_sb, gains[:, n, :], u0 if mem else None)
                split(u0 + 1)
                if mem:
                    mem_copy(mem)
                split(u0 + 2, n=2)

                def gate(i, it=0):
                    j, k = NF * f + i, k0 + 2 * i
                    act.wait_ge(w_used, (u0 + 1 if i == 0 else u0 + 3 * i) + 6 * it)
                    if i >= 1:
                        act.wait_ge(out_free[(k + 1) % NB], (k + 1) // NB + it)
                    A(silu[:, j % 2, :], outp[:, k % NB, :], ACT.Silu).then_inc(out_free[k % NB], 1)
                    out_emptied(act, k + 1, it=it)
                    if i >= 1:
                        act.wait_ge(w_used, u0 + 3 * i - 1 + 6 * it)
                    A(f_hi[:, (j % 2) * 512:(j % 2 + 1) * 512], hf[:, j % 2, :], ACT.Copy).then_inc(f_hi_done, 1)

                def turn(i, it=0):
                    gate(i, it)
                    split(u0 + 4 + 3 * i, it, 3)
                turn(0)
                with act.Fori(0, 4) as it:
                    turn(1, it)
                    turn(2, it)
                gate(9)
                split(u0 + 31, n=2)
                gate(10)
                split(u0 + 33)

            def even():
                u0, k0 = UNITS["even"], OUT["even"]
                act.wait_ge(x_loaded, 16)
                squares(0, x_sb)
                norm_rows(0, x_sb)
                split(0)
                act.wait_ge(gain0_in, 16)
                norm_parts(0, gains[:, 0, :])
                split(1)
                act.wait_ge(ssm_in, 16 * SSM)
                A(small[:, 0, :], log_dt, ACT.Exp).then_inc(dt_ready, 1)
                for j, dst in enumerate([br, bi, cr, ci]):
                    k = ACC["prep_bc"] + j
                    written(act, k)
                    A(dst.rearrange("p c g -> p (c g)"), acc[:, k % NB, :], ACT.Copy).then_inc(acc_free[k % NB], 1)
                act.wait_ge(lam_mag, 1)
                A(tmp_u, tmp_u, ACT.Exp).then_inc(lam_exp, 1)
                A(small[:, 12, :], small[:, 1, :], ACT.Exp, scale=float(S)).then_inc(decay_ready, 1)
                act.wait_ge(lam_frac, 1)
                A(tmp_t, tmp_t, ACT.Sin, scale=TWO_PI).then_inc(lam_sin, 1)

                for j in range(2):
                    act.wait_ge(w_used, u0 + j + 1)
                    k = k0 + j
                    A(flat(u_t[:, 2 * j:2 * j + 2, :]), outp[:, k % NB, :], ACT.Copy).then_inc(out_free[k % NB], 1)
                    split(u0 + 2 + j)
                for j in range(2):
                    for q in range(4):
                        k = ACC["uc"] + 4 * j + q
                        written(act, k)
                        A(uc_part(j, q), uc_bank(k), ACT.Copy).then_inc(acc_free[k % NB], 1)
                for j in range(3):
                    act.wait_ge(w_used, u0 + 2 + j + 1)
                    k = k0 + 2 + j
                    src = outp[:, k % NB, :].rearrange("p (t n) -> p t n", n=UW)
                    if j < 2:
                        for t in range(T):
                            ins = A(qkv[:, t, 0:512].rearrange("p (h b d) -> p h b d", b=2, d=64)[:, :, j, :],
                                    src[:, t, :].rearrange("p (h d) -> p h d", d=64), ACT.Copy)
                    else:
                        ins = A(qkv[:, :, 512:768], src, ACT.Copy)
                    ins.then_inc(out_free[k % NB], 1)
                    split(u0 + 4 + j)
                for j in range(8):
                    acc_copy(ACC["vt"] + j, flat(vt[:, 4 * j:4 * j + 4, :]))
                act.wait_ge(small_in, 16 * SMALL)
                for j in range(3):
                    k = ACC["qk"] + j
                    written(act, k)
                    dst, w = (flat(q_t[j]), 512) if j < 2 else (k_t, L)
                    A(dst, acc[:, k % NB, 0:w], ACT.Copy,
                      scale=qk_gain[:, (j == 2) * 1:(j == 2) * 1 + 1]).then_inc(acc_free[k % NB], 1)
                for j in range(2):
                    acc_copy(ACC["u"] + j, flat(u_ch[:, 16 * j:16 * j + 16, :]))
                for n in range(3):
                    exps(n, 0, sc_tiles[n], sink=True)
                act.wait_ge(al_frac, 1)
                for j in range(2):
                    acc_copy(ACC["s"] + j, s_ch[:, j * 512:(j + 1) * 512])
                A(alpha, alpha, ACT.Sin, scale=TWO_PI).then_inc(al_sin, 1)
                for j in range(8):
                    acc_copy(ACC["k"] + j, lags[:, 4 * j:4 * j + 4, :], PC, P)
                for n in range(3, 6):
                    exps(n, 0, sc_tiles[n], sink=True)
                for b in range(2):
                    for j in range(3):
                        acc_copy(ACC[f"pt{b}"] + j, pt[:, b, j * 512:(j + 1) * 512])
                    mix_part(ACC[f"pv{b}"], 2 * b)
                for j in range(2):
                    k = ACC["y"] + j
                    written(act, k)
                    A(y_ch[:, :, 4 * j:4 * j + 4, :].rearrange("p s g c -> p g s c"),
                      acc[:, k % NB, :].rearrange("p (g s c) -> p g s c", g=4, c=PC),
                      ACT.Copy).then_inc(acc_free[k % NB], 1)
                for cc in range(4):
                    k = ACC["yt"] + cc
                    written(act, k)
                    A(y_f[:, cc, :].rearrange("p (c s) -> p s c", s=S),
                      acc[:, k % NB, 0:L].rearrange("p (s c) -> p s c", c=NC),
                      ACT.Gelu_apprx_tanh).then_inc(acc_free[k % NB], 1)
                for cc in range(4):
                    emptied(act, ACC["yt"] + cc)
                    A(f_hi[:, cc * L:(cc + 1) * L], y_f[:, cc, :], ACT.Copy).then_inc(yhi_ready, 1)
                act.wait_ge(mem_in, 16)
                squares(8, mem_sb)
                norm_rows(8, mem_sb)
                act.wait_ge(w_used, u0 + 6)
                for j in range(2):
                    k = OUT["glu"] + j
                    for m in range(2):
                        cc = 2 * j + m
                        ins = A(sig[:, cc, :], outp[:, k % NB, m * L:(m + 1) * L], ACT.Sigmoid,
                                bias=b_glu[:, cc:cc + 1])
                        if m == 1:
                            ins.then_inc(out_free[k % NB], 1)
                for cc in range(4):
                    act.wait_ge(glu_done, cc + 1)
                    A(h_hi[:, 4 + cc, :], sig[:, cc, :], ACT.Copy).then_inc(glu_hi, 1)
                split(u0 + 7)
                norm_parts(8, gains[:, 8, :], m_hi)
                split(u0 + 8, n=3)

            def exps(n, before, s, scale=1.0, sink=False, k=None):
                act.wait_ge(sub_done, before + n + 1)
                at = stat_at(n, before)
                h = s.shape[1]
                if sink:
                    sk = st[:, 24 + at:24 + at + h]
                    A(sk, sk, ACT.Exp)
                for i in range(h):
                    src = s[:, i, :] if k is None else acc[:, k % NB, i * L:(i + 1) * L]
                    ins = A(s[:, i, :], src, ACT.Exp, scale=scale, bias=st[:, 120 + at + i:121 + at + i],
                            accum_out=st[:, 48 + at + i:49 + at + i])
                ins.then_inc(exp_done if k is None else acc_free[k % NB], 1)

            def acc_copy(k, dst, parts=P, inner=512):
                written(act, k)
                src = acc[0:parts, k % NB, :]
                if inner < 512:
                    src = src.rearrange("p (a b) -> p a b", b=inner)
                A(dst, src, ACT.Copy).then_inc(acc_free[k % NB], 1)

            def mix_part(k, c):
                written(act, k)
                A(flat(h_hi[:, c:c + 2, :]), acc[:, k % NB, :], ACT.Copy).then_inc(mix_hi, 1)

            def odd():
                u0, k0 = UNITS["odd"], OUT["odd"]
                norm(2, x_sb, gains[:, 2, :], u0)
                split(u0 + 1)
                mem_copy("mem_k0")

                def unit_out(j):
                    k = ODD_BANK["unit", j]
                    g = j // 3
                    if j % 3 == 0:
                        act.wait_ge(w_used, u0 + j + 1)
                        A(flat(sq_t[:, 2 * g:2 * g + 2, :]), outp[:, k % NB, :], ACT.Copy,
                          scale=0.125).then_inc(out_free[k % NB], 1)
                    elif j % 3 == 2:
                        act.wait_ge(w_used, u0 + j + 1)
                        A(sv[:, :, g * UW:(g + 1) * UW], outp[:, k % NB, :].rearrange("p (t n) -> p t n", n=UW),
                          ACT.Copy).then_inc(out_free[k % NB], 1)

                def softplus(h):
                    k = ACC["sb"] + h
                    written(act, k)
                    if h >= 4:
                        act.wait_ge(sb_sp_done, h - 3)
                    e = sb_e[:, h % 4, :]
                    own.link(A(e, acc[:, k % NB, 0:384], ACT.Abs))
                    own.link(A(e, e, ACT.Exp, scale=-1.0))
                    A(e, e, ACT.Ln, bias=1.0).then_inc(sb_ln, 1)

                def weigh(h):
                    k = ACC["sb"] + h
                    act.wait_ge(sb_cum, h + 1)
                    if h >= 4:
                        act.wait_ge(pv_ready, h - 3)
                    A(sb_w[:, h % 4, :], acc[:, k % NB, 0:384], ACT.Exp).then_inc(acc_free[k % NB], 1)

                def pv(j):
                    k = ODD_BANK["pv", j]
                    act.wait_ge(pv_ready, 2 * j + 2)
                    A(sb_o[:, j, :], outp[:, k % NB, 0:L], ACT.Copy).then_inc(out_free[k % NB], 1)

                def high(j):
                    out_emptied(act, ODD_BANK["pv", j])
                    A(h_hi[:, j, :], sb_o[:, j, :], ACT.Copy).then_inc(mix_hi, 1)
                for what, i in ODD_ORDER:
                    if what == "half" and i % 2 == 1:
                        unit_out(i // 2)
                        split(u0 + 2 + i // 2)
                    elif what == "fill" and i == 1:
                        split(u0 + 14)
                        mem_copy("mem_k1")
                        for j in range(4):
                            high(j)
                    elif what == "head":
                        if i < 16:
                            softplus(i)
                        if 2 <= i < 18:
                            weigh(i - 2)
                        if i >= 5 and i % 2 == 1:
                            pv((i - 5) // 2)
                            if i > 12:
                                high((i - 5) // 2)
                pv(7)
                high(7)
                for j in range(3):
                    split(UNITS["odd_out"] + 2 + j)

            def mix():
                u0, k0 = UNITS["mix"], OUT["mix"]
                norm(5, x_sb, gains[:, 5, :], u0)
                split(u0 + 1)
                mem_copy("mem_v0")
                act.wait_ge(rope_frac, 1)
                own.link(A(rot[:, 2, :, :], rot[:, 1, :, :], ACT.Sin, scale=0.5))
                A(rot[:, 3, :, :], rot[:, 1, :, :], ACT.Sin).then_inc(rope_sin, 1)
                for j in range(10):
                    act.wait_ge(w_used, u0 + j + 1)
                    k = k0 + j
                    src = outp[:, k % NB, :].rearrange("p (t n) -> p t n", n=UW)
                    if j < 4:
                        A(dqk[:, :, 4 * j:4 * j + 4, :].rearrange("p t h d -> p t (h d)"), src,
                          ACT.Copy).then_inc(out_free[k % NB], 1)
                    elif j < 8:
                        dst = (zv if j < 6 else zu)[:, :, (j % 2) * UW:(j % 2 + 1) * UW]
                        A(dst, src, ACT.Gelu).then_inc(out_free[k % NB], 1)
                    else:
                        A(dv[:, :, (j - 8) * UW:(j - 7) * UW], src, ACT.Copy).then_inc(out_free[k % NB], 1)
                    split(u0 + 2 + j)
                    if j == 4:
                        for i in range(4):
                            acc_copy(ACC["dqk"] + i, flat((dq_t if i < 2 else dk_t)[:, 2 * (i % 2):2 * (i % 2) + 2, :]))
                    if j == 5:
                        for n in range(3):
                            exps(n, 6, dsc_tiles[n])
                    if j == 7:
                        for n in range(3, 6):
                            exps(n, 6, dsc_tiles[n])
                for b in range(2):
                    for j in range(3):
                        acc_copy(ACC[f"dpt{b}"] + j, dpt[:, b, j * 512:(j + 1) * 512])
                emptied(act, ACC["sgu"], 2)
                for b in range(2):
                    emptied(act, ACC[f"dpv{b}"])
                squares(6, y_nat)
                norm_rows(6, y_nat)
                mem_copy("mem_v1")
                split(u0 + 12)
                norm_parts(6, g_ab)
                split(u0 + 13)
                mem_copy("mem_v2")
                for j in range(3):
                    split(UNITS["mix_out"] + 2 + j)

            def cross():
                u0 = UNITS["cross"]
                norm(7, x_sb, gains[:, 7, :], u0)
                split(u0 + 1)
                mem_copy("mem_v3")
                for j in range(4):
                    act.wait_ge(w_used, u0 + j + 1)
                    k = OUT["cross"] + j
                    A(flat(xq_t[:, 2 * j:2 * j + 2, :]), outp[:, k % NB, :], ACT.Copy).then_inc(out_free[k % NB], 1)
                    split(u0 + 2 + j)
                for n in range(4):
                    exps(n, 12, xs_tiles[n], 1 / 16, k=ACC["xsc"] + n)
                for kt in range(T):
                    for j in range(2):
                        acc_copy(ACC["xpt"] + 2 * kt + j, flat(xpt[:, kt, 2 * j:2 * j + 2, :]))
                for h in range(4):
                    mix_part(ACC["xpv"] + h, 2 * h)
                for j in range(3):
                    split(u0 + 6 + j)

            if "even" in running:
                even()
            if "ffn0" in running:
                ffn("ffn0")
            if "odd" in running:
                odd()
            if "ffn1" in running:
                ffn("ffn1", "mem_k2")
            if "ffn2" in running:
                ffn("ffn2", "mem_k3")
            if "mix" in running:
                mix()
            if "cross" in running:
                cross()
            if "ffn3" in running:
                ffn("ffn3")
            if "final" in running:
                squares(10, x_sb)

        @block.vector
        def _(dve):
            own = Own(dve, dve_step)
            V = nc.vector
            tt, ts, stt = V.tensor_tensor, V.tensor_scalar, V.scalar_tensor_tensor
            link = own.link

            def split(u, it=0, n=1):
                for u in range(u, u + n):
                    if u >= NU:
                        return
                    dve.wait_ge(w_hi_ready, u + 1 + 6 * it)
                    tt(w_lo[:, u % 2, :], raw[:, u % RAW, :], w_hi[:, u % 2, :].bitcast(F32),
                       ALU.subtract).then_inc(w_lo_ready, 1)

            def norm_front(n, src):
                if n in (0, 8):
                    for h in range(2):
                        c = slice(h * 512, (h + 1) * 512)
                        V.tensor_tensor_reduce(out=xn[:, 0, c], in0=src[:, 0, c], in1=src[:, 0, c], scale=1.0,
                                               scalar=0.0, op0=ALU.mult, op1=ALU.add,
                                               accum_out=ss[:, NTH[n], h:h + 1]).then_inc(sq_v, 1)
                if n == 10:
                    dve.wait_ge(fin_in, 16)
                    for t in range(T):
                        dve.wait_ge(rms_ready, RMS[n] + t + 1)
                        stt(xn[:, t, :], src[:, t, :], rms[:, NTH[n], 2 * t:2 * t + 1], fin_g, ALU.mult,
                            ALU.mult).then_inc(result_ready, 1)
                    return
                if n == 6:
                    for h in range(2):
                        c = slice(h * 512, (h + 1) * 512)
                        dve.wait_ge(rms_ready, RMS[n] + h + 1)
                        ins = ts(xn[:, 0, c], src[:, 0, c], rms[:, NTH[n], h:h + 1], None, ALU.mult)
                else:
                    dve.wait_ge(rms_ready, RMS[n] + 1)
                    ins = ts(xn[:, 0, :], src[:, 0, :], rms[:, NTH[n], 0:1], None, ALU.mult)
                ins.then_inc(xn_v, 1)
                dve.wait_ge(rms_ready, RMS[n] + (3 if n == 6 else 2))
                ts(xn[:, 1, 0:512], src[:, 1, 0:512], rms[:, NTH[n], 2:3], None, ALU.mult).then_inc(xn_v, 1)

            def norm_back(n, gain, hi=h_hi, lo=h_lo):
                for q in range(4):
                    k = ACC[f"norm{n}"] + q
                    dve.wait_ge(h_hi_ready, 8 * NTH[n] + 2 * q + 2)
                    for c in range(2):
                        ch = 2 * q + c
                        ins = stt(lo[:, ch, :], acc[:, k % NB, c * L:(c + 1) * L], gain[:, ch:ch + 1],
                                  hi[:, ch, :].bitcast(F32), ALU.mult, ALU.subtract)
                    ins.then_inc(acc_free[k % NB], 1)

            def ffn(name, mem=None):
                _, f, _, _, _, scale, n = FFN[name]
                u0, k0, d0 = UNITS[name], OUT[name], ACC[name]
                norm_front(n, x_sb)
                if mem:
                    split(u0)
                norm_back(n, gains[:, n, :])
                split(u0 + 1)
                split(u0 + 2, n=2)

                def product(i, it=0):
                    j, k = NF * f + i, k0 + 2 * i
                    out_emptied(dve, k, it=it)
                    dve.wait_ge(w_used, (u0 + 2 if i == 0 else u0 + 3 * i + 1) + 6 * it)
                    if j >= 2:
                        dve.wait_ge(f_hi_done, j - 1 + 2 * it)
                        dve.wait_ge(f_lo_done, j - 1 + 2 * it)
                    b = j % 2
                    tt(hf[:, b, :], silu[:, b, :], outp[:, (k + 1) % NB, :], ALU.mult).then_inc(out_free[(k + 1) % NB], 1)
                    out_emptied(dve, k + 1, it=it)
                    dve.wait_ge(f_hi_done, j + 1 + 2 * it)
                    tt(f_lo[:, b * 512:(b + 1) * 512], hf[:, b, :], f_hi[:, b * 512:(b + 1) * 512].bitcast(F32),
                       ALU.subtract).then_inc(f_lo_done, 1)

                def turn(i, it=0):
                    product(i, it)
                    split(u0 + 4 + 3 * i, it, 3)
                turn(0)
                with dve.Fori(0, 4) as it:
                    turn(1, it)
                    turn(2, it)
                product(9)
                split(u0 + 31, n=2)
                product(10)
                split(u0 + 33)
                for t in range(T):
                    for h in range(2):
                        k = d0 + 2 * t + h
                        dve.wait_ge(*((sum_ready, SUMS[name] + 2 * t + h + 1) if t + h < 2 else (w_used, u0 + 33)))
                        xs_ = x_sb[:, t, h * 512:(h + 1) * 512]
                        stt(xs_, acc[:, k % NB, :], scale, xs_, ALU.mult, ALU.add).then_inc(acc_free[k % NB], 1)

            def add_out(name, u, k):
                for j in range(3):
                    dve.wait_ge(w_used, u + j + 1)
                    xs_ = x_sb[:, :, j * UW:(j + 1) * UW]
                    tt(xs_, xs_, outp[:, (k + j) % NB, :].rearrange("p (t n) -> p t n", n=UW),
                       ALU.add).then_inc(out_free[(k + j) % NB], 1)
                    split(u + j + 2)
                for t in range(T):
                    dve.wait_ge(*((sum_ready, SUMS[name] + 1) if t == 0 else (w_used, u + 4)))
                    xs_ = x_sb[:, t, 3 * UW:]
                    tt(xs_, xs_, outp[:, (k + 3 + t) % NB, 0:UW], ALU.add).then_inc(out_free[(k + 3 + t) % NB], 1)

            def soft_front(n, before, s, scale, k, mask=None, sink=None):
                _, h, w = s.shape
                at = stat_at(n, before)
                written(dve, k)
                src = acc[:, k % NB, :].rearrange("p (h w) -> p h w", w=w)
                mx, nm = st[:, at:at + h], st[:, 120 + at:120 + at + h]
                if mask is None:
                    link(V.reduce_max(mx, src, AX))
                    ts(nm, mx, -scale, None, ALU.mult).then_inc(sub_done, 1)
                    return
                for i in range(h):
                    ins = stt(s[:, i, :], src[:, i, :], scale, mask, ALU.mult, ALU.add)
                ins.then_inc(acc_free[k % NB], 1)
                emptied(dve, k)
                link(V.reduce_max(mx, s, AX))
                if sink is None:
                    ts(nm, mx, -1.0, None, ALU.mult).then_inc(sub_done, 1)
                else:
                    link(tt(mx, mx, sink, ALU.max))
                    link(ts(nm, mx, -1.0, None, ALU.mult))
                    tt(st[:, 24 + at:24 + at + h], sink, nm, ALU.add).then_inc(sub_done, 1)

            def soft_back(n, before, s, sink=False):
                _, h, w = s.shape
                at = stat_at(n, before)
                sm = st[:, 48 + at:48 + at + h]
                if sink:
                    link(tt(sm, sm, st[:, 24 + at:24 + at + h], ALU.add))
                link(V.reciprocal(sm, sm))
                tt(s, s, sm.unsqueeze(2).to_broadcast([P, h, w]), ALU.mult).then_inc(p_ready, 1)

            def mix_low(n, k, c):
                dve.wait_ge(mix_hi, n + 1)
                tt(flat(h_lo[:, c:c + 2, :]), acc[:, k % NB, :], flat(h_hi[:, c:c + 2, :]).bitcast(F32),
                   ALU.subtract).then_inc(acc_free[k % NB], 1)

            def turns_off(x, n):
                link(ts(n, x, MAGIC, MAGIC, ALU.add, ALU.subtract))
                return tt(x, x, n, ALU.subtract)

            def radians_off(r, x, n):
                link(ts(n, x, float(1 / (2 * np.pi)), MAGIC, ALU.mult, ALU.add))
                link(ts(n, n, MAGIC, None, ALU.subtract))
                link(stt(r, n, -PI_A, x, ALU.mult, ALU.add))
                link(stt(r, n, -PI_B, r, ALU.mult, ALU.add))
                return stt(r, n, -PI_C, r, ALU.mult, ALU.add)

            def even():
                u0, k0 = UNITS["even"], OUT["even"]
                dve.wait_ge(x_loaded, 16)
                norm_front(0, x_sb)
                split(0)
                norm_back(0, gains[:, 0, :])
                split(1)
                k = ACC["prep_a"]
                written(dve, k)
                V.tensor_copy(flat(a_t), acc[:, k % NB, 0:2 * G]).then_inc(acc_free[k % NB], 1)
                emptied(dve, k)
                dve.wait_ge(dt_ready, 1)
                are, aim = a_t[:, 0, :], a_t[:, 1, :]
                sm = [small[:, j, :] for j in range(16)]
                link(tt(sm[1], are, sm[0], ALU.mult))
                link(tt(sm[2], aim, sm[0], ALU.mult))
                tt(tmp_u, steps.unsqueeze(2).to_broadcast([P, 36, G]), sm[1].unsqueeze(1).to_broadcast([P, 36, G]),
                   ALU.mult).then_inc(lam_mag, 1)
                link(radians_off(sm[4], sm[2], sm[3]))
                link(ts(sm[5], sm[4], float(1 / (2 * np.pi)), None, ALU.mult))
                link(tt(tmp_t, steps.unsqueeze(2).to_broadcast([P, 36, G]),
                        sm[5].unsqueeze(1).to_broadcast([P, 36, G]), ALU.mult))
                link(tt(tmp_t, tmp_t, phase.unsqueeze(2).to_broadcast([P, 36, G]), ALU.add))
                turns_off(tmp_t, tmp_n).then_inc(lam_frac, 1)
                dve.wait_ge(lam_exp, 1)
                dve.wait_ge(lam_sin, 1)
                tt(tab, tmp_t, tmp_u, ALU.mult).then_inc(tab_ready, 1)
                dve.wait_ge(tab_ready, 1)
                split(u0 + 2)
                lre, lim = tab[:, 34, :], tab[:, 35, :]
                link(tt(sm[7], are, are, ALU.mult))
                link(tt(sm[8], aim, aim, ALU.mult))
                link(tt(sm[7], sm[7], sm[8], ALU.add))
                link(V.reciprocal(sm[8], sm[7]))
                link(ts(sm[11], lre, -1.0, None, ALU.add))
                link(tt(sm[9], sm[11], are, ALU.mult))
                link(tt(sm[10], lim, aim, ALU.mult))
                link(tt(sm[9], sm[9], sm[10], ALU.add))
                link(tt(sm[10], lim, are, ALU.mult))
                link(tt(sm[13], sm[11], aim, ALU.mult))
                link(tt(sm[10], sm[10], sm[13], ALU.subtract))
                link(tt(sm[9], sm[9], sm[8], ALU.mult))
                link(tt(sm[10], sm[10], sm[8], ALU.mult))
                emptied(dve, ACC["prep_bc"], 4)
                split(u0 + 3)
                wr = sm[9].unsqueeze(1).to_broadcast([P, PC, G])
                wi = sm[10].unsqueeze(1).to_broadcast([P, PC, G])
                scr = view(REG_V, PC, G)
                link(tt(scr, wi, bi, ALU.mult))
                link(tt(cbr, wr, br, ALU.mult))
                link(tt(cbr, cbr, scr, ALU.subtract))
                link(tt(scr, wi, br, ALU.mult))
                link(tt(cbi, wr, bi, ALU.mult))
                link(tt(cbi, cbi, scr, ALU.add))
                V.tensor_copy(bst[0:N, :, :], cbr[0:N, :, :]).then_inc(bb_ready, 1)
                V.tensor_copy(bst[N:P, :, :], cbi[N:P, :, :]).then_inc(bb_ready, 1)
                split(u0 + 4)

                def carry_in(s0):
                    n = S // 2
                    dst = v_in[:, :, s0:s0 + n, :].rearrange("p g s c -> p s g c")
                    scr = flat(xn[:, :, :]).rearrange("p (s g c) -> p s g c", s=n, c=PC)
                    shape = [P, n, G, PC]
                    p1 = tab[:, s0:s0 + n, :].unsqueeze(3).to_broadcast(shape)
                    p2 = tab[:, S + s0:S + s0 + n, :].unsqueeze(3).to_broadcast(shape)
                    link(tt(scr, p2, cbi.rearrange("p c g -> p g c").unsqueeze(1).to_broadcast(shape), ALU.mult))
                    link(tt(dst, p1, cbr.rearrange("p c g -> p g c").unsqueeze(1).to_broadcast(shape), ALU.mult))
                    return tt(dst, dst, scr, ALU.add)

                link(carry_in(0))
                out_emptied(dve, k0 + 2, 3)
                for t in range(T):
                    qk = qkv[:, t, 0:640]
                    scr = arena[:, o_u:o_u + 640]
                    if t:
                        dve.wait_ge(qk_sq, t)
                    link(tt(scr, qk, qk, ALU.mult))
                    V.reduce_sum(st[:, 80 + 10 * t:90 + 10 * t], scr.rearrange("p (h d) -> p h d", d=64),
                                 AX).then_inc(qk_sq, 1)
                carry_in(S // 2).then_inc(v_ready, 1)
                for t in range(T):
                    qk = qkv[:, t, 0:640].rearrange("p (h d) -> p h d", d=64)
                    if t == 0:
                        dve.wait_ge(qk_rms, 1)
                    ins = tt(qk, qk, st[:, 80 + 10 * t:90 + 10 * t].unsqueeze(2).to_broadcast([P, 10, 64]), ALU.mult)
                    if t == 0:
                        link(ins)
                ins.then_inc(qk_ready, 1)
                dve.wait_ge(small_in, 16 * SMALL)

                def front(n):
                    t = sc_tiles[n]
                    h0 = 4 * (n // 3) + (0, 0, 2)[n % 3]
                    soft_front(n, 0, t, 0.125, ACC[f"sc{n // 3}"] + n % 3,
                               swa_mask[:, 0:P] if n % 3 == 0 else swa_mask[:, P:384], sinks[:, h0:h0 + t.shape[1]])

                def back(n):
                    dve.wait_ge(exp_done, n + 1)
                    soft_back(n, 0, sc_tiles[n], sink=True)
                for n in range(3):
                    front(n)
                link(ts(sm[6], sm[5], float(S), None, ALU.mult))
                link(turns_off(sm[6], sm[3]))
                link(tt(alpha[:, 1, :, :], sm[6].unsqueeze(2).to_broadcast([P, G, NC]),
                        chunk.unsqueeze(1).to_broadcast([P, G, NC]), ALU.mult))
                link(ts(alpha[:, 0, :, :], alpha[:, 1, :, :], 0.25, None, ALU.add))
                turns_off(alpha.rearrange("p a g c -> p (a g c)"), flat(xn[:, :, :])).then_inc(al_frac, 1)
                for n in range(3):
                    back(n)
                dve.wait_ge(al_sin, 1)
                cos_, sin_ = [alpha[:, j, :, :].rearrange("p g c -> p (g c)") for j in range(2)]
                gf = flat(g_st)
                for j in range(2):
                    k = ACC["js"] + j
                    o = slice(j * 512, (j + 1) * 512)
                    written(dve, k)
                    tt(t_ch[:, o], sin_[:, o], acc[:, k % NB, :], ALU.mult).then_inc(acc_free[k % NB], 1)
                    link(tt(gf[:, o], cos_[:, o], s_ch[:, o], ALU.mult))
                    emptied(dve, k)
                    link(tt(gf[:, o], gf[:, o], t_ch[:, o], ALU.subtract))
                dve.wait_ge(rho_ready, 1)
                V.tensor_tensor_scan(gf, flat(rho), gf, 0.0, ALU.mult, ALU.add).then_inc(g_ready, 1)
                for n in range(3, 6):
                    front(n)
                split(u0 + 5)
                dve.wait_ge(g_ready, 1)
                for j in range(2):
                    k = ACC["jg"] + j
                    o = slice(j * 512, (j + 1) * 512)
                    written(dve, k)
                    tt(t_ch[:, o], sin_[:, o], acc[:, k % NB, :], ALU.mult).then_inc(acc_free[k % NB], 1)
                    link(tt(s_ch[:, o], cos_[:, o], gf[:, o], ALU.mult))
                    emptied(dve, k)
                link(V.memset(hpad[:, :, 0:1], 0.0))
                tt(hpad[:, :, 1:], s_ch.rearrange("p (g c) -> p g c", c=NC),
                   t_ch.rearrange("p (g c) -> p g c", c=NC), ALU.add).then_inc(h_ready, 1)
                for n in range(3, 6):
                    back(n)
                split(u0 + 6)
                for b in range(2):
                    mix_low(b, ACC[f"pv{b}"], 2 * b)
                for cc in range(4):
                    dve.wait_ge(yhi_ready, cc + 1)
                    tt(f_lo[:, cc * L:(cc + 1) * L], y_f[:, cc, :], f_hi[:, cc * L:(cc + 1) * L].bitcast(F32),
                       ALU.subtract).then_inc(ylo_ready, 1)
                dve.wait_ge(mem_in, 16)
                norm_front(8, mem_sb)
                out_emptied(dve, OUT["glu"], 2)
                for cc in range(4):
                    tt(sig[:, cc, :], sig[:, cc, :], y_f[:, cc, :], ALU.mult).then_inc(glu_done, 1)
                for cc in range(4):
                    dve.wait_ge(glu_hi, cc + 1)
                    tt(h_lo[:, 4 + cc, :], sig[:, cc, :], h_hi[:, 4 + cc, :].bitcast(F32),
                       ALU.subtract).then_inc(glu_lo, 1)
                split(u0 + 7)
                norm_back(8, gains[:, 8, :], m_hi, m_lo)
                add_out("even", u0 + 6, OUT["even_out"])

            def odd():
                u0, k0 = UNITS["odd"], OUT["odd"]
                norm_front(2, x_sb)
                split(u0)
                norm_back(2, gains[:, 2, :])
                split(u0 + 1)
                dve.wait_ge(late_in, 16)

                def keys_out(g):
                    k = ODD_BANK["unit", 3 * g + 1]
                    dve.wait_ge(w_used, u0 + 3 * g + 2)
                    V.tensor_copy(flat(sk_t[:, 2 * g:2 * g + 2, :]), outp[:, k % NB, :]).then_inc(out_free[k % NB], 1)

                def softplus(h):
                    k = ACC["sb"] + h
                    dve.wait_ge(sb_ln, h + 1)
                    if h >= 4:
                        dve.wait_ge(sb_cum, h - 3)
                    b = sb_sp[:, h % 4, :]
                    link(stt(b, acc[:, k % NB, 0:384], 0.0, sb_e[:, h % 4, :], ALU.max, ALU.add))
                    d = b.rearrange("p (a b) -> p a b", b=P)[:, 0:3:2, :]
                    tt(d, d, const("strict").unsqueeze(1).to_broadcast([P, 2, P]), ALU.mult).then_inc(sb_sp_done, 1)

                def low(j):
                    dve.wait_ge(mix_hi, 2 + j + 1)
                    tt(h_lo[:, j, :], sb_o[:, j, :], h_hi[:, j, :].bitcast(F32), ALU.subtract).then_inc(o_lo_done, 1)
                for what, i in ODD_ORDER:
                    if what == "half" and i % 2 == 1:
                        if i // 2 % 3 == 1:
                            keys_out(i // 6)
                        split(u0 + 2 + i // 2)
                    elif what == "fill" and i == 1:
                        split(u0 + 14)
                        for j in range(4):
                            low(j)
                    elif what == "head":
                        if 1 <= i < 17:
                            softplus(i - 1)
                        if i > 12 and i % 2 == 1:
                            low((i - 5) // 2)
                low(7)
                add_out("odd", UNITS["odd_out"], OUT["odd_out"])

            def mix():
                u0, k0 = UNITS["mix"], OUT["mix"]
                norm_front(5, x_sb)
                split(u0)
                norm_back(5, gains[:, 5, :])
                split(u0 + 1)
                dve.wait_ge(late2_in, 16 * LATE2)
                link(V.tensor_copy(pos_f, pos_i[:, :]))
                link(tt(rot[:, 0, :, :], pos_f.unsqueeze(2).to_broadcast([P, T, 8]),
                        const("invf").unsqueeze(1).to_broadcast([P, T, 8]), ALU.mult))
                r1 = flat(rot[:, 1, :, :])
                link(radians_off(r1, flat(rot[:, 0, :, :]), flat(rot[:, 2, :, :])))
                ts(r1, r1, 3.1415925, -3.1415925, ALU.min, ALU.max).then_inc(rope_frac, 1)
                for j in range(3):
                    split(u0 + 2 + j)
                for j in range(2):
                    k = ACC["ws"] + j
                    written(dve, k)
                    tt(ws_t[:, 4 * j:4 * j + 4, :], acc[:, k % NB, :].rearrange("p (g i) -> p g i", i=P),
                       const("tril").unsqueeze(1).to_broadcast([P, 4, P]), ALU.mult).then_inc(acc_free[k % NB], 1)
                k = ACC["ws"] + 2
                written(dve, k)
                V.tensor_copy(bs_t, acc[:, k % NB, 0:8]).then_inc(acc_free[k % NB], 1)
                dve.wait_ge(rope_sin, 1)
                link(tt(rot[:, 4, :, :], rot[:, 2, :, :], rot[:, 2, :, :], ALU.mult))
                link(ts(rot[:, 4, :, :], rot[:, 4, :, :], -2.0, 1.0, ALU.mult, ALU.add))
                split(u0 + 5)
                out_emptied(dve, k0, 4)
                cosb = rot[:, 4, :, :].unsqueeze(2).to_broadcast([P, T, 16, 8])
                sinb = rot[:, 3, :, :].unsqueeze(2).to_broadcast([P, T, 16, 8])
                x1, x2 = dqk[:, :, :, 0:8], dqk[:, :, :, 8:16]
                r = [ropet[:, j, :, :, :] for j in range(4)]
                link(tt(r[0], x1, cosb, ALU.mult))
                link(tt(r[1], x2, sinb, ALU.mult))
                link(tt(r[2], x2, cosb, ALU.mult))
                link(tt(r[3], x1, sinb, ALU.mult))
                link(tt(x1, r[0], r[1], ALU.subtract))
                tt(x2, r[2], r[3], ALU.add).then_inc(rot_done, 1)
                split(u0 + 6)
                split(u0 + 7)
                dm = const("dil")

                def front(n):
                    soft_front(n, 6, dsc_tiles[n], 0.125, ACC["dsc"] + n, dm[:, 0:P] if n % 3 == 0 else dm[:, P:384])
                for n in range(3):
                    front(n)
                out_emptied(dve, k0 + 4, 2)
                z = zv.rearrange("p t (g c) -> p (t g) c", c=64)
                zq = zs.rearrange("p t (g c) -> p (t g) c", c=64)
                mean, var = dst_[:, 0:16], dst_[:, 16:32]
                wide = [P, 16, 64]
                link(V.reduce_sum(mean, z, AX))
                link(ts(mean, mean, 1 / 64, None, ALU.mult))
                link(tt(z, z, mean.unsqueeze(2).to_broadcast(wide), ALU.subtract))
                link(tt(zq, z, z, ALU.mult))
                V.reduce_sum(var, zq, AX).then_inc(ln_v, 1)
                split(u0 + 8)
                dve.wait_ge(ln_rms, 1)
                link(tt(z, z, var.unsqueeze(2).to_broadcast(wide), ALU.mult))
                link(tt(zv, zv, ln_g.unsqueeze(1).to_broadcast([P, T, 512]), ALU.mult))
                tt(zv, zv, ln_b.unsqueeze(1).to_broadcast([P, T, 512]), ALU.add).then_inc(ln_ready, 1)
                split(u0 + 9)
                for n in range(3, 6):
                    front(n)
                split(u0 + 10)
                out_emptied(dve, k0 + 6, 2)
                for j in range(2):
                    k = ACC["sgu"] + j
                    written(dve, k)
                    for g in range(4):
                        gg = 4 * j + g
                        c = slice(gg * 64, (gg + 1) * 64)
                        ins = stt(y_nat[:, :, c], acc[:, k % NB, g * P:(g + 1) * P].rearrange("p (t c) -> p t c", c=64),
                                  bs_t[:, gg:gg + 1], zu[:, :, c], ALU.add, ALU.mult)
                    ins.then_inc(acc_free[k % NB], 1)
                split(u0 + 11)
                dve.wait_ge(exp_done, 12)
                sm = st[:, 48:64]
                link(V.reciprocal(sm, sm))
                for b in range(2):
                    k = ACC[f"dpv{b}"]
                    written(dve, k)
                    for t in range(T):
                        ins = tt(y_nat[:, t, 512:].rearrange("p (h b d) -> p h b d", b=2, d=64)[:, :, b, :],
                                 acc[:, k % NB, t * 256:(t + 1) * 256].rearrange("p (h d) -> p h d", d=64),
                                 sm[:, 8 * b + 4 * t:8 * b + 4 * t + 4].unsqueeze(2).to_broadcast([P, 4, 64]), ALU.mult)
                    ins.then_inc(acc_free[k % NB], 1)
                emptied(dve, ACC["sgu"], 2)
                for b in range(2):
                    emptied(dve, ACC[f"dpv{b}"])
                norm_front(6, y_nat)
                split(u0 + 12)
                norm_back(6, g_ab)
                split(u0 + 13)
                add_out("mix", UNITS["mix_out"], OUT["mix_out"])

            def cross():
                u0 = UNITS["cross"]
                norm_front(7, x_sb)
                split(u0)
                norm_back(7, gains[:, 7, :])
                split(u0 + 1)
                for j in range(4):
                    split(u0 + 2 + j)
                for n in range(4):
                    soft_front(n, 12, xs_tiles[n], 1 / 16, ACC["xsc"] + n)
                for n in range(4):
                    emptied(dve, ACC["xsc"] + n)
                    soft_back(n, 12, xs_tiles[n])
                for h in range(4):
                    mix_low(10 + h, ACC["xpv"] + h, 2 * h)
                add_out("cross", u0 + 4, OUT["cross_out"])

            if "even" in running:
                even()
            if "ffn0" in running:
                ffn("ffn0")
            if "odd" in running:
                odd()
            if "ffn1" in running:
                ffn("ffn1", "mem_k2")
            if "ffn2" in running:
                ffn("ffn2", "mem_k3")
            if "mix" in running:
                mix()
            if "cross" in running:
                cross()
            if "ffn3" in running:
                ffn("ffn3")
            if "final" in running:
                norm_front(10, x_sb)


_INS = ["x", "even_norm", "even_w_in", "q_norm", "k_norm", "sinks", "ssm_a_re", "ssm_a_im", "ssm_b_re", "ssm_b_im",
        "ssm_c_re", "ssm_c_im", "ssm_d", "ssm_log_dt", "ssm_w_glu", "ssm_b_glu", "even_w_out", "odd_norm",
        "odd_w_in", "odd_w_out", "ffn_norm", "ffn_w_gate", "ffn_w_up", "ffn_w_down", "mem_2", "positions_2",
        "ffn1_norm_2", "ffn1_w_gate_2", "ffn1_w_up_2", "ffn1_w_down_2", "mix_norm_2", "w_in_2", "sgu_ln_g_2",
        "sgu_ln_b_2", "sgu_w_s_2", "sgu_b_s_2", "out_norm_a_2", "out_norm_b_2", "w_out_2", "cross_norm_2",
        "mem_norm_2", "cross_wq_2", "cross_wk_2", "cross_wv_2", "cross_wo_2", "ffn2_norm_2", "ffn2_w_gate_2",
        "ffn2_w_up_2", "ffn2_w_down_2", "final_norm_2"]


def kernel(**inputs):
    import concourse.bacc as _bacc
    from concourse.bass_utils import run_bass_kernel_spmd as _run

    nc = _bacc.Bacc("TRN2", target_bir_lowering=False, num_devices=1, dynamic_dma_scratch_size=1024)
    arrays, args = {}, {}
    for name in _INS:
        v = np.ascontiguousarray(inputs[name])
        arrays[f"in_{name}_dram"] = v
        args[name] = nc.dram_tensor(f"in_{name}_dram", v.shape, mybir.dt.from_np(v.dtype), kind="ExternalInput").ap()
    v = shape_constants()
    arrays["in_consts_dram"] = v
    args["consts"] = nc.dram_tensor("in_consts_dram", v.shape, F32, kind="ExternalInput").ap()
    out = nc.dram_tensor("out_0_dram", (1, L, D), F32, kind="ExternalOutput").ap()
    build(nc, args, out)
    r = _run(nc, [arrays], core_ids=[0])
    return r.results[0]["out_0_dram"]
```
